# Optimizing a Trainium2 kernel written in Bass

```python
import math, functools
import jax, jax.numpy as jnp
from jax import lax
import numpy as np

D_MODEL = 1024
BATCH = 1
SEQ = 1024
DEPTH = 1
DEC_BATCH = 8
DEC_SEQ = 4
PAST_LEN = 4096
PAGE_SIZE = 128

HEAD_DIM = 64
ATT_WIDTH = D_MODEL // 2
ATT_HEADS = ATT_WIDTH // HEAD_DIM
ATT_BRANCHES = ((128, 1), (512, 4), (2048, 16))
ATT_WINDOW = max(w for w, _ in ATT_BRANCHES)
ATT_SCALE = HEAD_DIM ** -0.5
HGRN_WIDTH = D_MODEL // 2
HGRN_DK = 128
HGRN_DV = 128
HGRN_HEADS = HGRN_WIDTH // HGRN_DK
HGRN_CHUNK = 64
MIX_WIDTH = ATT_WIDTH + HGRN_WIDTH
IN_SPLITS = (ATT_WIDTH, ATT_WIDTH, ATT_WIDTH, HGRN_WIDTH, HGRN_WIDTH, HGRN_WIDTH, HGRN_WIDTH)
IN_COLS = sum(IN_SPLITS)
N_KEYS = 128
N_EXPERTS = N_KEYS * N_KEYS
PEER_HEADS = 8
PEER_DKEY = 256
PEER_TOPK = 16
PEER_BLOCK = 128
EPS = 1e-6

kernel_name = "hybrid_dilated_attn_hgrn2_peer_step"

def rmsnorm(x, w):
    xf = x.astype(jnp.float32)
    y = xf * lax.rsqrt(jnp.mean(xf * xf, axis=-1, keepdims=True) + EPS)
    return (y * w.astype(jnp.float32)).astype(x.dtype)

def dilated_branch_prompt(q, k, v, dil, steps):
    B, S, H, Dh = q.shape
    L = S // dil
    nb = -(-L // steps)
    Lp = nb * steps

    def to_blocks(t):
        t = t.reshape(B, L, dil, H, Dh).transpose(0, 2, 1, 3, 4)
        t = jnp.pad(t, ((0, 0), (0, 0), (0, Lp - L), (0, 0), (0, 0)))
        return t.reshape(B, dil, nb, steps, H, Dh)

    def with_prev(t):
        prev = jnp.pad(t[:, :, :-1], ((0, 0), (0, 0), (1, 0), (0, 0), (0, 0), (0, 0)))
        return jnp.concatenate([prev, t], axis=3)

    qb, kb, vb = to_blocks(q), to_blocks(k), to_blocks(v)
    kw, vw = with_prev(kb), with_prev(vb)
    s = jnp.einsum('brnqhd,brnkhd->brnhqk', qb, kw, preferred_element_type=jnp.float32)
    a = jnp.arange(steps)[:, None]
    c = jnp.arange(2 * steps)[None, :]
    dist = steps + a - c
    blk = jnp.arange(nb)[:, None, None]
    valid = (dist >= 0) & (dist <= steps) & ((blk > 0) | (c >= steps))
    s = jnp.where(valid[:, None], s, -jnp.inf)
    m = jnp.max(s, axis=-1)
    p = jnp.exp(s - m[..., None])
    l = jnp.sum(p, axis=-1)
    acc = jnp.einsum('brnhqk,brnkhd->brnqhd', p, vw.astype(jnp.float32))

    def back(t):
        rest = t.shape[5:]
        t = t.reshape((B, dil, Lp, H) + rest)[:, :, :L]
        t = jnp.swapaxes(t, 1, 2)
        return t.reshape((B, S, H) + rest)

    return (back(jnp.swapaxes(m, 3, 4)), back(jnp.swapaxes(l, 3, 4)), back(acc))

def dilated_branch_sample(q, kk, vv, dil, steps, n_buf):
    T = q.shape[1]
    idx = n_buf + jnp.arange(T)[:, None] - jnp.arange(steps + 1)[None, :] * dil
    valid = idx >= 0
    idxc = jnp.maximum(idx, 0)
    kg = kk[:, idxc]
    vg = vv[:, idxc]
    s = jnp.einsum('bthd,btjhd->bthj', q, kg, preferred_element_type=jnp.float32)
    s = jnp.where(valid[None, :, None, :], s, -jnp.inf)
    m = jnp.max(s, axis=-1)
    p = jnp.exp(s - m[..., None])
    l = jnp.sum(p, axis=-1)
    acc = jnp.einsum('bthj,btjhd->bthd', p, vg.astype(jnp.float32))
    return m, l, acc

def combine_branches(parts):
    m = jnp.stack([p_[0] for p_ in parts])
    l = jnp.stack([p_[1] for p_ in parts])
    acc = jnp.stack([p_[2] for p_ in parts])
    w = jnp.exp(m - jnp.max(m, axis=0, keepdims=True))
    den = jnp.sum(w * l, axis=0)
    num = jnp.sum(w[..., None] * acc, axis=0)
    return num / den[..., None]

def attention_prompt(q, k, v):
    parts = [dilated_branch_prompt(q, k, v, d, w // d) for (w, d) in ATT_BRANCHES]
    out = combine_branches(parts).astype(q.dtype)
    keep = min(ATT_WINDOW, q.shape[1])
    return out, k[:, -keep:], v[:, -keep:]

def attention_sample(q, k, v, cache_k, cache_v):
    n_buf = cache_k.shape[1]
    kk = jnp.concatenate([cache_k.astype(k.dtype), k], axis=1)
    vv = jnp.concatenate([cache_v.astype(v.dtype), v], axis=1)
    parts = [dilated_branch_sample(q, kk, vv, d, w // d, n_buf) for (w, d) in ATT_BRANCHES]
    out = combine_branches(parts).astype(q.dtype)
    return out, kk[:, -n_buf:], vv[:, -n_buf:]

def hgrn2_scan(q, k, i, logf, S0):
    B, L, H, Dk = q.shape
    Dv = i.shape[-1]
    C = HGRN_CHUNK if L % HGRN_CHUNK == 0 else L
    n = L // C

    def chunks(t):
        return jnp.swapaxes(t.reshape(B, n, C, H, t.shape[-1]), 0, 1)

    causal = jnp.arange(C)[:, None] >= jnp.arange(C)[None, :]

    def step(S, inp):
        qc, kc, ic, gc = inp
        b = jnp.cumsum(gc, axis=1)
        inter = jnp.einsum('bchk,bhkv->bchv', qc * jnp.exp(b), S)
        diff = b[:, :, None] - b[:, None, :]
        decay = jnp.exp(jnp.where(causal[None, :, :, None, None], diff, -jnp.inf))
        A = jnp.einsum('bthk,btshk,bshk->bhts', qc, decay, kc)
        intra = jnp.einsum('bhts,bshv->bthv', A, ic)
        b_last = b[:, -1]
        S_new = jnp.exp(b_last)[..., None] * S + jnp.einsum(
            'bshk,bshv->bhkv', kc * jnp.exp(b_last[:, None] - b), ic)
        return S_new, inter + intra

    S_fin, o = lax.scan(step, S0, (chunks(q), chunks(k), chunks(i), chunks(logf)))
    o = jnp.swapaxes(o, 0, 1).reshape(B, L, H, Dv)
    return o, S_fin

def peer(xn, wq, sub_keys, u, v):
    B, T, D = xn.shape
    n = B * T
    xt = xn.reshape(n, D)
    half = PEER_DKEY // 2
    q = (xt @ wq).reshape(n, PEER_HEADS, PEER_DKEY).astype(jnp.float32)
    sk = sub_keys.astype(jnp.float32)
    s1 = jnp.einsum('nhd,hkd->nhk', q[..., :half], sk[:, 0])
    s2 = jnp.einsum('nhd,hkd->nhk', q[..., half:], sk[:, 1])
    v1, i1 = lax.top_k(s1, PEER_TOPK)
    v2, i2 = lax.top_k(s2, PEER_TOPK)
    cand = (v1[..., :, None] + v2[..., None, :]).reshape(n, PEER_HEADS, PEER_TOPK * PEER_TOPK)
    cidx = (i1[..., :, None] * N_KEYS + i2[..., None, :]).reshape(n, PEER_HEADS, PEER_TOPK * PEER_TOPK)
    sv, si = lax.top_k(cand, PEER_TOPK)
    e = jnp.take_along_axis(cidx, si, axis=-1)
    g = jax.nn.softmax(sv, axis=-1)
    pad = (-n) % PEER_BLOCK
    nb = (n + pad) // PEER_BLOCK
    xp = jnp.pad(xt, ((0, pad), (0, 0))).reshape(nb, PEER_BLOCK, D)
    ep = jnp.pad(e, ((0, pad), (0, 0), (0, 0))).reshape(nb, PEER_BLOCK, PEER_HEADS, PEER_TOPK)
    gp = jnp.pad(g, ((0, pad), (0, 0), (0, 0))).reshape(nb, PEER_BLOCK, PEER_HEADS, PEER_TOPK)

    def block(args):
        xb, eb, gb = args
        ue = u[eb]
        act = jax.nn.gelu(jnp.einsum('nd,nhkd->nhk', xb, ue, preferred_element_type=jnp.float32),
                          approximate=False)
        return jnp.einsum('nhk,nhkd->nd', (gb * act).astype(v.dtype), v[eb],
                          preferred_element_type=jnp.float32)

    y = lax.map(block, (xp, ep, gp)).reshape(nb * PEER_BLOCK, D)[:n]
    return y.reshape(B, T, D).astype(xn.dtype)

def layer(x, attn_fn, S0, lb, norm1_w, w_in, hgrn_norm_w, w_out, norm2_w,
          peer_wq, peer_sub_keys, peer_u, peer_v):
    B, T, _ = x.shape
    xn = rmsnorm(x, norm1_w)
    proj = xn @ w_in
    aq, ak, av, hq, hf, hi, hg = jnp.split(proj, list(np.cumsum(IN_SPLITS)[:-1]), axis=-1)
    att, k_state, v_state = attn_fn(
        aq.reshape(B, T, ATT_HEADS, HEAD_DIM) * ATT_SCALE,
        ak.reshape(B, T, ATT_HEADS, HEAD_DIM),
        av.reshape(B, T, ATT_HEADS, HEAD_DIM))
    f = lb + (1.0 - lb) * jax.nn.sigmoid(hf.astype(jnp.float32))
    hh = lambda t, d: t.reshape(B, T, HGRN_HEADS, d)
    o, S = hgrn2_scan(hh(jax.nn.silu(hq.astype(jnp.float32)), HGRN_DK),
                      hh(1.0 - f, HGRN_DK),
                      hh(hi.astype(jnp.float32), HGRN_DV),
                      hh(jnp.log(f), HGRN_DK),
                      S0)
    o = o * lax.rsqrt(jnp.mean(o * o, axis=-1, keepdims=True) + EPS) * hgrn_norm_w.astype(jnp.float32)
    o = o * jax.nn.silu(hh(hg.astype(jnp.float32), HGRN_DV))
    mix = jnp.concatenate([att.reshape(B, T, ATT_WIDTH),
                           o.reshape(B, T, HGRN_WIDTH).astype(x.dtype)], axis=-1)
    h = x + mix @ w_out
    h = h + peer(rmsnorm(h, norm2_w), peer_wq, peer_sub_keys, peer_u, peer_v)
    return h, k_state, v_state, S

def setup_inputs(seed: int = 0) -> dict:
    key = jax.random.key(seed)
    ks = jax.random.split(key, 20)
    f32 = jnp.float32
    win_buf = min(ATT_WINDOW, PAST_LEN)
    nrm = lambda k, shape, s: jax.random.normal(k, shape, f32) * s
    return {
        "x_prompt": nrm(ks[0], (BATCH, SEQ, D_MODEL), 1.0),
        "x_sample": nrm(ks[1], (DEC_BATCH, DEC_SEQ, D_MODEL), 1.0),
        "cache_k_win": nrm(ks[2], (DEPTH, DEC_BATCH, win_buf, ATT_HEADS, HEAD_DIM), 1.0),
        "cache_v_win": nrm(ks[3], (DEPTH, DEC_BATCH, win_buf, ATT_HEADS, HEAD_DIM), 1.0),
        "state_hgrn": nrm(ks[4], (DEPTH, DEC_BATCH, HGRN_HEADS, HGRN_DK, HGRN_DV), 0.5),
        "norm1_w": 1.0 + nrm(ks[5], (DEPTH, D_MODEL), 0.02),
        "w_in": nrm(ks[6], (DEPTH, D_MODEL, IN_COLS), D_MODEL ** -0.5),
        "hgrn_norm_w": 1.0 + nrm(ks[7], (DEPTH, HGRN_DV), 0.02),
        "hgrn_lb_logits": nrm(ks[8], (DEPTH + 1, HGRN_WIDTH), 0.1),
        "w_out": nrm(ks[9], (DEPTH, MIX_WIDTH, D_MODEL), MIX_WIDTH ** -0.5),
        "norm2_w": 1.0 + nrm(ks[10], (DEPTH, D_MODEL), 0.02),
        "peer_wq": nrm(ks[11], (DEPTH, D_MODEL, PEER_HEADS * PEER_DKEY), D_MODEL ** -0.5),
        "peer_sub_keys": nrm(ks[12], (DEPTH, PEER_HEADS, 2, N_KEYS, PEER_DKEY // 2), (PEER_DKEY // 2) ** -0.5),
        "peer_u": nrm(ks[13], (DEPTH, N_EXPERTS, D_MODEL), D_MODEL ** -0.5),
        "peer_v": nrm(ks[14], (DEPTH, N_EXPERTS, D_MODEL), 0.5),
        "norm_f_w": 1.0 + nrm(ks[15], (D_MODEL,), 0.02),
    }

def reference(x_prompt, x_sample, cache_k_win, cache_v_win, state_hgrn, norm1_w, w_in,
              hgrn_norm_w, hgrn_lb_logits, w_out, norm2_w, peer_wq, peer_sub_keys,
              peer_u, peer_v, norm_f_w):
    lb_all = jnp.cumsum(jax.nn.softmax(hgrn_lb_logits.astype(jnp.float32), axis=0), axis=0)
    hp, hs = x_prompt, x_sample
    kp, vp, sp, ksm, vsm, ssm = [], [], [], [], [], []
    for l in range(DEPTH):
        w = (norm1_w[l], w_in[l], hgrn_norm_w[l], w_out[l], norm2_w[l],
             peer_wq[l], peer_sub_keys[l], peer_u[l], peer_v[l])
        S0p = jnp.zeros((hp.shape[0], HGRN_HEADS, HGRN_DK, HGRN_DV), jnp.float32)
        hp, k_, v_, s_ = layer(hp, attention_prompt, S0p, lb_all[l], *w)
        kp.append(k_); vp.append(v_); sp.append(s_.astype(x_prompt.dtype))
        attn_s = functools.partial(attention_sample, cache_k=cache_k_win[l], cache_v=cache_v_win[l])
        hs, k_, v_, s_ = layer(hs, attn_s, state_hgrn[l].astype(jnp.float32), lb_all[l], *w)
        ksm.append(k_); vsm.append(v_); ssm.append(s_.astype(state_hgrn.dtype))
    y_prompt = rmsnorm(hp, norm_f_w)
    y_sample = rmsnorm(hs, norm_f_w)
    return (y_prompt, y_sample, jnp.stack(kp), jnp.stack(vp), jnp.stack(sp),
            jnp.stack(ksm), jnp.stack(vsm), jnp.stack(ssm))


_drawn_inputs = setup_inputs


def setup_inputs(seed=0):
    import zlib

    import numpy as np

    out = dict(_drawn_inputs(seed))
    spreads = {}
    factors = {}
    for name, (base, spread) in spreads.items():
        noise = np.random.default_rng([zlib.crc32(name.encode()), seed]).standard_normal(out[name].shape)
        drawn = base * np.exp(spread * noise) if base else spread * noise
        out[name] = __import__('jax').numpy.asarray(drawn.astype(out[name].dtype))
    for name, factor in factors.items():
        out[name] = (out[name] * factor).astype(out[name].dtype)
    return out
```

```python
from contextlib import ExitStack

import concourse.bass as bass
from concourse import mybir

F32 = mybir.dt.float32
I32 = mybir.dt.int32
U32 = mybir.dt.uint32
ALU = mybir.AluOpType
ACT = mybir.ActivationFunctionType
AX = mybir.AxisListType

P = 128
D = 1024
DC = D // P
SEQ = 1024
SB, ST = 8, 4
NS = SB * ST
T = SEQ + NS
TT = SEQ // P
SL = 352
NSL = T // SL
H, DH = 8, 64
G, DK = 4, 128
NB = 2048
EPS = 1e-6
EXPERTS = 16384
PH, PK, TOPK = 8, 128, 16
LOWEST = -3.0e38
NSPARSE = 384
NRECENT = 512
NKEY = NSPARSE + NRECENT
NCOL = NKEY + NS
CH = 32
NCH = SEQ // CH

FQ, FK, FHQ, FHF, FHG = range(5)

XT0 = 0
F0 = XT0 + DC * T
V0 = F0 + 5 * 4 * T
HI0 = V0 + 9 * 512
W0 = HI0 + 9 * 512
H0 = XT0 + DC * T
S0 = H0 + 9 * D
W3 = S0 + 9 * 2 * PH * PK
WORDS = 52880


def build(nc, x):
    with ExitStack() as whole:
        arena = whole.enter_context(nc.sbuf_tensor("arena", [P, WORDS], F32))
        psum = whole.enter_context(nc.psum_tensor("psum", [P, 8, 512], F32))
        consts = whole.enter_context(nc.sbuf_tensor("consts", [P, 288], F32))

        def at(word, *shape):
            n = 1
            for s in shape:
                n *= s
            v = arena[:, word:word + n]
            if len(shape) == 2:
                v = v.rearrange("p (a b) -> p a b", a=shape[0])
            if len(shape) == 3:
                v = v.rearrange("p (a b c) -> p a b c", a=shape[0], b=shape[1])
            return v

        m = {
            "arena": arena, "psum": psum, "at": at,
            "xn": at(XT0, DC, T), "mix": at(XT0, DC, T),
            "feat": at(F0, 5, 4, T), "v": at(V0, 9, 512), "hi": at(HI0, 9, 512),
            "ident": consts[:, 0:128], "ones": consts[:, 128:256], "io16": consts[:, 256:272],
            "eps": consts[:, 272:273], "rstd2": consts[:, 273:282],
            "norm2": at(WORDS - D, D), "h": at(H0, 9, D), "scores": at(S0, 9, 2 * PH * PK),
        }
        done = whole.enter_context(nc.semaphore("windows_shifted"))
        project_in(nc, x, m, done)
        attend_prompt(nc, x, m)
        attend_sample(nc, x, m)
        hgrn(nc, x, m)
        project_out(nc, x, m)
        experts(nc, x, m, done)


def project_in(nc, x, m, windows_shifted):
    psum, xn, feat, at = m["psum"], m["xn"], m["feat"], m["at"]
    with ExitStack() as c:
        sem = lambda n: c.enter_context(nc.semaphore(n))
        w = at(W0, 2, DC, 256)
        sq = at(W0 + 4096, 2, T)
        rstd = at(W0 + 4096 + 2 * T, T)
        nw = at(W0 + 4096 + 3 * T, DC)
        kscale = at(W0 + 4096 + 3 * T + DC, 5)
        x_loaded = sem("x_loaded")
        w_loaded = [sem(f"w_loaded{i}") for i in range(2)]
        consts_ready = sem("consts_ready")
        squared = sem("squared")
        square_used = sem("square_used")
        sums_ready = sem("sums_ready")
        rms_ready = sem("rms_ready")
        x_normed = sem("x_normed")
        piece_done = sem("piece_done")
        group_ready = sem("group_ready")
        bank_free = sem("bank_free")
        tile_ready = sem("tile_ready")
        tile_free = sem("tile_free")
        kv_out = sem("kv_out")
        block = c.enter_context(nc.Block())

        @block.sync
        def _(sp):
            for q in range(DC):
                sp.dma_start(xn[:, q, :], x["x_feat"][:, q, :]).then_inc(x_loaded, 16)
            sp.dma_start(nw, x["norm1"]).then_inc(x_loaded, 16)
            for p in range(2):
                sp.dma_start(w[:, p, :, :], x["w_in"][p]).then_inc(w_loaded[p], 16)
            with sp.Fori(1, 7) as i:
                for p in range(2):
                    sp.wait_ge(piece_done, i * 2 + p - 1)
                    sp.dma_start(w[:, p, :, :], x["w_in"][bass.ds(i * 2 + p, 1)].squeeze(0)).then_inc(w_loaded[p], 16)
            for name in ("k", "v"):
                for b in range(SB):
                    sp.dma_start(x[f"{name}_win_sample"][b, 0:NB - ST, :],
                                 x[f"cache_{name}"][b, ST:NB, :]).then_inc(windows_shifted, 16)
            sp.wait_ge(x_normed, DC + 6)
            sp.wait_ge(tile_free, 2 + 4 * 9)
            sp.dma_start(x["k_feat_out"], feat[:, FK, :, :]).then_inc(kv_out, 16)
            sp.dma_start(x["v_out"], m["v"][:, 0:TT, :]).then_inc(kv_out, 16)
            sp.dma_start(x["v_out_s"], m["v"][0:NS, TT, :]).then_inc(kv_out, 16)
            sp.wait_ge(kv_out, 48)

        @block.gpsimd
        def _(pool):
            pool.memset(m["ones"], 1.0).then_inc(consts_ready, 1)
            pool.memset(m["ident"], 0.0).then_inc(consts_ready, 1)
            pool.wait_ge(consts_ready, 2)
            pool.affine_select(out=m["ident"], in_=m["ident"], compare_op=ALU.not_equal, fill=1.0,
                               base=0, pattern=[[-1, P]], channel_multiplier=1).then_inc(consts_ready, 1)
            pool.iota(m["io16"].bitcast(I32), pattern=[[1, 16]], base=0, channel_multiplier=0).then_inc(consts_ready, 1)
            pool.memset(m["eps"], EPS).then_inc(consts_ready, 1)
            pool.wait_ge(consts_ready, 5)
            pool.tensor_copy(m["io16"], m["io16"].bitcast(I32)).then_inc(consts_ready, 1)
            pool.wait_ge(consts_ready, 6)

        @block.scalar
        def _(act):
            act.wait_ge(x_loaded, 16 * (DC + 1))
            for q in range(DC):
                if q >= 2:
                    act.wait_ge(square_used, q - 1)
                act.activation(sq[:, q % 2, :], xn[:, q, :], ACT.Square).then_inc(squared, 1)
            act.wait_ge(consts_ready, 6)
            act.wait_ge(square_used, DC)
            for s in range(NSL):
                last = act.activation(rstd[:, s * SL:(s + 1) * SL], psum[:, s, 0:SL], ACT.Sqrt,
                                      bias=m["eps"], scale=1.0 / D)
            last.then_inc(rms_ready, 1)

        @block.tensor
        def _(pe):
            pe.wait_ge(consts_ready, 6)
            for q in range(DC):
                pe.wait_ge(squared, q + 1)
                for s in range(NSL):
                    last = pe.matmul(psum[:, s, 0:SL], m["ones"], sq[:, q % 2, s * SL:(s + 1) * SL],
                                     start=q == 0, stop=q == DC - 1)
                last.then_inc(square_used, 1)
            pe.wait_ge(x_normed, DC)
            with pe.Fori(0, 5) as i:
                for p in range(2):
                    pe.wait_ge(w_loaded[p], i * 16 + 16)
                    for j in range(2):
                        pe.wait_ge(bank_free, i * 4 + 2 * p + j + 1)
                        for s in range(NSL):
                            for q in range(DC):
                                last = pe.matmul(psum[:, 3 * j + s, 0:SL], w[:, p, q, j * P:(j + 1) * P],
                                                 xn[:, q, s * SL:(s + 1) * SL],
                                                 start=q == 0, stop=q == DC - 1)
                        last.then_inc(group_ready, 1)
                    pe.wait_ge(group_ready, i * 4 + 2 * p + 2)
                    pe.sem_inc(piece_done, 1)
            for i in range(2):
                for p in range(2):
                    pe.wait_ge(w_loaded[p], (5 + i) * 16 + 16)
                    n0 = (2 * i + p) * 9
                    for t in range(9):
                        rows = P if t < TT else NS
                        pe.wait_ge(tile_free, n0 + t + 1)
                        for q in range(DC):
                            last = pe.matmul(psum[0:rows, 6 + (n0 + t) % 2, 0:256],
                                             xn[:, q, t * P:t * P + rows], w[:, p, q, :],
                                             start=q == 0, stop=q == DC - 1)
                        last.then_inc(tile_ready, 1)
                    pe.wait_ge(tile_ready, n0 + 9)
                    pe.sem_inc(piece_done, 1)

        @block.vector
        def _(dve):
            for i in range(5):
                dve.memset(kscale[:, i:i + 1], DH ** -0.5 if i == FQ else 1.0)
            dve.drain()
            dve.sem_inc(bank_free, 2)
            dve.sem_inc(tile_free, 2)
            dve.wait_ge(rms_ready, 1)
            dve.reciprocal(rstd, rstd)
            dve.drain()
            for q in range(DC):
                dve.scalar_tensor_tensor(out=xn[:, q, :], in0=xn[:, q, :], scalar=nw[:, q:q + 1], in1=rstd,
                                         op0=ALU.mult, op1=ALU.mult).then_inc(x_normed, 1)
            with dve.Fori(0, 5) as i:
                for p in range(2):
                    for j in range(2):
                        dve.wait_ge(group_ready, i * 4 + 2 * p + j + 1)
                        for s in range(NSL):
                            last = dve.tensor_scalar(
                                m["arena"][:, bass.ds(F0 + i * (4 * T) + (2 * p + j) * T + s * SL, SL)],
                                psum[:, 3 * j + s, 0:SL], kscale[:, bass.ds(i, 1)], None, ALU.mult)
                        last.then_inc(bank_free, 1)
            dve.drain().then_inc(x_normed, 6)
            for i in range(2):
                for p in range(2):
                    for t in range(9):
                        n = (2 * i + p) * 9 + t
                        rows = P if t < TT else NS
                        dve.wait_ge(tile_ready, n + 1)
                        dst = (m["v"], m["hi"])[i]
                        dve.tensor_copy(dst[0:rows, t, p * 256:(p + 1) * 256],
                                        psum[0:rows, 6 + n % 2, 0:256]).then_inc(tile_free, 1)


def attend_prompt(nc, x, m):
    psum, at, arena, mix = m["psum"], m["at"], m["arena"], m["mix"]
    with ExitStack() as c:
        sem = lambda n: c.enter_context(nc.semaphore(n))
        bias = at(W0, SEQ)
        probs = at(W0 + SEQ, 2, SEQ)
        turned = at(W0 + 3 * SEQ, 2, SEQ)
        top = at(W0 + 5 * SEQ, 2, 1)
        neg_top = at(W0 + 5 * SEQ + 2, 2, 1)
        total = at(W0 + 5 * SEQ + 4, 2, 1)
        inv = at(W0 + 5 * SEQ + 6, 2, 1)
        pair_q = at(W0 + 5 * SEQ + 8, SEQ)
        pair_v = at(W0 + 6 * SEQ + 8, TT, P)
        pair_k = at(W0 + 7 * SEQ + 8, SEQ)
        bias_loaded = sem("bias_loaded")
        pair_staged = sem("pair_staged")
        scores_ready = sem("scores_ready")
        scores_read = sem("scores_read")
        max_ready = sem("max_ready")
        exp_ready = sem("exp_ready")
        probs_ready = sem("probs_ready")
        piece_ready = sem("piece_ready")
        piece_copied = sem("piece_copied")
        out_ready = sem("out_ready")
        out_copied = sem("out_copied")
        settled = {e: sem(f"settled_{e}") for e in ("pe", "act", "dve", "pool")}
        block = c.enter_context(nc.Block())

        BLOCKS = 2 * TT
        pieces = [1 if n % TT < 4 else 2 for n in range(BLOCKS)]
        before = [sum(pieces[:n]) for n in range(BLOCKS + 1)]
        PIECES = before[-1]
        SPARE = 4

        @block.sync
        def _(sp):
            sp.dma_start(bias, x["bias_prompt"]).then_inc(bias_loaded, 16)

        @block.gpsimd
        def _(pool):
            with pool.Fori(0, H // 2) as j:
                pool.wait_ge(out_ready, j * BLOCKS + 2)
                pool.sem_inc(settled["pool"], 1)
                pool.tensor_copy(pair_q, arena[:, bass.ds(F0 + FQ * 4 * T + j * T, SEQ)]).then_inc(pair_staged, 1)
                pool.tensor_copy(pair_k, arena[:, bass.ds(F0 + FK * 4 * T + j * T, SEQ)]).then_inc(pair_staged, 1)
                pool.tensor_copy(pair_v, m["v"][:, 0:TT, bass.ds(j * P, P)]).then_inc(pair_staged, 1)

        @block.tensor
        def _(pe):
            with pe.Fori(0, H // 2) as j:
                def scores(n):
                    half, i = divmod(n, TT)
                    r = slice(64 * half, 64 * half + 64)
                    pe.wait_ge(scores_read, j * BLOCKS + n + 1)
                    pe.sem_inc(settled["pe"], 1)
                    width = (i + 1) * P
                    for s in range(0, width, 512):
                        e = min(width, s + 512)
                        last = pe.matmul(
                                             psum[:, 2 * (n % 2) + s // 512, 0:e - s],
                                             pair_q[r, i * P:(i + 1) * P],
                                             pair_k[r, s:e],
                                             start=True, stop=True)
                    last.then_inc(scores_ready, 1)

                def turn(n):
                    i = n % TT
                    pe.wait_ge(probs_ready, j * BLOCKS + n + 1)
                    for b in range(pieces[n]):
                        pe.wait_ge(piece_copied, j * PIECES + before[n] + b + SPARE - 1)
                        for k in range(4 * b, min(i + 1, 4 * b + 4)):
                            last = pe.transpose(psum[:, 4 + (before[n] + b) % 2, (k % 4) * P:(k % 4 + 1) * P],
                                                probs[:, n % 2, k * P:(k + 1) * P], m["ident"])
                        last.then_inc(piece_ready, 1)

                def values(n):
                    half, i = divmod(n, TT)
                    pe.wait_ge(piece_copied, j * PIECES + before[n + 1] + SPARE)
                    pe.sem_inc(settled["pe"], 1)
                    pe.wait_ge(out_copied, j * BLOCKS + n + 1)
                    pe.sem_inc(settled["pe"], 1)
                    for k in range(i + 1):
                        last = pe.matmul(psum[64 * half:64 * half + 64, 6 + n % 2, 0:P],
                                         pair_v[:, k, half * 64:half * 64 + 64],
                                         turned[:, n % 2, k * P:(k + 1) * P],
                                         start=k == 0, stop=k == i)
                    last.then_inc(out_ready, 1)

                pe.wait_ge(pair_staged, 3 * j + 3)
                pe.sem_inc(settled["pe"], 1)
                scores(0)
                for n in range(BLOCKS):
                    if n + 1 < BLOCKS:
                        scores(n + 1)
                    turn(n)
                    if n >= 1:
                        values(n - 1)
                values(BLOCKS - 1)

        @block.vector
        def _(dve):
            dve.sem_inc(scores_read, 2)
            dve.wait_ge(bias_loaded, 16)
            with dve.Fori(0, H // 2) as j:
                def add_bias(n):
                    width = (n % TT + 1) * P
                    dve.wait_ge(scores_ready, j * BLOCKS + n + 1)
                    dve.sem_inc(settled["dve"], 1)
                    dve.wait_ge(piece_copied, j * PIECES + SPARE + (before[n - 1] if n else -pieces[-1]))
                    dve.sem_inc(settled["dve"], 1)
                    scores = psum[:, 2 * (n % 2):2 * (n % 2) + 2, :].rearrange("p a b -> p (a b)")
                    dve.tensor_tensor_reduce(probs[:, n % 2, 0:width], scores[:, 0:width],
                                             bias[:, SEQ - width:SEQ], 1.0, LOWEST, ALU.add, ALU.max,
                                             top[:, n % 2, :]).then_inc(scores_read, 1)
                    dve.drain()
                    dve.tensor_scalar(neg_top[:, n % 2, :], top[:, n % 2, :], -1.0, None,
                                      ALU.mult).then_inc(max_ready, 1)

                def normalize(n):
                    width = (n % TT + 1) * P
                    dve.wait_ge(exp_ready, j * BLOCKS + n + 1)
                    dve.reciprocal(inv[:, n % 2, :], total[:, n % 2, :])
                    dve.drain()
                    dve.tensor_scalar(probs[:, n % 2, 0:width], probs[:, n % 2, 0:width], inv[:, n % 2, :],
                                      None, ALU.mult).then_inc(probs_ready, 1)

                for n in range(BLOCKS):
                    add_bias(n)
                    if n >= 1:
                        normalize(n - 1)
                normalize(BLOCKS - 1)

        @block.scalar
        def _(act):
            act.sem_inc(piece_copied, SPARE)
            act.sem_inc(out_copied, 2)
            act.sem_inc(out_ready, 2)
            with act.Fori(0, H // 2) as j:
                def exps(n):
                    width = (n % TT + 1) * P
                    act.wait_ge(max_ready, j * BLOCKS + n + 1)
                    act.activation(probs[:, n % 2, 0:width], probs[:, n % 2, 0:width], ACT.Exp,
                                   bias=neg_top[:, n % 2, :], accum_out=total[:, n % 2, :]).then_inc(exp_ready, 1)

                def copy_pieces(n):
                    width = (n % TT + 1) * P
                    act.wait_ge(out_ready, j * BLOCKS + n + 1)
                    act.sem_inc(settled["act"], 1)
                    for b in range(pieces[n]):
                        s, e = 512 * b, min(width, 512 * b + 512)
                        act.wait_ge(piece_ready, j * PIECES + before[n] + b + 1)
                        act.copy(turned[:, n % 2, s:e],
                                 psum[:, 4 + (before[n] + b) % 2, 0:e - s]).then_inc(piece_copied, 1)

                def copy_out(n):
                    half, i = divmod(n, TT)
                    r = slice(64 * half, 64 * half + 64)
                    act.wait_ge(out_ready, j * BLOCKS + n + 3)
                    act.sem_inc(settled["act"], 1)
                    act.copy(arena[r, bass.ds(XT0 + i * P + j * T, P)],
                             psum[r, 6 + n % 2, 0:P]).then_inc(out_copied, 1)

                for n in range(BLOCKS):
                    exps(n)
                    if n >= 1:
                        copy_pieces(n - 1)
                    if n >= 2:
                        copy_out(n - 2)
                copy_pieces(BLOCKS - 1)
                copy_out(BLOCKS - 2)
                copy_out(BLOCKS - 1)


def hgrn(nc, x, m):
    psum, at, feat, mix, hi = m["psum"], m["at"], m["feat"], m["mix"], m["hi"]
    GT = 4 * T
    with ExitStack() as c:
        sem = lambda n: c.enter_context(nc.semaphore(n))
        q, b, gate = feat[:, FHQ, :, :], feat[:, FHF, :, :], feat[:, FHG, :, :]
        word = W0
        k = at(word, G, T); word += GT
        ek = at(word, G, T); word += GT
        resets = at(word, T); word += T
        causal = at(word, P); word += P
        causal_s = at(word, NS); word += NS
        only = at(word, SB); word += SB
        logits = at(word, 2, G); word += 2 * G
        lbt = at(word, 8, G); word += 8 * G
        hnorm = at(word, 1); word += 1
        carry = at(word, G, NCH + 1); word += G * (NCH + 1)
        carry_s = at(word, 2, G * SB).rearrange("p a (g b) -> p a g b", g=G); word += 2 * G * SB
        state = at(word, G, 2, P); word += G * 2 * P
        sum_state = at(word, G, P); word += G * P
        masked = at(word, G, P); word += G * P
        assert word <= WORDS, word
        eq = at(F0, G, T)
        state_s = at(F0 + GT, G, SB * P).rearrange("p g (b v) -> p g b v", b=SB)
        k_tok = at(V0, 9, 512)
        hi_only = m["arena"][0:NS, W0 + GT:W0 + GT + SB * 512].rearrange("p (b n) -> p b n", b=SB)
        loaded = sem("hgrn_loaded")
        step_act = sem("hgrn_act")
        step_dve = sem("hgrn_dve")
        turn_ready = sem("hgrn_turn_ready")
        turn_copied = sem("hgrn_turn_copied")
        pair_ready = sem("hgrn_pair_ready")
        masked_ready = sem("hgrn_masked_ready")
        update_ready = sem("hgrn_update_ready")
        update_read = sem("hgrn_update_read")
        state_ready = sem("hgrn_state_ready")
        out_ready = sem("hgrn_out_ready")
        out_copied = sem("hgrn_out_copied")
        squared = sem("hgrn_squared")
        summed = sem("hgrn_summed")
        stored = sem("hgrn_stored")
        settled = {e: sem(f"hgrn_settled_{e}") for e in ("pe", "act", "dve")}
        block = c.enter_context(nc.Block())

        @block.sync
        def _(sp):
            for dst, name in ((resets, "resets"), (causal, "causal"), (causal_s[0:NS], "causal_s"), (only[0:NS], "only"),
                              (logits, "lb_logits"), (hnorm, "hgrn_norm"), (state_s, "state")):
                sp.dma_start(dst, x[name]).then_inc(loaded, 16)
            sp.wait_ge(step_dve, 6)
            sp.dma_start(x["hgrn_p"], sum_state).then_inc(stored, 16)
            sp.dma_start(x["hgrn_s"], state_s).then_inc(stored, 16)
            sp.wait_ge(stored, 32)

        @block.scalar
        def _(act):
            act.wait_ge(loaded, 16 * 7)
            act.wait_ge(step_dve, 1)
            act.activation(lbt[:, 1:3, :], lbt[:, 1:3, :], ACT.Exp).then_inc(step_act, 1)
            act.activation(b, b, ACT.Sigmoid).then_inc(step_act, 1)
            act.wait_ge(step_dve, 2)
            act.activation(b, b, ACT.Ln).then_inc(step_act, 1)
            act.wait_ge(step_dve, 3)
            act.activation(ek, eq, ACT.Exp, scale=-1.0)
            act.drain()
            act.activation(eq, eq, ACT.Exp)
            act.activation(carry[:, :, 1:], carry[:, :, 1:], ACT.Exp)
            act.activation(carry_s, carry_s, ACT.Exp).then_inc(step_act, 1)
            act.activation(q, q, ACT.Silu).then_inc(step_act, 1)
            act.activation(gate, gate, ACT.Silu).then_inc(step_act, 1)
            for t in range(9):
                rows = P if t < TT else NS
                act.wait_ge(turn_ready, t + 1)
                act.copy(k_tok[0:rows, t, :], psum[0:rows, t % 2, :]).then_inc(turn_copied, 1)
            act.wait_ge(step_dve, 7)
            act.activation(ek, ek, ACT.Sqrt).then_inc(step_act, 1)

        @block.tensor
        def _(pe):
            pe.wait_ge(step_dve, 4)
            for t in range(9):
                rows = P if t < TT else NS
                if t >= 2:
                    pe.wait_ge(turn_copied, t - 1)
                for g in range(G):
                    last = pe.transpose(psum[0:rows, t % 2, g * P:(g + 1) * P], k[:, g, t * P:t * P + rows],
                                        m["ident"])
                last.then_inc(turn_ready, 1)
            pe.wait_ge(turn_copied, 9)
            for t in range(TT):
                tok = slice(t * P, (t + 1) * P)
                if t >= 1:
                    pe.wait_ge(masked_ready, t)
                for g in range(G):
                    last = pe.matmul(psum[:, 2, g * P:(g + 1) * P], k[:, g, tok], q[:, g, tok],
                                     start=True, stop=True)
                last.then_inc(pair_ready, 1)
                for j in range(4):
                    if t >= 1:
                        pe.wait_ge(update_read, 4 * (4 * t + j) - 12)
                    rows = slice(CH * j, CH * j + CH)
                    for g in range(G):
                        last = pe.matmul(psum[:, 4 + j, g * P:(g + 1) * P], k_tok[rows, t, g * P:(g + 1) * P],
                                         hi[rows, t, g * P:(g + 1) * P], start=True, stop=True)
                    last.then_inc(update_ready, 1)
                pe.wait_ge(masked_ready, t + 1)
                if t >= 1:
                    pe.wait_ge(out_copied, t)
                for g in range(G):
                    pe.matmul(psum[:, 3, g * P:(g + 1) * P], hi[:, t, g * P:(g + 1) * P], masked[:, g, :],
                              start=g == 0, stop=False, skip_group_check=True)
                for j in range(4):
                    n = 4 * t + j
                    pe.wait_ge(state_ready, n + 1)
                    for g in range(G):
                        last = pe.matmul(psum[:, 3, g * P + CH * j:g * P + CH * j + CH], state[:, g, n % 2, :],
                                         q[:, g, n * CH:n * CH + CH], start=False, stop=j == 3,
                                         skip_group_check=True)
                    last.then_inc(out_ready, 1)
            tok = slice(SEQ, T)
            pe.wait_ge(masked_ready, TT)
            for g in range(G):
                last = pe.matmul(psum[0:NS, 2, g * NS:(g + 1) * NS], k[:, g, tok], q[:, g, tok],
                                 start=True, stop=True)
            last.then_inc(pair_ready, 1)
            pe.wait_ge(masked_ready, TT + 1)
            pe.wait_ge(out_copied, TT)
            for g in range(G):
                pe.matmul(psum[:, 3, g * NS:(g + 1) * NS], hi[0:NS, TT, g * P:(g + 1) * P],
                          masked[0:NS, g, 0:NS], start=g == 0, stop=False, skip_group_check=True)
            pe.wait_ge(step_dve, 5)
            for g in range(G):
                for s in range(SB):
                    last = pe.matmul(psum[:, 3, g * NS + ST * s:g * NS + ST * s + ST], state_s[:, g, s, :],
                                     q[:, g, SEQ + ST * s:SEQ + ST * s + ST], start=False, stop=s == SB - 1,
                                     skip_group_check=True)
            last.then_inc(out_ready, 1)
            for n in range(2 * G):
                g, half = divmod(n, 2)
                if n < 4:
                    pe.wait_ge(update_read, 4 * NCH)
                else:
                    pe.wait_ge(update_read, 4 * NCH + n - 3)
                last = pe.matmul(psum[:, 4 + n % 4, :].rearrange("p (b v) -> p b v", b=4),
                                 k_tok[0:NS, TT, g * P:(g + 1) * P],
                                 hi_only[:, 4 * half:4 * half + 4, g * P:(g + 1) * P], start=True, stop=True)
                last.then_inc(update_ready, 1)
            for g in range(G):
                pe.wait_ge(squared, g + 1)
                if g >= 2:
                    pe.wait_ge(summed, g - 1)
                if g == 0:
                    pe.wait_ge(update_read, 4 * NCH + 2 * G)
                for s in range(NSL):
                    last = pe.matmul(psum[:, 4 * (g % 2) + s, 0:SL], m["ones"],
                                     eq[:, g, s * SL:(s + 1) * SL], start=True, stop=True)
                last.then_inc(turn_ready, 1)

        @block.vector
        def _(dve):
            dve.wait_ge(loaded, 16 * 7)
            dve.tensor_tensor(lbt[:, 0, :], logits[:, 0, :], logits[:, 1, :], ALU.max)
            dve.drain()
            for i in range(2):
                last = dve.tensor_tensor(lbt[:, 1 + i, :], logits[:, i, :], lbt[:, 0, :], ALU.subtract)
            last.then_inc(step_dve, 1)
            dve.wait_ge(step_act, 1)
            dve.tensor_tensor(lbt[:, 3, :], lbt[:, 1, :], lbt[:, 2, :], ALU.add)
            dve.drain()
            dve.reciprocal(lbt[:, 4, :], lbt[:, 3, :])
            dve.drain()
            dve.tensor_tensor(lbt[:, 5, :], lbt[:, 1, :], lbt[:, 4, :], ALU.mult)
            dve.drain()
            dve.tensor_scalar(lbt[:, 6, :], lbt[:, 5, :], -1.0, 1.0, ALU.mult, ALU.add)
            dve.drain()
            dve.wait_ge(step_act, 2)
            for g in range(G):
                dve.tensor_scalar(b[:, g, :], b[:, g, :], lbt[:, 6, g:g + 1], lbt[:, 5, g:g + 1], ALU.mult, ALU.add)
            dve.drain()
            dve.tensor_scalar(k, b, -1.0, 1.0, ALU.mult, ALU.add)
            dve.drain().then_inc(step_dve, 1)
            dve.wait_ge(step_act, 3)
            for g in range(G):
                dve.tensor_tensor_scan(ek[:, g, :], resets, b[:, g, :], 0.0, ALU.mult, ALU.add)
            dve.drain()
            mid, mid_s = CH // 2 - 1, ST // 2 - 1
            chunks = ek[:, :, 0:SEQ].rearrange("p g (n c) -> p g n c", c=CH)
            chunks_s = ek[:, :, SEQ:T].rearrange("p g (n c) -> p g n c", c=ST)
            for g in range(G):
                dve.tensor_tensor(eq[:, g, 0:SEQ].rearrange("p (n c) -> p n c", c=CH), chunks[:, g],
                                  chunks[:, g, :, mid:mid + 1].broadcast_to([P, NCH, CH]), ALU.subtract)
                dve.tensor_tensor(eq[:, g, SEQ:T].rearrange("p (n c) -> p n c", c=ST), chunks_s[:, g],
                                  chunks_s[:, g, :, mid_s:mid_s + 1].broadcast_to([P, SB, ST]), ALU.subtract)
            dve.drain()
            ends = eq[:, :, 0:SEQ].rearrange("p g (n c) -> p g n c", c=CH)[:, :, :, CH - 1]
            ends_s = eq[:, :, SEQ:T].rearrange("p g (n c) -> p g n c", c=ST)[:, :, :, ST - 1]
            dve.tensor_copy(carry[:, :, NCH], ends[:, :, NCH - 1])
            dve.memset(carry[:, :, 0], 1.0)
            dve.tensor_tensor(carry[:, :, 1:NCH], ends[:, :, 0:NCH - 1], chunks[:, :, 1:NCH, mid], ALU.add)
            dve.tensor_copy(carry_s[:, 0], chunks_s[:, :, :, mid_s])
            dve.tensor_copy(carry_s[:, 1], ends_s)
            dve.drain()
            dve.tensor_scalar(eq, eq, 40.0, -40.0, ALU.min, ALU.max)
            dve.drain().then_inc(step_dve, 1)
            dve.wait_ge(step_act, 4)
            dve.tensor_tensor(k, k, ek, ALU.mult)
            dve.drain()
            dve.wait_ge(step_act, 5)
            dve.tensor_tensor(q, q, eq, ALU.mult)
            dve.memset(sum_state, 0.0)
            dve.drain().then_inc(step_dve, 1)
            for t in range(TT):
                dve.wait_ge(pair_ready, t + 1)
                if t >= 1:
                    dve.wait_ge(out_ready, 4 * t - 3)
                dve.tensor_tensor(masked, psum[:, 2, :].rearrange("p (g t) -> p g t", g=G),
                                  causal.unsqueeze(1).broadcast_to([P, G, P]), ALU.mult).then_inc(masked_ready, 1)
                for j in range(4):
                    n = 4 * t + j
                    if n >= 2:
                        dve.wait_ge(out_ready, n - 1)
                    for g in range(G):
                        last = dve.tensor_scalar(state[:, g, n % 2, :], sum_state[:, g, :], carry[:, g, n:n + 1],
                                                 None, ALU.mult)
                    last.then_inc(state_ready, 1)
                    dve.wait_ge(state_ready, n + 1)
                    dve.wait_ge(update_ready, n + 1)
                    for g in range(G):
                        dve.tensor_tensor(sum_state[:, g, :], state[:, g, n % 2, :],
                                          psum[:, 4 + j, g * P:(g + 1) * P], ALU.add).then_inc(update_read, 1)
                    dve.wait_ge(update_read, 4 * (n + 1))
                dve.wait_ge(out_ready, 4 * t + 4)
                dve.tensor_copy(mix[:, 4:8, t * P:(t + 1) * P],
                                psum[:, 3, :].rearrange("p (g t) -> p g t", g=G)).then_inc(out_copied, 1)
            for g in range(G):
                dve.tensor_scalar(sum_state[:, g, :], sum_state[:, g, :], carry[:, g, NCH:NCH + 1], None, ALU.mult)
            dve.wait_ge(pair_ready, TT + 1)
            dve.tensor_tensor(masked[0:NS, :, 0:NS], psum[0:NS, 2, 0:P].rearrange("p (g t) -> p g t", g=G),
                              causal_s[0:NS].unsqueeze(1).broadcast_to([NS, G, NS]), ALU.mult).then_inc(masked_ready, 1)
            dve.tensor_tensor(state_s, state_s, carry_s[:, 0].unsqueeze(3).broadcast_to([P, G, SB, P]), ALU.mult)
            for s in range(SB):
                dve.tensor_scalar(hi_only[:, s, :], hi[0:NS, TT, :], only[0:NS, s:s + 1], None, ALU.mult)
            dve.drain().then_inc(step_dve, 1)
            dve.wait_ge(out_ready, 4 * TT + 1)
            dve.tensor_copy(mix[:, 4:8, SEQ:T],
                            psum[:, 3, 0:P].rearrange("p (g t) -> p g t", g=G)).then_inc(out_copied, 1)
            for n in range(2 * G):
                g, half = divmod(n, 2)
                dve.wait_ge(update_ready, NCH + n + 1)
                dve.tensor_tensor(state_s[:, g, 4 * half:4 * half + 4, :], state_s[:, g, 4 * half:4 * half + 4, :],
                                  psum[:, 4 + n % 4, :].rearrange("p (b v) -> p b v", b=4),
                                  ALU.add).then_inc(update_read, 1)
            dve.drain()
            dve.tensor_tensor(state_s, state_s, carry_s[:, 1].unsqueeze(3).broadcast_to([P, G, SB, P]), ALU.mult)
            dve.drain().then_inc(step_dve, 1)
            dve.tensor_tensor(eq, mix[:, 4:8, :], mix[:, 4:8, :], ALU.mult)
            dve.drain().then_inc(squared, G)
            for g in range(G):
                dve.wait_ge(turn_ready, 9 + g + 1)
                first = 0 if g % 2 == 0 else 4
                for s in range(NSL):
                    last = dve.tensor_scalar(ek[:, g, s * SL:(s + 1) * SL], psum[:, first + s, 0:SL], 1.0 / DK, EPS,
                                             ALU.mult, ALU.add)
                last.then_inc(summed, 1)
            dve.drain().then_inc(step_dve, 1)
            dve.wait_ge(step_act, 7)
            dve.reciprocal(ek, ek)
            dve.drain()
            dve.scalar_tensor_tensor(out=mix[:, 4:8, :], in0=mix[:, 4:8, :], scalar=hnorm, in1=ek,
                                     op0=ALU.mult, op1=ALU.mult)
            dve.drain()
            dve.tensor_tensor(mix[:, 4:8, :], mix[:, 4:8, :], gate, ALU.mult)
            dve.drain()



def attend_sample(nc, x, m):
    psum, at, feat, mix = m["psum"], m["at"], m["feat"], m["mix"]
    KT = NKEY // P
    ROUND = 4
    with ExitStack() as c:
        sem = lambda n: c.enter_context(nc.semaphore(n))
        word = W0
        q_apart = at(word, 4 * SB, NS).rearrange("p (c b) r -> p c b r", c=4); word += 4 * SB * NS
        k_new = at(word, 4, NS); word += 4 * NS
        bias = at(word, 2, NCOL); word += 2 * NCOL
        probs = at(word, 2, NCOL); word += 2 * NCOL
        turned = at(word, KT + 1, P); word += (KT + 1) * P
        top = at(word, 2, 1); neg_top = at(word + 2, 2, 1); total = at(word + 4, 2, 1); inv = at(word + 6, 2, 1)
        word += 8
        keys = [at(word, 4, NKEY), at(F0, 4, NKEY)]
        vals = [at(word + 4 * NKEY, KT, 512), at(F0 + 4 * NKEY, KT, 512)]
        assert word + 4 * NKEY + KT * 512 <= WORDS
        bias_loaded = sem("sample_bias_loaded")
        keys_loaded = [sem(f"keys_loaded{i}") for i in range(2)]
        vals_loaded = [sem(f"vals_loaded{i}") for i in range(2)]
        zeroed = sem("q_zeroed")
        new_ready = sem("new_ready")
        keys_used = sem("keys_used")
        vals_used = sem("vals_used")
        max_ready = sem("sample_max_ready")
        exp_ready = sem("sample_exp_ready")
        probs_ready = sem("sample_probs_ready")
        turn_ready = sem("sample_turn_ready")
        turn_copied = sem("sample_turn_copied")
        out_done = sem("sample_out_done")
        block = c.enter_context(nc.Block())

        @block.sync
        def _(sp):
            sp.dma_start(bias, x["bias_sample"]).then_inc(bias_loaded, 16)

            def load_keys(b):
                if b >= 2:
                    sp.wait_ge(keys_used, b - 1)
                sp.dma_start(keys[b % 2], x["keys_feat"][b]).then_inc(keys_loaded[b % 2], 16)

            def load_vals(b):
                if b >= 2:
                    sp.wait_ge(vals_used, b - 1)
                sp.dma_start(vals[b % 2], x["vals_tok"][b]).then_inc(vals_loaded[b % 2], 16)

            load_keys(0)
            sp.wait_ge(new_ready, 9)
            load_keys(1)
            load_keys(2)
            load_keys(3)
            load_vals(0)
            load_vals(1)
            for b in range(ROUND, SB):
                load_keys(b)
            for b in range(2, SB):
                load_vals(b)

        @block.gpsimd
        def _(pool):
            pool.memset(q_apart, 0.0).then_inc(zeroed, 1)
            pool.tensor_copy(k_new, feat[:, FK, :, SEQ:T]).then_inc(new_ready, 1)

        @block.tensor
        def _(pe):
            def scores(b):
                rows = slice(32 * (b % ROUND), 32 * (b % ROUND) + 32)
                bank = 2 * (b // ROUND)
                pe.wait_ge(keys_loaded[b % 2], 16 * (b // 2 + 1))
                for (k0, k1, where) in ((0, 512, bank), (512, NKEY, bank + 1)):
                    for q in range(4):
                        pe.matmul(psum[rows, where, 0:k1 - k0], q_apart[:, q, b, :], keys[b % 2][:, q, k0:k1],
                                  start=q == 0, stop=q == 3)
                for q in range(4):
                    last = pe.matmul(psum[rows, bank + 1, NKEY - 512:NCOL - 512], q_apart[:, q, b, :], k_new[:, q, :],
                                     start=q == 0, stop=q == 3)
                last.then_inc(keys_used, 1)

            def turn(r):
                pe.wait_ge(probs_ready, r + 1)
                if r >= 1:
                    pe.wait_ge(turn_copied, 2 * r)
                for k in range(KT + 1):
                    cols = P if k < KT else NS
                    last = pe.transpose(psum[0:cols, 4 + k // 4, (k % 4) * P:(k % 4 + 1) * P],
                                        probs[:, r, k * P:k * P + cols], m["ident"])
                last.then_inc(turn_ready, 1)

            def values(b):
                r, col = b // ROUND, 32 * (b % ROUND)
                pe.wait_ge(turn_copied, 2 * r + 2)
                pe.wait_ge(vals_loaded[b % 2], 16 * (b // 2 + 1))
                for q in range(4):
                    out = psum[:, 6 + r, (4 * (b % ROUND) + q) * 8:(4 * (b % ROUND) + q) * 8 + 8]
                    for k in range(KT):
                        pe.matmul(out, vals[b % 2][:, k, q * P:(q + 1) * P],
                                  turned[:, k, col + 8 * q:col + 8 * q + 8], start=k == 0, stop=False)
                    last = pe.matmul(out, m["v"][0:NS, TT, q * P:(q + 1) * P],
                                     turned[0:NS, KT, col + 8 * q:col + 8 * q + 8], start=False, stop=True)
                last.then_inc(vals_used, 1)

            pe.wait_ge(new_ready, 9)
            for b in range(SB):
                scores(b)
            for r in range(2):
                turn(r)
                for b in range(ROUND * r, ROUND * r + ROUND):
                    values(b)

        @block.vector
        def _(dve):
            dve.wait_ge(zeroed, 1)
            for h in range(H):
                r = slice(64 * (h % 2), 64 * (h % 2) + 64)
                dve.tensor_copy(q_apart[r, h // 2, :, ST * h:ST * h + ST],
                                feat[r, FQ, h // 2, SEQ:T].rearrange("p (b i) -> p b i", b=SB)).then_inc(new_ready, 1)
            dve.wait_ge(bias_loaded, 16)

            def add_bias(r):
                dve.wait_ge(keys_used, ROUND * r + ROUND)
                scores = psum[:, 2 * r:2 * r + 2, :].rearrange("p a b -> p (a b)")
                dve.tensor_tensor_reduce(probs[:, r, :], scores[:, 0:NCOL], bias[:, r, :], 1.0, LOWEST,
                                         ALU.add, ALU.max, top[:, r, :])
                dve.drain()
                dve.tensor_scalar(neg_top[:, r, :], top[:, r, :], -1.0, None, ALU.mult).then_inc(max_ready, 1)

            def normalize(r):
                dve.wait_ge(exp_ready, r + 1)
                dve.reciprocal(inv[:, r, :], total[:, r, :])
                dve.drain()
                dve.tensor_scalar(probs[:, r, :], probs[:, r, :], inv[:, r, :], None,
                                  ALU.mult).then_inc(probs_ready, 1)

            def write_out(r):
                dve.wait_ge(vals_used, ROUND * r + ROUND)
                for half in range(2):
                    rows = slice(64 * half, 64 * half + 64)
                    new = slice(SEQ + ROUND * ST * r, SEQ + ROUND * ST * (r + 1))
                    dve.tensor_copy(
                        mix[rows, 0:4, new].rearrange("p c (b i) -> p b c i", b=ROUND),
                        psum[rows, 6 + r, 0:P].rearrange("p (b c e) -> p b c e", b=ROUND, c=4)[
                            :, :, :, ST * half:ST * half + ST]).then_inc(out_done, 1)

            add_bias(0)
            normalize(0)
            add_bias(1)
            normalize(1)
            write_out(0)
            write_out(1)
            dve.wait_ge(out_done, 4)

        @block.scalar
        def _(act):
            def exps(r):
                act.wait_ge(max_ready, r + 1)
                act.activation(probs[:, r, :], probs[:, r, :], ACT.Exp, bias=neg_top[:, r, :],
                               accum_out=total[:, r, :]).then_inc(exp_ready, 1)

            def copy_turned(r):
                act.wait_ge(turn_ready, r + 1)
                if r >= 1:
                    act.wait_ge(vals_used, ROUND * r)
                act.copy(turned[:, 0:4, :], psum[:, 4, :].rearrange("p (a b) -> p a b", a=4)).then_inc(turn_copied, 1)
                act.copy(turned[:, 4:KT, :],
                         psum[:, 5, 0:(KT - 4) * P].rearrange("p (a b) -> p a b", a=KT - 4))
                act.copy(turned[0:NS, KT, :], psum[0:NS, 5, (KT - 4) * P:(KT - 3) * P]).then_inc(turn_copied, 1)

            exps(0)
            exps(1)
            copy_turned(0)
            copy_turned(1)



def project_out(nc, x, m):
    psum, at, arena, mix, xn = m["psum"], m["at"], m["arena"], m["mix"], m["xn"]
    h, scores = m["h"], m["scores"]
    HALF = 2 * PH
    with ExitStack() as c:
        sem = lambda n: c.enter_context(nc.semaphore(n))
        w_out = at(S0, DC, D)
        word = W3
        x_tile = at(word, 2, D); word += 2 * D
        normed = at(word, 2, D); word += 2 * D
        wq = at(word, 2, DC, P); word += 2 * DC * P
        query = at(word, 2, T); word += 2 * T
        word_keys = word
        keys = at(word, HALF, PK); word += HALF * PK
        junk = at(word, D); word += D
        ms = at(word, 9); word += 9
        assert word <= WORDS
        weights_loaded = sem("out_weights_loaded")
        x_loaded = [sem(f"x_tile_loaded{i}") for i in range(2)]
        wq_loaded = [sem(f"wq_loaded{i}") for i in range(2)]
        mixed = sem("mixed")
        added = sem("added")
        rms_ready = sem("rms2_ready")
        normed_ready = sem("normed_ready")
        turn_ready = sem("normed_turned")
        turn_copied = sem("normed_copied")
        query_ready = sem("query_ready")
        query_copied = sem("query_copied")
        scored = sem("scored")
        score_copied = sem("score_copied")
        settled = {e: sem(f"out_settled_{e}") for e in ("pe", "dve")}
        block = c.enter_context(nc.Block())

        @block.sync
        def _(sp):
            sp.dma_start(w_out, x["w_out"]).then_inc(weights_loaded, 16)
            sp.dma_start(m["norm2"], x["norm2"]).then_inc(weights_loaded, 16)
            sp.dma_start(keys, x["sub_keys"]).then_inc(weights_loaded, 16)
            for p in range(2):
                sp.dma_start(wq[:, p], x["wq"][p]).then_inc(wq_loaded[p], 16)
            for t in range(9):
                rows = P if t < TT else NS
                if t >= 2:
                    sp.wait_ge(added, t - 1)
                sp.dma_start(x_tile[0:rows, t % 2, :], x["x_tok"][t * P:t * P + rows, :]).then_inc(x_loaded[t % 2], 16)
            with sp.Fori(1, PH) as i:
                for p in range(2):
                    sp.wait_ge(query_ready, i * 2 + p - 1)
                    sp.dma_start(wq[:, p], x["wq"][bass.ds(i * 2 + p, 1)].squeeze(0)).then_inc(wq_loaded[p], 16)

        @block.tensor
        def _(pe):
            def mix_out(t):
                rows = P if t < TT else NS
                if t >= 2:
                    pe.wait_ge(added, t - 1)
                for s in range(2):
                    for q in range(DC):
                        last = pe.matmul(psum[0:rows, 2 * (t % 2) + s, :], mix[:, q, t * P:t * P + rows],
                                         w_out[:, q, s * 512:(s + 1) * 512], start=q == 0, stop=q == DC - 1)
                last.then_inc(mixed, 1)

            def turn(t):
                rows = P if t < TT else NS
                pe.wait_ge(normed_ready, t + 1)
                if t >= 2:
                    pe.wait_ge(turn_copied, t - 1)
                for q in range(DC):
                    last = pe.transpose(psum[:, 4 + 2 * (t % 2) + q // 4, (q % 4) * P:(q % 4) * P + rows],
                                        normed[0:rows, t % 2, q * P:(q + 1) * P], m["ident"][0:rows, 0:rows])
                last.then_inc(turn_ready, 1)

            pe.wait_ge(weights_loaded, 48)
            for t in range(9):
                mix_out(t)
                if t >= 1:
                    turn(t - 1)
            turn(8)
            pe.wait_ge(turn_copied, 9)
            with pe.Fori(0, PH) as i:
                for p in range(2):
                    pe.wait_ge(wq_loaded[p], i * 16 + 16)
                    pe.sem_inc(settled["pe"], 1)
                    pe.wait_ge(query_copied, i * 2 + p + 1)
                    for s in range(NSL):
                        for q in range(DC):
                            last = pe.matmul(psum[:, s, 0:SL], wq[:, p, q, :], xn[:, q, s * SL:(s + 1) * SL],
                                             start=q == 0, stop=q == DC - 1)
                    last.then_inc(query_ready, 1)
                    pe.wait_ge(query_copied, i * 2 + p + 2)
                    pe.sem_inc(settled["pe"], 1)
                    for b in range(3):
                        pe.wait_ge(score_copied, i * 6 + 3 * p + b + 1)
                        pe.sem_inc(settled["pe"], 1)
                        for t in range(4 * b, min(9, 4 * b + 4)):
                            rows = P if t < TT else NS
                            last = pe.matmul(psum[0:rows, 3 + b, (t % 4) * P:(t % 4 + 1) * P],
                                             query[:, p, t * P:t * P + rows],
                                             arena[:, bass.ds(word_keys + i * 2 * PK + p * PK, PK)],
                                             start=True, stop=True)
                        last.then_inc(scored, 1)

        @block.vector
        def _(dve):
            for t in range(9):
                rows = P if t < TT else NS
                dve.wait_ge(mixed, t + 1)
                dve.wait_ge(x_loaded[t % 2], 16 * (t // 2 + 1))
                dve.tensor_tensor(h[0:rows, t, :], x_tile[0:rows, t % 2, :],
                                  psum[0:rows, 2 * (t % 2):2 * (t % 2) + 2, :].rearrange("p a b -> p (a b)"),
                                  ALU.add).then_inc(added, 1)
                dve.wait_ge(rms_ready, t + 1)
                dve.reciprocal(m["rstd2"][0:rows, t:t + 1], ms[0:rows, t:t + 1])
                dve.drain()
                if t >= 2:
                    dve.wait_ge(turn_ready, t - 1)
                dve.scalar_tensor_tensor(out=normed[0:rows, t % 2, :], in0=h[0:rows, t, :],
                                         scalar=m["rstd2"][0:rows, t:t + 1], in1=m["norm2"][0:rows],
                                         op0=ALU.mult, op1=ALU.mult).then_inc(normed_ready, 1)
            dve.sem_inc(query_copied, 1)
            dve.sem_inc(score_copied, 3)
            with dve.Fori(0, PH) as i:
                for p in range(2):
                    dve.wait_ge(query_ready, i * 2 + p + 1)
                    dve.sem_inc(settled["dve"], 1)
                    for s in range(NSL):
                        last = dve.tensor_copy(query[:, p, s * SL:(s + 1) * SL], psum[:, s, 0:SL])
                    last.then_inc(query_copied, 1)
                    for b in range(3):
                        tiles = min(9, 4 * b + 4) - 4 * b
                        rows = P if b < 2 else NS
                        dve.wait_ge(scored, i * 6 + 3 * p + b + 1)
                        dve.tensor_scalar(
                            arena[0:rows, S0:S0 + 9 * 2048].rearrange("p (t n) -> p t n", t=9)[
                                :, 4 * b:4 * b + tiles, bass.ds(i * 2 * PK + p * PK, PK)],
                            psum[0:rows, 3 + b, 0:tiles * P].rearrange("p (a b) -> p a b", b=P), 1.0, None,
                            ALU.mult).then_inc(score_copied, 1)

        @block.scalar
        def _(act):
            for t in range(9):
                rows = P if t < TT else NS
                act.wait_ge(added, t + 1)
                act.activation(junk[0:rows], h[0:rows, t, :], ACT.Square, accum_out=ms[0:rows, t:t + 1])
                act.drain()
                act.activation(ms[0:rows, t:t + 1], ms[0:rows, t:t + 1], ACT.Sqrt, bias=m["eps"][0:rows],
                               scale=1.0 / D).then_inc(rms_ready, 1)
                act.wait_ge(turn_ready, t + 1)
                act.copy(xn[:, 0:4, t * P:t * P + rows],
                         psum[:, 4 + 2 * (t % 2), :].rearrange("p (a b) -> p a b", a=4)[:, :, 0:rows])
                act.copy(xn[:, 4:8, t * P:t * P + rows],
                         psum[:, 5 + 2 * (t % 2), :].rearrange("p (a b) -> p a b", a=4)[:, :, 0:rows])\
                   .then_inc(turn_copied, 1)
                act.drain()


def experts(nc, x, m, windows_shifted):
    psum, at, arena = m["psum"], m["at"], m["arena"]
    h, scores = m["h"], m["scores"]
    RING = 4
    with ExitStack() as c:
        sem = lambda n: c.enter_context(nc.semaphore(n))
        word = 0
        top_in = at(word, 16, PK); word += 2048
        left = at(word, 16, PK); word += 2048
        sums = at(word, PH, 256); word += 2048
        hot = at(word, 2 * P, 16); word += 4096 - 1792
        word = 2048 * 3
        word = W3
        ring_u = at(word, RING, D); word += RING * D
        ring_v = at(word, RING, D); word += RING * D
        xn2 = at(word, D); word += D
        final = at(word, D); word += D
        val = at(word, 16, 16); word += 256
        idx = at(word, 16, 16); word += 256
        idx_f = at(word, 16, 16); word += 256
        best = at(word, PH, 16); word += 128
        best_i = at(word, P); word += 128
        parts_i = at(word, 2, P); word += 256
        parts = at(word, 2, P); word += 256
        picked = at(word, 2, P); word += 256
        expert = at(word, P); word += 128
        gate = at(word, PH, 16); word += 128
        gate_n = at(word, P); word += 128
        den = at(word, 2, PH); word += 16
        act_in = at(word, P); word += 128
        weight = at(word, P); word += 128
        diag = at(word, RING, P); word += RING * P
        norm_f = at(word, D); word += D
        rms = at(word, 2); word += 2
        assert word <= WORDS, word
        one_hot = [at(6144, P, 16), at(4096, P, 16)]
        inner = at(6144, PH, 256)
        loaded = sem("final_loaded")
        tile_in = sem("tile_in")
        gate_ready = sem("gate_ready")
        exp_done = sem("gate_exp_done")
        experts_ready = sem("experts_ready")
        u_loaded = [sem(f"u_loaded{i}") for i in range(RING)]
        v_loaded = [sem(f"v_loaded{i}") for i in range(RING)]
        u_used = sem("u_used")
        v_used = sem("v_used")
        acts_ready = sem("acts_ready")
        gelu_done = sem("gelu_done")
        weights_ready = sem("weights_ready")
        diag_ready = sem("diag_ready")
        residual_in = sem("residual_in")
        y_read = sem("y_read")
        final_ready = sem("final_ready")
        stored = sem("y_stored")
        settled = {e: sem(f"ex_settled_{e}") for e in ("pool", "act", "dve", "pe", "sp")}
        block = c.enter_context(nc.Block())

        @block.sync
        def _(sp):
            sp.dma_start(norm_f, x["norm_f"]).then_inc(loaded, 16)
            for t in range(9):
                rows = P if t < TT else NS
                sp.wait_ge(final_ready, t + 1)
                sp.dma_start(x["y"][t * P:t * P + rows, :], final[0:rows]).then_inc(stored, 16)
            sp.wait_ge(stored, 16 * 9)
            sp.wait_ge(windows_shifted, 16 * 2 * SB)

        @block.gpsimd
        def _(pool):
            for t in range(9):
                rows = P if t < TT else NS
                pool.wait_ge(experts_ready, t + 1)
                for n in range(P):
                    k = t * P + n
                    off = bass.IndirectOffsetOnAxis(expert[0:rows, n:n + 1].bitcast(U32), 0)
                    if k >= RING:
                        pool.wait_ge(u_used, k - RING + 1)
                    pool.indirect_dma_start(ring_u[0:rows, k % RING, :], None, x["peer_u"], off)\
                        .then_inc(u_loaded[k % RING], 16)
                    if n % 16 == 15:
                        for v in range(n - 15, n + 1):
                            kv = t * P + v
                            offv = bass.IndirectOffsetOnAxis(expert[0:rows, v:v + 1].bitcast(U32), 0)
                            if kv >= RING:
                                pool.wait_ge(v_used, kv - RING + 1)
                            pool.indirect_dma_start(ring_v[0:rows, kv % RING, :], None, x["peer_v"], offv)\
                                .then_inc(v_loaded[kv % RING], 16)

        @block.tensor
        def _(pe):
            for t in range(9):
                rows = P if t < TT else NS
                if t >= 1:
                    pe.wait_ge(y_read, t)
                for s in range(2):
                    pe.matmul(psum[0:rows, s, :], m["ident"][0:rows, 0:rows], h[0:rows, t, s * 512:(s + 1) * 512],
                              start=True, stop=False, skip_group_check=True)
                for n in range(P):
                    k = t * P + n
                    pe.wait_ge(diag_ready, k + 1)
                    pe.wait_ge(v_loaded[k % RING], 16 * (k // RING + 1))
                    for s in range(2):
                        last = pe.matmul(psum[0:rows, s, :], diag[0:rows, k % RING, 0:rows],
                                         ring_v[0:rows, k % RING, s * 512:(s + 1) * 512], start=False,
                                         stop=n == P - 1, skip_group_check=True)
                    last.then_inc(v_used, 1)

        @block.vector
        def _(dve):
            def top16(width, values, where, src, tmp, r):
                for i in range(width):
                    dve.max(values[r, i, 0:8], src[r, i, :])
                dve.drain()
                for i in range(width):
                    dve.max_index(where[r, i, 0:8].bitcast(U32), values[r, i, 0:8], src[r, i, :])
                for i in range(width):
                    dve.match_replace(tmp[r, i, :], values[r, i, 0:8], src[r, i, :], LOWEST)
                dve.drain()
                for i in range(width):
                    dve.max(values[r, i, 8:16], tmp[r, i, :])
                dve.drain()
                for i in range(width):
                    dve.max_index(where[r, i, 8:16].bitcast(U32), values[r, i, 8:16], tmp[r, i, :])
                dve.drain()

            dve.wait_ge(loaded, 16)
            for t in range(9):
                rows = P if t < TT else NS
                r = slice(0, rows)
                src = scores[:, t].rearrange("p (a b) -> p a b", a=16)
                top16(16, val, idx, src, left, r)
                both = val[r].rearrange("p (h f) k -> p h f k", f=2)
                dve.tensor_tensor(sums[r].rearrange("p h (a b) -> p h a b", a=16),
                                  both[:, :, 0, :].unsqueeze(3).broadcast_to([rows, PH, 16, 16]),
                                  both[:, :, 1, :].unsqueeze(2).broadcast_to([rows, PH, 16, 16]), ALU.add)
                dve.tensor_copy(idx_f[r], idx[r].bitcast(U32))
                dve.drain()
                top16(PH, best, best_i.rearrange("p (h k) -> p h k", h=PH), sums, inner, r)
                dve.tensor_tensor(gate[r], best[r], best[r, :, 0:1].broadcast_to([rows, PH, 16]),
                                  ALU.subtract).then_inc(gate_ready, 1)
                bi = best_i[r].bitcast(U32)
                pi = parts_i[r].bitcast(U32)
                dve.tensor_scalar(pi[:, 0, :], bi, 4, None, ALU.logical_shift_right)
                dve.tensor_scalar(pi[:, 1, :], bi, 15, None, ALU.bitwise_and)
                dve.drain()
                dve.tensor_copy(parts[r], pi)
                dve.drain()
                for f in range(2):
                    dve.tensor_tensor(one_hot[f][r], parts[r, f, :].unsqueeze(2).broadcast_to([rows, P, 16]),
                                      m["io16"][r].unsqueeze(1).broadcast_to([rows, P, 16]), ALU.is_equal)
                dve.drain()
                index = idx_f[r].rearrange("p (h f) k -> p h f k", f=2)
                for f in range(2):
                    o = one_hot[f][r].rearrange("p (h k) j -> p h k j", h=PH)
                    dve.tensor_tensor(o, o, index[:, :, f, :].unsqueeze(2).broadcast_to([rows, PH, 16, 16]), ALU.mult)
                dve.drain()
                for f in range(2):
                    dve.tensor_reduce(picked[r, f, :], one_hot[f][r], AX.X, ALU.add)
                dve.drain()
                if t >= 1:
                    dve.wait_ge(v_used, t * P)
                dve.scalar_tensor_tensor(out=expert[r].bitcast(I32), in0=picked[r, 0, :], scalar=float(PK),
                                         in1=picked[r, 1, :], op0=ALU.mult, op1=ALU.add).then_inc(experts_ready, 1)
                dve.wait_ge(exp_done, t + 1)
                dve.tensor_reduce(den[r, 0, :], gate[r], AX.X, ALU.add)
                dve.scalar_tensor_tensor(out=xn2[r], in0=h[r, t, :], scalar=m["rstd2"][r, t:t + 1],
                                         in1=m["norm2"][r], op0=ALU.mult, op1=ALU.mult)
                dve.drain()
                dve.reciprocal(den[r, 1, :], den[r, 0, :])
                dve.drain()
                dve.tensor_tensor(gate_n[r].rearrange("p (h k) -> p h k", h=PH), gate[r],
                                  den[r, 1, :].unsqueeze(2).broadcast_to([rows, PH, 16]), ALU.mult)
                dve.drain()
                for g in range(PH):
                    for n in range(16 * g, 16 * g + 16):
                        k = t * P + n
                        dve.wait_ge(u_loaded[k % RING], 16 * (k // RING + 1))
                        dve.tensor_tensor_reduce(ring_u[r, k % RING, :], ring_u[r, k % RING, :], xn2[r], 1.0, 0.0,
                                                 ALU.mult, ALU.add, act_in[r, n:n + 1]).then_inc(u_used, 1)
                    dve.drain().then_inc(acts_ready, 1)
                    dve.wait_ge(gelu_done, t * PH + g + 1)
                    dve.tensor_tensor(weight[r, 16 * g:16 * g + 16], weight[r, 16 * g:16 * g + 16],
                                      gate_n[r, 16 * g:16 * g + 16], ALU.mult).then_inc(weights_ready, 1)
                dve.wait_ge(v_used, (t + 1) * P)
                if t >= 1:
                    dve.wait_ge(stored, 16 * t)
                dve.tensor_copy(final[r], psum[r, 0:2, :].rearrange("p a b -> p (a b)")).then_inc(y_read, 1)
                dve.wait_ge(y_read, t + 1)
                dve.tensor_tensor_reduce(xn2[r], final[r], final[r], 1.0, 0.0, ALU.mult, ALU.add, rms[r, 0:1])
                dve.drain()
                dve.sem_inc(residual_in, 1)
                dve.wait_ge(settled["act"], t + 1)
                dve.reciprocal(rms[r, 1:2], rms[r, 1:2])
                dve.drain()
                dve.scalar_tensor_tensor(out=final[r], in0=final[r], scalar=rms[r, 1:2], in1=norm_f[r],
                                         op0=ALU.mult, op1=ALU.mult).then_inc(final_ready, 1)

        @block.scalar
        def _(act):
            for t in range(9):
                rows = P if t < TT else NS
                r = slice(0, rows)
                act.wait_ge(gate_ready, t + 1)
                act.activation(gate[r], gate[r], ACT.Exp).then_inc(exp_done, 1)
                for g in range(PH):
                    act.wait_ge(acts_ready, t * PH + g + 1)
                    act.activation(weight[r, 16 * g:16 * g + 16], act_in[r, 16 * g:16 * g + 16],
                                   ACT.Gelu).then_inc(gelu_done, 1)
                    act.wait_ge(weights_ready, t * PH + g + 1)
                    for n in range(16 * g, 16 * g + 16):
                        k = t * P + n
                        if k >= RING:
                            act.wait_ge(v_used, k - RING + 1)
                        act.activation(diag[r, k % RING, 0:rows], m["ident"][r, 0:rows], ACT.Copy,
                                       scale=weight[r, n:n + 1]).then_inc(diag_ready, 1)
                act.wait_ge(residual_in, t + 1)
                act.activation(rms[r, 1:2], rms[r, 0:1], ACT.Sqrt, bias=m["eps"][r], scale=1.0 / D)\
                   .then_inc(settled["act"], 1)


def log_count(distance):
    import numpy as np
    count = sum(((distance >= 0) & (distance <= window) & (distance % dilation == 0)).astype(np.int64)
                for window, dilation in ((128, 1), (512, 4), (2048, 16)))
    return np.where(count > 0, np.log(np.maximum(count, 1)), -1.0e30).astype(np.float32)


def prompt_bias():
    import numpy as np
    return log_count(np.arange(P)[:, None] + (SEQ - P) - np.arange(SEQ)[None, :])


def key_positions():
    import numpy as np
    far = np.arange(0, NB - NRECENT).reshape(-1, 16)[:, :ST].reshape(-1)
    assert len(far) == NSPARSE
    return np.concatenate([far, np.arange(NB - NRECENT, NB)])


def sample_bias():
    import numpy as np
    i = np.arange(ST)
    cached = log_count(NB + i[:, None] - key_positions()[None, :])
    own = np.where(i[:, None] >= i[None, :], log_count(i[:, None] - i[None, :]), np.float32(-1.0e30))
    new = np.full((SB, ST, SB, ST), -1.0e30, np.float32)
    for s in range(SB):
        new[s, :, s, :] = own
    rows = np.concatenate([np.broadcast_to(cached, (SB, ST, NKEY)), new.reshape(SB, ST, NS)], 2)
    rows = np.broadcast_to(rows[:, None], (SB, H, ST, NCOL)).reshape(2, P, NCOL)
    return rows.transpose(1, 0, 2).astype(np.float32)


def hgrn_constants():
    import numpy as np
    t = np.arange(T)
    chunk = np.where(t < SEQ, t // CH, NCH + (t - SEQ) // ST)
    same = lambda a: (chunk[a][:, None] == chunk[a][None, :]) & (t[a][:, None] <= t[a][None, :])
    resets = np.concatenate([[0.0], chunk[1:] == chunk[:-1]])
    return {
        "resets": np.broadcast_to(resets, (P, T)).astype(np.float32),
        "causal": same(slice(0, P)).astype(np.float32),
        "causal_s": same(slice(SEQ, T)).astype(np.float32),
        "only": (np.arange(NS)[:, None] // ST == np.arange(SB)[None, :]).astype(np.float32),
    }


def kernel(**inputs):
    import numpy as np
    import concourse.bacc as bacc
    from concourse.bass_utils import run_bass_kernel_spmd

    a = {k: np.asarray(v) for k, v in inputs.items()}
    x_all = np.concatenate([a["x_prompt"].reshape(SEQ, D), a["x_sample"].reshape(NS, D)], 0)
    w = a["w_in"][0].reshape(D, 7, 512)
    w = np.stack([w[:, i] for i in (0, 1, 3, 4, 6, 2, 5)])
    w = w.reshape(7, DC, P, 2, 256).transpose(0, 3, 2, 1, 4)
    ck = a["cache_k_win"][0].reshape(SB, NB, H * DH)
    cv = a["cache_v_win"][0].reshape(SB, NB, H * DH)
    chunked = lambda t: t.reshape(-1, P).T
    arrays = {
        "x_feat": x_all.T.reshape(DC, P, T).transpose(1, 0, 2),
        "x_tok": x_all,
        "norm1": chunked(a["norm1_w"][0]),
        "w_in": w.reshape(14, P, DC, 256),
        "bias_prompt": prompt_bias(),
        "bias_sample": sample_bias(),
        **hgrn_constants(),
        "keys_feat": ck[:, key_positions()].transpose(0, 2, 1).reshape(SB, 4, P, NKEY).transpose(0, 2, 1, 3),
        "vals_tok": cv[:, key_positions()].reshape(SB, NKEY // P, P, 512).transpose(0, 2, 1, 3),
        "lb_logits": a["hgrn_lb_logits"].reshape(2, G, P).transpose(2, 0, 1),
        "w_out": a["w_out"][0].reshape(DC, P, D).transpose(1, 0, 2),
        "norm2": np.broadcast_to(a["norm2_w"][0], (P, D)),
        "norm_f": np.broadcast_to(a["norm_f_w"], (P, D)),
        "wq": a["peer_wq"][0].reshape(DC, P, 2 * PH, P).transpose(2, 1, 0, 3),
        "sub_keys": a["peer_sub_keys"][0].reshape(2 * PH, PK, P).transpose(2, 0, 1),
        "peer_u": a["peer_u"][0],
        "peer_v": a["peer_v"][0],
        "hgrn_norm": a["hgrn_norm_w"][0].reshape(P, 1),
        "state": a["state_hgrn"][0].transpose(2, 1, 0, 3),
        "cache_k": ck,
        "cache_v": cv,
    }
    arrays = {k: np.ascontiguousarray(v) for k, v in arrays.items()}
    outs = {
        "y": (T, D), "k_feat_out": (P, 4, T), "v_out": (P, TT, 512), "v_out_s": (NS, 512),
        "k_win_sample": (SB, NB, 512), "v_win_sample": (SB, NB, 512),
        "hgrn_p": (P, G, P), "hgrn_s": (P, G, SB, P),
    }
    nc = bacc.Bacc("TRN2", target_bir_lowering=False, num_devices=1)
    x = {k: nc.dram_tensor(f"in_{k}", v.shape, mybir.dt.from_np(v.dtype), kind="ExternalInput").ap()
         for k, v in arrays.items()}
    x.update({k: nc.dram_tensor(f"out_{k}", s, F32, kind="ExternalOutput").ap() for k, s in outs.items()})
    build(nc, x)
    r = run_bass_kernel_spmd(nc, [{f"in_{k}": v for k, v in arrays.items()}], core_ids=[0]).results[0]
    got = {k: np.asarray(r[f"out_{k}"]) for k in outs}
    k_all = got["k_feat_out"].transpose(2, 1, 0).reshape(T, 512)
    v_all = got["v_out"].transpose(1, 0, 2).reshape(SEQ, 512)
    kw, vw = got["k_win_sample"], got["v_win_sample"]
    kw = np.concatenate([kw[:, :NB - ST], k_all[SEQ:].reshape(SB, ST, 512)], 1)
    vw = np.concatenate([vw[:, :NB - ST], got["v_out_s"].reshape(SB, ST, 512)], 1)
    win = (1, SB, NB, H, DH)
    return (
        got["y"][:SEQ].reshape(1, SEQ, D),
        got["y"][SEQ:].reshape(SB, ST, D),
        np.ascontiguousarray(k_all[:SEQ]).reshape(1, 1, SEQ, H, DH),
        np.ascontiguousarray(v_all).reshape(1, 1, SEQ, H, DH),
        np.ascontiguousarray(got["hgrn_p"].transpose(1, 0, 2)).reshape(1, 1, G, DK, DK),
        kw.reshape(win), vw.reshape(win),
        np.ascontiguousarray(got["hgrn_s"].transpose(2, 1, 0, 3)).reshape(1, SB, G, DK, DK),
    )
```

```python
from contextlib import ExitStack

import concourse.bass as bass
from concourse import mybir

F32 = mybir.dt.float32
F16 = mybir.dt.float16
I32 = mybir.dt.int32
U32 = mybir.dt.uint32
ALU = mybir.AluOpType
ACT = mybir.ActivationFunctionType
AX = mybir.AxisListType

P = 128
D = 1024
DC = D // P
SEQ = 1024
SB, ST = 8, 4
NS = SB * ST
T = SEQ + NS
TT = SEQ // P
SL = 352
NSL = T // SL
H, DH = 8, 64
G, DK = 4, 128
NB = 2048
EPS = 1e-6
EXPERTS = 16384
PH, PK, TOPK = 8, 128, 16
LOWEST = -3.0e38
NSPARSE = 384
NRECENT = 512
NKEY = NSPARSE + NRECENT
NCOL = NKEY + NS
CH = 32
NCH = SEQ // CH

FQ, FK, FHQ, FHF, FHG = range(5)

XT0 = 0
F0 = XT0 + DC * T
V0 = F0 + 5 * 4 * T
HI0 = V0 + 9 * 512
W0 = HI0 + 9 * 512
WORDS = 52880
XH0 = WORDS - DC * T

PRODUCTS = ((0, 0), (0, 1), (1, 0))
W_SCALE = 16.0
H_SCALE = 16.0
CREDIT = 2
SHIFT = (NB - ST) // 4
SHIFTS = 2 * SB * 4


def flat(ap):
    return ap.rearrange("p a b -> p (a b)")


def build(nc, x):
    with ExitStack() as whole:
        arena = whole.enter_context(nc.sbuf_tensor("arena", [P, WORDS], F32))
        psum = whole.enter_context(nc.psum_tensor("psum", [P, 8, 512], F32))
        consts = whole.enter_context(nc.sbuf_tensor("consts", [P, 288], F32))

        def at(word, *shape):
            n = 1
            for s in shape:
                n *= s
            v = arena[:, word:word + n]
            if len(shape) == 2:
                v = v.rearrange("p (a b) -> p a b", a=shape[0])
            if len(shape) == 3:
                v = v.rearrange("p (a b c) -> p a b c", a=shape[0], b=shape[1])
            return v

        m = {
            "arena": arena, "psum": psum, "at": at,
            "xn": at(XT0, DC, T), "mix": at(XT0, DC, T),
            "feat": at(F0, 5, 4, T), "v": at(V0, 9, 512), "hi": at(HI0, 9, 512),
            "ident": consts[:, 0:128], "ones": consts[:, 128:256], "io16": consts[:, 256:272],
            "eps": consts[:, 272:273],
            "x_hi": at(XH0, DC * T // 2).bitcast(F16).rearrange("p (c t) -> p c t", c=DC),
            "x_lo": at(XH0 + DC * T // 2, DC * T // 2).bitcast(F16).rearrange("p (c t) -> p c t", c=DC),
        }
        done = whole.enter_context(nc.semaphore("windows_shifted"))
        project_in(nc, x, m)
        attend_prompt(nc, x, m)
        attend_sample(nc, x, m)
        hgrn(nc, x, m)
        project_out(nc, x, m)
        expert_inputs(nc, x, m, done)
        expert_outputs(nc, x, m, done)


def project_in(nc, x, m):
    psum, xn, feat, at = m["psum"], m["xn"], m["feat"], m["at"]
    parts = xn.bitcast(F16).rearrange("p c (k t) -> p c k t", k=2)
    with ExitStack() as c:
        sem = lambda n: c.enter_context(nc.semaphore(n))
        word = W0
        w = at(word, 2, DC, 256); word += 2 * DC * 256
        w_parts = at(word, 2 * DC * 256).bitcast(F16)\
            .rearrange("p (s k c n) -> p s k c n", s=2, k=2, c=DC); word += 2 * DC * 256
        sq = at(word, 2, T); word += 2 * T
        rstd = at(word, T); word += T
        nw = at(word, DC); word += DC
        kscale = at(word, 5); word += 5
        assert word <= WORDS
        chunk_loaded = [sem(f"chunk{q}_loaded") for q in range(DC)]
        norm_loaded = sem("norm_loaded")
        w_hi_ready = sem("w_hi_ready")
        w_lo_ready = sem("w_lo_ready")
        x_scaled = sem("x_scaled")
        x_hi_ready = sem("x_hi_ready")
        w_loaded = [sem(f"w_loaded{i}") for i in range(2)]
        consts_ready = sem("consts_ready")
        squared = sem("squared")
        square_used = sem("square_used")
        sums_ready = sem("sums_ready")
        rms_ready = sem("rms_ready")
        x_normed = sem("x_normed")
        piece_done = sem("piece_done")
        group_ready = sem("group_ready")
        bank_free = sem("bank_free")
        tile_ready = sem("tile_ready")
        tile_free = sem("tile_free")
        kv_out = sem("kv_out")
        settled = {e: sem(f"in_settled_{e}") for e in ("act", "dve")}
        block = c.enter_context(nc.Block())

        @block.sync
        def _(sp):
            for q in range(DC):
                sp.dma_start(xn[:, q, :], x["x_feat"][:, q, :]).then_inc(chunk_loaded[q], 16)
            sp.dma_start(nw, x["norm1"]).then_inc(norm_loaded, 16)
            for p in range(2):
                sp.dma_start(w[:, p, :, :], x["w_in"][p]).then_inc(w_loaded[p], 16)
            with sp.Fori(1, 7) as i:
                for p in range(2):
                    sp.wait_ge(w_lo_ready, i * 2 + p - 1)
                    sp.dma_start(w[:, p, :, :], x["w_in"][bass.ds(i * 2 + p, 1)].squeeze(0)).then_inc(w_loaded[p], 16)
            sp.wait_ge(x_normed, DC + 6)
            sp.wait_ge(tile_free, 2 + 4 * 9)
            sp.dma_start(x["k_feat_out"], feat[:, FK, :, :]).then_inc(kv_out, 16)
            sp.dma_start(x["v_out"], m["v"][:, 0:TT, :]).then_inc(kv_out, 16)
            sp.dma_start(x["v_out_s"], m["v"][0:NS, TT, :]).then_inc(kv_out, 16)
            sp.wait_ge(kv_out, 48)

        @block.gpsimd
        def _(pool):
            pool.memset(m["ones"], 1.0).then_inc(consts_ready, 1)
            pool.memset(m["ident"], 0.0).then_inc(consts_ready, 1)
            pool.wait_ge(consts_ready, 2)
            pool.affine_select(out=m["ident"], in_=m["ident"], compare_op=ALU.not_equal, fill=1.0,
                               base=0, pattern=[[-1, P]], channel_multiplier=1).then_inc(consts_ready, 1)
            pool.iota(m["io16"].bitcast(I32), pattern=[[1, 16]], base=0, channel_multiplier=0).then_inc(consts_ready, 1)
            pool.memset(m["eps"], EPS).then_inc(consts_ready, 1)
            pool.wait_ge(consts_ready, 5)
            pool.tensor_copy(m["io16"], m["io16"].bitcast(I32)).then_inc(consts_ready, 1)
            pool.wait_ge(consts_ready, 6)

        @block.scalar
        def _(act):
            for q in range(DC):
                act.wait_ge(chunk_loaded[q], 16)
                if q >= 2:
                    act.wait_ge(square_used, q - 1)
                act.activation(sq[:, q % 2, :], xn[:, q, :], ACT.Square).then_inc(squared, 1)
            act.wait_ge(consts_ready, 6)
            act.wait_ge(square_used, DC)
            for s in range(NSL):
                last = act.activation(rstd[:, s * SL:(s + 1) * SL], psum[:, s, 0:SL], ACT.Sqrt,
                                      bias=m["eps"], scale=1.0 / D)
            last.then_inc(rms_ready, 1)
            for q in range(DC):
                act.wait_ge(x_scaled, q + 1)
                act.copy(parts[:, q, 0, :], sq[:, q % 2, :]).then_inc(x_hi_ready, 1)
                if q < 2:
                    act.wait_ge(w_loaded[q], 16)
                    act.mul(w_parts[:, q, 0], w[:, q], W_SCALE).then_inc(w_hi_ready, 1)
            with act.Fori(1, 7) as i:
                for p in range(2):
                    act.wait_ge(w_loaded[p], i * 16 + 16)
                    act.sem_inc(settled["act"], 1)
                    act.wait_ge(piece_done, i * 2 + p - 1)
                    act.sem_inc(settled["act"], 1)
                    act.mul(w_parts[:, p, 0], w[:, p], W_SCALE).then_inc(w_hi_ready, 1)

        @block.tensor
        def _(pe):
            pe.wait_ge(consts_ready, 6)
            for q in range(DC):
                pe.wait_ge(squared, q + 1)
                for s in range(NSL):
                    last = pe.matmul(psum[:, s, 0:SL], m["ones"], sq[:, q % 2, s * SL:(s + 1) * SL],
                                     start=q == 0, stop=q == DC - 1)
                last.then_inc(square_used, 1)
            pe.wait_ge(x_normed, DC)
            with pe.Fori(0, 5) as i:
                for p in range(2):
                    pe.wait_ge(w_lo_ready, i * 2 + p + 1)
                    for j in range(2):
                        pe.wait_ge(bank_free, i * 4 + 2 * p + j + 1)
                        for q in range(DC):
                            for w_part, x_part in PRODUCTS:
                                for s in range(NSL):
                                    last = pe.matmul(psum[:, 3 * j + s, 0:SL],
                                                     w_parts[:, p, w_part, q, j * P:(j + 1) * P],
                                                     parts[:, q, x_part, s * SL:(s + 1) * SL],
                                                     start=q == 0 and w_part == x_part,
                                                     stop=q == DC - 1 and w_part == 1)
                        last.then_inc(group_ready, 1)
                    pe.wait_ge(group_ready, i * 4 + 2 * p + 2)
                    pe.sem_inc(piece_done, 1)
            for i in range(2):
                for p in range(2):
                    pe.wait_ge(w_lo_ready, (5 + i) * 2 + p + 1)
                    n0 = (2 * i + p) * 9
                    for t in range(9):
                        rows = P if t < TT else NS
                        pe.wait_ge(tile_free, n0 + t + 1)
                        for q in range(DC):
                            for w_part, x_part in PRODUCTS:
                                last = pe.matmul(psum[0:rows, 6 + (n0 + t) % 2, 0:256],
                                                 parts[:, q, x_part, t * P:t * P + rows], w_parts[:, p, w_part, q, :],
                                                 start=q == 0 and w_part == x_part,
                                                 stop=q == DC - 1 and w_part == 1)
                        last.then_inc(tile_ready, 1)
                    pe.wait_ge(tile_ready, n0 + 9)
                    pe.sem_inc(piece_done, 1)

        @block.vector
        def _(dve):
            for i in range(5):
                dve.memset(kscale[:, i:i + 1], (DH ** -0.5 if i == FQ else 1.0) / W_SCALE)
            dve.drain()
            dve.sem_inc(bank_free, 2)
            dve.sem_inc(tile_free, 2)
            dve.wait_ge(rms_ready, 1)
            dve.reciprocal(rstd, rstd)
            dve.drain()
            dve.wait_ge(norm_loaded, 16)

            def w_low_part(p, n):
                dve.wait_ge(w_hi_ready, n)
                dve.scalar_tensor_tensor(out=w_parts[:, p, 1].rearrange("p c n -> p (c n)"), in0=flat(w[:, p]),
                                         scalar=W_SCALE, in1=w_parts[:, p, 0].rearrange("p c n -> p (c n)"),
                                         op0=ALU.mult, op1=ALU.subtract).then_inc(w_lo_ready, 1)

            def x_low_part(q):
                dve.wait_ge(x_hi_ready, q + 1)
                dve.tensor_tensor(parts[:, q, 1, :], sq[:, q % 2, :], parts[:, q, 0, :],
                                  ALU.subtract).then_inc(x_normed, 1)

            for q in range(DC):
                if q >= 2:
                    dve.wait_ge(x_normed, q - 1)
                dve.scalar_tensor_tensor(out=sq[:, q % 2, :], in0=xn[:, q, :], scalar=nw[:, q:q + 1], in1=rstd,
                                         op0=ALU.mult, op1=ALU.mult).then_inc(x_scaled, 1)
                if q >= 1:
                    x_low_part(q - 1)
                if q in (2, 3):
                    w_low_part(q - 2, q - 1)
            x_low_part(DC - 1)
            with dve.Fori(0, 5) as i:
                for p in range(2):
                    for j in range(2):
                        dve.wait_ge(group_ready, i * 4 + 2 * p + j + 1)
                        dve.sem_inc(settled["dve"], 1)
                        for s in range(NSL):
                            last = dve.tensor_scalar(
                                m["arena"][:, bass.ds(F0 + i * (4 * T) + (2 * p + j) * T + s * SL, SL)],
                                psum[:, 3 * j + s, 0:SL], kscale[:, bass.ds(i, 1)], None, ALU.mult)
                        last.then_inc(bank_free, 1)
                    w_low_part(p, i * 2 + p + 3)
            dve.drain().then_inc(x_normed, 6)
            for i in range(2):
                for p in range(2):
                    for t in range(9):
                        n = (2 * i + p) * 9 + t
                        rows = P if t < TT else NS
                        dve.wait_ge(tile_ready, n + 1)
                        dst = (m["v"], m["hi"])[i]
                        dve.tensor_scalar(dst[0:rows, t, p * 256:(p + 1) * 256], psum[0:rows, 6 + n % 2, 0:256],
                                          1.0 / W_SCALE, None, ALU.mult).then_inc(tile_free, 1)
                    if i == 0:
                        w_low_part(p, 13 + p)


def attend_prompt(nc, x, m):
    psum, at, arena = m["psum"], m["at"], m["arena"]
    with ExitStack() as c:
        sem = lambda n: c.enter_context(nc.semaphore(n))
        word = W0
        bias = at(word, SEQ); word += SEQ
        probs = at(word, 2, SEQ); word += 2 * SEQ
        turned = at(word, 2, SEQ); word += 2 * SEQ
        pair_q = at(word, 2, SEQ); word += 2 * SEQ
        pair_k = at(word, 2, SEQ); word += 2 * SEQ
        out_tok = at(word, 2, P); word += 2 * P
        top = at(word, 2, 1); word += 2
        neg_top = at(word, 2, 1); word += 2
        total = at(word, 2, 2); word += 4
        inv = at(word, 2, 2); word += 4
        assert word <= WORDS
        bias_loaded = sem("bias_loaded")
        pair_staged = sem("pair_staged")
        scores_ready = sem("scores_ready")
        scores_read = sem("scores_read")
        max_ready = sem("max_ready")
        exp_ready = sem("exp_ready")
        piece_ready = sem("piece_ready")
        piece_copied = sem("piece_copied")
        values_ready = sem("values_ready")
        out_scaled = sem("out_scaled")
        out_turned = sem("out_turned")
        out_copied = sem("out_copied")
        settled = {e: sem(f"settled_{e}") for e in ("pe", "act", "dve")}
        block = c.enter_context(nc.Block())

        PAIRS = 2
        BLOCKS = PAIRS * 2 * TT
        TILES = PAIRS * TT
        tile = [n // 2 % TT for n in range(BLOCKS)]
        pieces = [1 if i < 4 else 2 for i in tile]
        before = [sum(pieces[:n]) for n in range(BLOCKS + 1)]
        PIECES = before[-1]
        SPARE = 4

        @block.sync
        def _(sp):
            sp.dma_start(bias, x["bias_prompt"]).then_inc(bias_loaded, 16)

        @block.gpsimd
        def _(pool):
            for j in range(H // 2):
                if j >= PAIRS:
                    pool.wait_ge(scores_ready, (j - PAIRS + 1) * 2 * TT)
                pool.tensor_copy(pair_q[:, j % PAIRS, :], m["feat"][:, FQ, j, 0:SEQ]).then_inc(pair_staged, 1)
                pool.tensor_copy(pair_k[:, j % PAIRS, :], m["feat"][:, FK, j, 0:SEQ]).then_inc(pair_staged, 1)

        @block.tensor
        def _(pe):
            with pe.Fori(0, H // 2 // PAIRS) as turns:
                def scores(n):
                    pair, half, i = n // (2 * TT), n % 2, tile[n]
                    r = slice(64 * half, 64 * half + 64)
                    if n % (2 * TT) == 0:
                        pe.wait_ge(pair_staged, turns * (2 * PAIRS) + 2 * pair + 2)
                        pe.sem_inc(settled["pe"], 1)
                    pe.wait_ge(scores_read, turns * BLOCKS + n + 1)
                    pe.sem_inc(settled["pe"], 1)
                    width = (i + 1) * P
                    for s in range(0, width, 512):
                        e = min(width, s + 512)
                        last = pe.matmul(psum[:, 2 * (n % 2) + s // 512, 0:e - s],
                                         pair_q[r, pair, i * P:(i + 1) * P], pair_k[r, pair, s:e],
                                         start=True, stop=True)
                    last.then_inc(scores_ready, 1)

                def turn(n):
                    i = tile[n]
                    pe.wait_ge(exp_ready, turns * BLOCKS + n + 1)
                    for b in range(pieces[n]):
                        pe.wait_ge(piece_copied, turns * PIECES + before[n] + b + SPARE - 1)
                        for k in range(4 * b, min(i + 1, 4 * b + 4)):
                            last = pe.transpose(psum[:, 4 + (before[n] + b) % 2, (k % 4) * P:(k % 4 + 1) * P],
                                                probs[:, n % 2, k * P:(k + 1) * P], m["ident"])
                        last.then_inc(piece_ready, 1)

                def values(n):
                    pair, half, i = n // (2 * TT), n % 2, tile[n]
                    pe.wait_ge(piece_copied, turns * PIECES + before[n + 1] + SPARE)
                    pe.sem_inc(settled["pe"], 1)
                    pe.wait_ge(out_copied, turns * TILES + n // 2 + 1)
                    pe.sem_inc(settled["pe"], 1)
                    for k in range(i + 1):
                        last = pe.matmul(psum[:, 6 + n // 2 % 2, 64 * half:64 * half + 64],
                                         turned[:, n % 2, k * P:(k + 1) * P],
                                         arena[:, bass.ds(V0 + k * 512 + turns * (PAIRS * P) + pair * P + 64 * half, 64)],
                                         start=k == 0, stop=k == i)
                    last.then_inc(values_ready, 1)

                def turn_out(t):
                    pe.wait_ge(out_scaled, turns * TILES + t + 1)
                    pe.transpose(psum[:, 6 + t % 2, P:2 * P], out_tok[:, t % 2, :], m["ident"]).then_inc(out_turned, 1)

                scores(0)
                for n in range(BLOCKS):
                    if n + 1 < BLOCKS:
                        scores(n + 1)
                    turn(n)
                    if n >= 1:
                        values(n - 1)
                    if n >= 3 and n % 2 == 1:
                        turn_out(n // 2 - 1)
                values(BLOCKS - 1)
                turn_out(TILES - 1)

        @block.vector
        def _(dve):
            dve.sem_inc(scores_read, 2)
            dve.wait_ge(bias_loaded, 16)
            with dve.Fori(0, H // 2 // PAIRS) as turns:
                def add_bias(n):
                    width = (tile[n] + 1) * P
                    dve.wait_ge(scores_ready, turns * BLOCKS + n + 1)
                    dve.sem_inc(settled["dve"], 1)
                    dve.wait_ge(piece_copied, turns * PIECES + SPARE + (before[n - 1] if n else -pieces[-1]))
                    dve.sem_inc(settled["dve"], 1)
                    scores = psum[:, 2 * (n % 2):2 * (n % 2) + 2, :].rearrange("p a b -> p (a b)")
                    dve.tensor_tensor_reduce(probs[:, n % 2, 0:width], scores[:, 0:width],
                                             bias[:, SEQ - width:SEQ], 1.0, LOWEST, ALU.add, ALU.max,
                                             top[:, n % 2, :]).then_inc(scores_read, 1)
                    dve.drain()
                    dve.tensor_scalar(neg_top[:, n % 2, :], top[:, n % 2, :], -1.0, None,
                                      ALU.mult).then_inc(max_ready, 1)

                def scale_out(t):
                    dve.wait_ge(values_ready, turns * BLOCKS + 2 * t + 4)
                    dve.sem_inc(settled["dve"], 1)
                    dve.reciprocal(inv[:, t % 2, :], total[:, t % 2, :])
                    dve.drain()
                    dve.tensor_tensor(out_tok[:, t % 2, :].rearrange("p (h d) -> p h d", h=2),
                                      psum[:, 6 + t % 2, 0:P].rearrange("p (h d) -> p h d", h=2),
                                      inv[:, t % 2, :].unsqueeze(2).broadcast_to([P, 2, 64]),
                                      ALU.mult).then_inc(out_scaled, 1)

                for n in range(BLOCKS):
                    add_bias(n)
                    if n >= 3 and n % 2 == 1:
                        scale_out(n // 2 - 1)
                scale_out(TILES - 1)

        @block.scalar
        def _(act):
            act.sem_inc(piece_copied, SPARE)
            act.sem_inc(out_copied, 2)
            act.sem_inc(values_ready, 2)
            with act.Fori(0, H // 2 // PAIRS) as turns:
                def exps(n):
                    width = (tile[n] + 1) * P
                    act.wait_ge(max_ready, turns * BLOCKS + n + 1)
                    act.activation(probs[:, n % 2, 0:width], probs[:, n % 2, 0:width], ACT.Exp,
                                   bias=neg_top[:, n % 2, :],
                                   accum_out=total[:, n // 2 % 2, n % 2:n % 2 + 1]).then_inc(exp_ready, 1)

                def copy_pieces(n):
                    width = (tile[n] + 1) * P
                    act.wait_ge(values_ready, turns * BLOCKS + n + 1)
                    act.sem_inc(settled["act"], 1)
                    for b in range(pieces[n]):
                        s, e = 512 * b, min(width, 512 * b + 512)
                        act.wait_ge(piece_ready, turns * PIECES + before[n] + b + 1)
                        act.copy(turned[:, n % 2, s:e],
                                 psum[:, 4 + (before[n] + b) % 2, 0:e - s]).then_inc(piece_copied, 1)

                def copy_out(t):
                    pair, i = divmod(t, TT)
                    act.wait_ge(out_turned, turns * TILES + t + 1)
                    act.sem_inc(settled["act"], 1)
                    act.copy(arena[:, bass.ds(XT0 + i * P + pair * T + turns * (PAIRS * T), P)],
                             psum[:, 6 + t % 2, P:2 * P]).then_inc(out_copied, 1)

                for n in range(BLOCKS):
                    exps(n)
                    if n >= 1:
                        copy_pieces(n - 1)
                    if n >= 4 and n % 2 == 0:
                        copy_out(n // 2 - 2)
                copy_pieces(BLOCKS - 1)
                copy_out(TILES - 2)
                copy_out(TILES - 1)


def hgrn(nc, x, m):
    psum, at, feat, mix, hi = m["psum"], m["at"], m["feat"], m["mix"], m["hi"]
    GT = 4 * T
    with ExitStack() as c:
        sem = lambda n: c.enter_context(nc.semaphore(n))
        q, b, gate = feat[:, FHQ, :, :], feat[:, FHF, :, :], feat[:, FHG, :, :]
        word = W0
        k = at(word, G, T); word += GT
        ek = at(word, G, T); word += GT
        resets = at(word, T); word += T
        causal = at(word, P); word += P
        causal_s = at(word, NS); word += NS
        only = at(word, SB); word += SB
        logits = at(word, 2, G); word += 2 * G
        lbt = at(word, 8, G); word += 8 * G
        hnorm = at(word, 1); word += 1
        carry = at(word, G, NCH + 1); word += G * (NCH + 1)
        carry_s = at(word, 2, G * SB).rearrange("p a (g b) -> p a g b", g=G); word += 2 * G * SB
        state = at(word, G, 2, P); word += G * 2 * P
        sum_state = at(word, G, P); word += G * P
        masked = at(word, G, P); word += G * P
        assert word <= WORDS, word
        eq = at(F0, G, T)
        state_s = at(F0 + GT, G, SB * P).rearrange("p g (b v) -> p g b v", b=SB)
        k_tok = at(V0, 9, 512)
        hi_only = m["arena"][0:NS, W0 + GT:W0 + GT + SB * 512].rearrange("p (b n) -> p b n", b=SB)
        loaded = sem("hgrn_loaded")
        step_act = sem("hgrn_act")
        step_dve = sem("hgrn_dve")
        turn_ready = sem("hgrn_turn_ready")
        turn_copied = sem("hgrn_turn_copied")
        pair_ready = sem("hgrn_pair_ready")
        masked_ready = sem("hgrn_masked_ready")
        update_ready = sem("hgrn_update_ready")
        update_read = sem("hgrn_update_read")
        state_ready = sem("hgrn_state_ready")
        out_ready = sem("hgrn_out_ready")
        out_copied = sem("hgrn_out_copied")
        squared = sem("hgrn_squared")
        summed = sem("hgrn_summed")
        stored = sem("hgrn_stored")
        settled = {e: sem(f"hgrn_settled_{e}") for e in ("pe", "act", "dve")}
        block = c.enter_context(nc.Block())

        @block.sync
        def _(sp):
            for dst, name in ((resets, "resets"), (causal, "causal"), (causal_s[0:NS], "causal_s"), (only[0:NS], "only"),
                              (logits, "lb_logits"), (hnorm, "hgrn_norm"), (state_s, "state")):
                sp.dma_start(dst, x[name]).then_inc(loaded, 16)
            sp.wait_ge(step_dve, 6)
            sp.dma_start(x["hgrn_p"], sum_state).then_inc(stored, 16)
            sp.dma_start(x["hgrn_s"], state_s).then_inc(stored, 16)
            sp.wait_ge(stored, 32)

        @block.scalar
        def _(act):
            act.wait_ge(loaded, 16 * 7)
            act.wait_ge(step_dve, 1)
            act.activation(lbt[:, 1:3, :], lbt[:, 1:3, :], ACT.Exp).then_inc(step_act, 1)
            act.activation(b, b, ACT.Sigmoid).then_inc(step_act, 1)
            act.wait_ge(step_dve, 2)
            act.activation(b, b, ACT.Ln).then_inc(step_act, 1)
            act.wait_ge(step_dve, 3)
            act.activation(ek, eq, ACT.Exp, scale=-1.0)
            act.drain()
            act.activation(eq, eq, ACT.Exp)
            act.activation(carry[:, :, 1:], carry[:, :, 1:], ACT.Exp)
            act.activation(carry_s, carry_s, ACT.Exp).then_inc(step_act, 1)
            act.activation(q, q, ACT.Silu).then_inc(step_act, 1)
            act.activation(gate, gate, ACT.Silu).then_inc(step_act, 1)
            for t in range(9):
                rows = P if t < TT else NS
                act.wait_ge(turn_ready, t + 1)
                act.copy(k_tok[0:rows, t, :], psum[0:rows, t % 2, :]).then_inc(turn_copied, 1)
            act.wait_ge(step_dve, 7)
            act.activation(ek, ek, ACT.Sqrt).then_inc(step_act, 1)

        @block.tensor
        def _(pe):
            pe.wait_ge(step_dve, 4)
            for t in range(9):
                rows = P if t < TT else NS
                if t >= 2:
                    pe.wait_ge(turn_copied, t - 1)
                for g in range(G):
                    last = pe.transpose(psum[0:rows, t % 2, g * P:(g + 1) * P], k[:, g, t * P:t * P + rows],
                                        m["ident"])
                last.then_inc(turn_ready, 1)
            pe.wait_ge(turn_copied, 9)
            for t in range(TT):
                tok = slice(t * P, (t + 1) * P)
                if t >= 1:
                    pe.wait_ge(masked_ready, t)
                for g in range(G):
                    last = pe.matmul(psum[:, 2, g * P:(g + 1) * P], k[:, g, tok], q[:, g, tok],
                                     start=True, stop=True)
                last.then_inc(pair_ready, 1)
                for j in range(4):
                    if t >= 1:
                        pe.wait_ge(update_read, 4 * (4 * t + j) - 12)
                    rows = slice(CH * j, CH * j + CH)
                    for g in range(G):
                        last = pe.matmul(psum[:, 4 + j, g * P:(g + 1) * P], k_tok[rows, t, g * P:(g + 1) * P],
                                         hi[rows, t, g * P:(g + 1) * P], start=True, stop=True)
                    last.then_inc(update_ready, 1)
                pe.wait_ge(masked_ready, t + 1)
                if t >= 1:
                    pe.wait_ge(out_copied, t)
                for g in range(G):
                    pe.matmul(psum[:, 3, g * P:(g + 1) * P], hi[:, t, g * P:(g + 1) * P], masked[:, g, :],
                              start=g == 0, stop=False, skip_group_check=True)
                for j in range(4):
                    n = 4 * t + j
                    pe.wait_ge(state_ready, n + 1)
                    for g in range(G):
                        last = pe.matmul(psum[:, 3, g * P + CH * j:g * P + CH * j + CH], state[:, g, n % 2, :],
                                         q[:, g, n * CH:n * CH + CH], start=False, stop=j == 3,
                                         skip_group_check=True)
                    last.then_inc(out_ready, 1)
            tok = slice(SEQ, T)
            pe.wait_ge(masked_ready, TT)
            for g in range(G):
                last = pe.matmul(psum[0:NS, 2, g * NS:(g + 1) * NS], k[:, g, tok], q[:, g, tok],
                                 start=True, stop=True)
            last.then_inc(pair_ready, 1)
            pe.wait_ge(masked_ready, TT + 1)
            pe.wait_ge(out_copied, TT)
            for g in range(G):
                pe.matmul(psum[:, 3, g * NS:(g + 1) * NS], hi[0:NS, TT, g * P:(g + 1) * P],
                          masked[0:NS, g, 0:NS], start=g == 0, stop=False, skip_group_check=True)
            pe.wait_ge(step_dve, 5)
            for g in range(G):
                for s in range(SB):
                    last = pe.matmul(psum[:, 3, g * NS + ST * s:g * NS + ST * s + ST], state_s[:, g, s, :],
                                     q[:, g, SEQ + ST * s:SEQ + ST * s + ST], start=False, stop=s == SB - 1,
                                     skip_group_check=True)
            last.then_inc(out_ready, 1)
            for n in range(2 * G):
                g, half = divmod(n, 2)
                if n < 4:
                    pe.wait_ge(update_read, 4 * NCH)
                else:
                    pe.wait_ge(update_read, 4 * NCH + n - 3)
                last = pe.matmul(psum[:, 4 + n % 4, :].rearrange("p (b v) -> p b v", b=4),
                                 k_tok[0:NS, TT, g * P:(g + 1) * P],
                                 hi_only[:, 4 * half:4 * half + 4, g * P:(g + 1) * P], start=True, stop=True)
                last.then_inc(update_ready, 1)
            for g in range(G):
                pe.wait_ge(squared, g + 1)
                if g >= 2:
                    pe.wait_ge(summed, g - 1)
                if g == 0:
                    pe.wait_ge(update_read, 4 * NCH + 2 * G)
                for s in range(NSL):
                    last = pe.matmul(psum[:, 4 * (g % 2) + s, 0:SL], m["ones"],
                                     eq[:, g, s * SL:(s + 1) * SL], start=True, stop=True)
                last.then_inc(turn_ready, 1)

        @block.vector
        def _(dve):
            dve.wait_ge(loaded, 16 * 7)
            dve.tensor_tensor(lbt[:, 0, :], logits[:, 0, :], logits[:, 1, :], ALU.max)
            dve.drain()
            for i in range(2):
                last = dve.tensor_tensor(lbt[:, 1 + i, :], logits[:, i, :], lbt[:, 0, :], ALU.subtract)
            last.then_inc(step_dve, 1)
            dve.wait_ge(step_act, 1)
            dve.tensor_tensor(lbt[:, 3, :], lbt[:, 1, :], lbt[:, 2, :], ALU.add)
            dve.drain()
            dve.reciprocal(lbt[:, 4, :], lbt[:, 3, :])
            dve.drain()
            dve.tensor_tensor(lbt[:, 5, :], lbt[:, 1, :], lbt[:, 4, :], ALU.mult)
            dve.drain()
            dve.tensor_scalar(lbt[:, 6, :], lbt[:, 5, :], -1.0, 1.0, ALU.mult, ALU.add)
            dve.drain()
            dve.wait_ge(step_act, 2)
            for g in range(G):
                dve.tensor_scalar(b[:, g, :], b[:, g, :], lbt[:, 6, g:g + 1], lbt[:, 5, g:g + 1], ALU.mult, ALU.add)
            dve.drain()
            dve.tensor_scalar(k, b, -1.0, 1.0, ALU.mult, ALU.add)
            dve.drain().then_inc(step_dve, 1)
            dve.wait_ge(step_act, 3)
            for g in range(G):
                dve.tensor_tensor_scan(ek[:, g, :], resets, b[:, g, :], 0.0, ALU.mult, ALU.add)
            dve.drain()
            mid, mid_s = CH // 2 - 1, ST // 2 - 1
            chunks = ek[:, :, 0:SEQ].rearrange("p g (n c) -> p g n c", c=CH)
            chunks_s = ek[:, :, SEQ:T].rearrange("p g (n c) -> p g n c", c=ST)
            for g in range(G):
                dve.tensor_tensor(eq[:, g, 0:SEQ].rearrange("p (n c) -> p n c", c=CH), chunks[:, g],
                                  chunks[:, g, :, mid:mid + 1].broadcast_to([P, NCH, CH]), ALU.subtract)
                dve.tensor_tensor(eq[:, g, SEQ:T].rearrange("p (n c) -> p n c", c=ST), chunks_s[:, g],
                                  chunks_s[:, g, :, mid_s:mid_s + 1].broadcast_to([P, SB, ST]), ALU.subtract)
            dve.drain()
            ends = eq[:, :, 0:SEQ].rearrange("p g (n c) -> p g n c", c=CH)[:, :, :, CH - 1]
            ends_s = eq[:, :, SEQ:T].rearrange("p g (n c) -> p g n c", c=ST)[:, :, :, ST - 1]
            dve.tensor_copy(carry[:, :, NCH], ends[:, :, NCH - 1])
            dve.memset(carry[:, :, 0], 1.0)
            dve.tensor_tensor(carry[:, :, 1:NCH], ends[:, :, 0:NCH - 1], chunks[:, :, 1:NCH, mid], ALU.add)
            dve.tensor_copy(carry_s[:, 0], chunks_s[:, :, :, mid_s])
            dve.tensor_copy(carry_s[:, 1], ends_s)
            dve.drain()
            dve.tensor_scalar(eq, eq, 40.0, -40.0, ALU.min, ALU.max)
            dve.drain().then_inc(step_dve, 1)
            dve.wait_ge(step_act, 4)
            dve.tensor_tensor(k, k, ek, ALU.mult)
            dve.drain()
            dve.wait_ge(step_act, 5)
            dve.tensor_tensor(q, q, eq, ALU.mult)
            dve.memset(sum_state, 0.0)
            dve.drain().then_inc(step_dve, 1)
            for t in range(TT):
                dve.wait_ge(pair_ready, t + 1)
                if t >= 1:
                    dve.wait_ge(out_ready, 4 * t - 3)
                dve.tensor_tensor(masked, psum[:, 2, :].rearrange("p (g t) -> p g t", g=G),
                                  causal.unsqueeze(1).broadcast_to([P, G, P]), ALU.mult).then_inc(masked_ready, 1)
                for j in range(4):
                    n = 4 * t + j
                    if n >= 2:
                        dve.wait_ge(out_ready, n - 1)
                    for g in range(G):
                        last = dve.tensor_scalar(state[:, g, n % 2, :], sum_state[:, g, :], carry[:, g, n:n + 1],
                                                 None, ALU.mult)
                    last.then_inc(state_ready, 1)
                    dve.wait_ge(state_ready, n + 1)
                    dve.wait_ge(update_ready, n + 1)
                    for g in range(G):
                        dve.tensor_tensor(sum_state[:, g, :], state[:, g, n % 2, :],
                                          psum[:, 4 + j, g * P:(g + 1) * P], ALU.add).then_inc(update_read, 1)
                    dve.wait_ge(update_read, 4 * (n + 1))
                dve.wait_ge(out_ready, 4 * t + 4)
                dve.tensor_copy(mix[:, 4:8, t * P:(t + 1) * P],
                                psum[:, 3, :].rearrange("p (g t) -> p g t", g=G)).then_inc(out_copied, 1)
            for g in range(G):
                dve.tensor_scalar(sum_state[:, g, :], sum_state[:, g, :], carry[:, g, NCH:NCH + 1], None, ALU.mult)
            dve.wait_ge(pair_ready, TT + 1)
            dve.tensor_tensor(masked[0:NS, :, 0:NS], psum[0:NS, 2, 0:P].rearrange("p (g t) -> p g t", g=G),
                              causal_s[0:NS].unsqueeze(1).broadcast_to([NS, G, NS]), ALU.mult).then_inc(masked_ready, 1)
            dve.tensor_tensor(state_s, state_s, carry_s[:, 0].unsqueeze(3).broadcast_to([P, G, SB, P]), ALU.mult)
            for s in range(SB):
                dve.tensor_scalar(hi_only[:, s, :], hi[0:NS, TT, :], only[0:NS, s:s + 1], None, ALU.mult)
            dve.drain().then_inc(step_dve, 1)
            dve.wait_ge(out_ready, 4 * TT + 1)
            dve.tensor_copy(mix[:, 4:8, SEQ:T],
                            psum[:, 3, 0:P].rearrange("p (g t) -> p g t", g=G)).then_inc(out_copied, 1)
            for n in range(2 * G):
                g, half = divmod(n, 2)
                dve.wait_ge(update_ready, NCH + n + 1)
                dve.tensor_tensor(state_s[:, g, 4 * half:4 * half + 4, :], state_s[:, g, 4 * half:4 * half + 4, :],
                                  psum[:, 4 + n % 4, :].rearrange("p (b v) -> p b v", b=4),
                                  ALU.add).then_inc(update_read, 1)
            dve.drain()
            dve.tensor_tensor(state_s, state_s, carry_s[:, 1].unsqueeze(3).broadcast_to([P, G, SB, P]), ALU.mult)
            dve.drain().then_inc(step_dve, 1)
            dve.tensor_tensor(eq, mix[:, 4:8, :], mix[:, 4:8, :], ALU.mult)
            dve.drain().then_inc(squared, G)
            for g in range(G):
                dve.wait_ge(turn_ready, 9 + g + 1)
                first = 0 if g % 2 == 0 else 4
                for s in range(NSL):
                    last = dve.tensor_scalar(ek[:, g, s * SL:(s + 1) * SL], psum[:, first + s, 0:SL], 1.0 / DK, EPS,
                                             ALU.mult, ALU.add)
                last.then_inc(summed, 1)
            dve.drain().then_inc(step_dve, 1)
            dve.wait_ge(step_act, 7)
            dve.reciprocal(ek, ek)
            dve.drain()
            dve.scalar_tensor_tensor(out=mix[:, 4:8, :], in0=mix[:, 4:8, :], scalar=hnorm, in1=ek,
                                     op0=ALU.mult, op1=ALU.mult)
            dve.drain()
            dve.tensor_tensor(mix[:, 4:8, :], mix[:, 4:8, :], gate, ALU.mult)
            dve.drain()



def attend_sample(nc, x, m):
    psum, at, feat, mix = m["psum"], m["at"], m["feat"], m["mix"]
    KT = NKEY // P
    ROUND = 4
    with ExitStack() as c:
        sem = lambda n: c.enter_context(nc.semaphore(n))
        word = W0
        q_apart = at(word, 4 * SB, NS).rearrange("p (c b) r -> p c b r", c=4); word += 4 * SB * NS
        k_new = at(word, 4, NS); word += 4 * NS
        bias = at(word, 2, NCOL); word += 2 * NCOL
        probs = at(word, 2, NCOL); word += 2 * NCOL
        turned = at(word, KT + 1, P); word += (KT + 1) * P
        top = at(word, 2, 1); neg_top = at(word + 2, 2, 1); total = at(word + 4, 2, 1); inv = at(word + 6, 2, 1)
        word += 8
        keys = [at(word, 4, NKEY), at(F0, 4, NKEY)]
        vals = [at(word + 4 * NKEY, KT, 512), at(F0 + 4 * NKEY, KT, 512)]
        assert word + 4 * NKEY + KT * 512 <= WORDS
        bias_loaded = sem("sample_bias_loaded")
        keys_loaded = [sem(f"keys_loaded{i}") for i in range(2)]
        vals_loaded = [sem(f"vals_loaded{i}") for i in range(2)]
        zeroed = sem("q_zeroed")
        new_ready = sem("new_ready")
        keys_used = sem("keys_used")
        vals_used = sem("vals_used")
        max_ready = sem("sample_max_ready")
        exp_ready = sem("sample_exp_ready")
        probs_ready = sem("sample_probs_ready")
        turn_ready = sem("sample_turn_ready")
        turn_copied = sem("sample_turn_copied")
        out_done = sem("sample_out_done")
        block = c.enter_context(nc.Block())

        @block.sync
        def _(sp):
            sp.dma_start(bias, x["bias_sample"]).then_inc(bias_loaded, 16)

            def load_keys(b):
                if b >= 2:
                    sp.wait_ge(keys_used, b - 1)
                sp.dma_start(keys[b % 2], x["keys_feat"][b]).then_inc(keys_loaded[b % 2], 16)

            def load_vals(b):
                if b >= 2:
                    sp.wait_ge(vals_used, b - 1)
                sp.dma_start(vals[b % 2], x["vals_tok"][b]).then_inc(vals_loaded[b % 2], 16)

            load_keys(0)
            sp.wait_ge(new_ready, 9)
            load_keys(1)
            load_keys(2)
            load_keys(3)
            load_vals(0)
            load_vals(1)
            for b in range(ROUND, SB):
                load_keys(b)
            for b in range(2, SB):
                load_vals(b)

        @block.gpsimd
        def _(pool):
            pool.memset(q_apart, 0.0).then_inc(zeroed, 1)
            pool.tensor_copy(k_new, feat[:, FK, :, SEQ:T]).then_inc(new_ready, 1)

        @block.tensor
        def _(pe):
            def scores(b):
                rows = slice(32 * (b % ROUND), 32 * (b % ROUND) + 32)
                bank = 2 * (b // ROUND)
                pe.wait_ge(keys_loaded[b % 2], 16 * (b // 2 + 1))
                for (k0, k1, where) in ((0, 512, bank), (512, NKEY, bank + 1)):
                    for q in range(4):
                        pe.matmul(psum[rows, where, 0:k1 - k0], q_apart[:, q, b, :], keys[b % 2][:, q, k0:k1],
                                  start=q == 0, stop=q == 3)
                for q in range(4):
                    last = pe.matmul(psum[rows, bank + 1, NKEY - 512:NCOL - 512], q_apart[:, q, b, :], k_new[:, q, :],
                                     start=q == 0, stop=q == 3)
                last.then_inc(keys_used, 1)

            def turn(r):
                pe.wait_ge(probs_ready, r + 1)
                if r >= 1:
                    pe.wait_ge(turn_copied, 2 * r)
                for k in range(KT + 1):
                    cols = P if k < KT else NS
                    last = pe.transpose(psum[0:cols, 4 + k // 4, (k % 4) * P:(k % 4 + 1) * P],
                                        probs[:, r, k * P:k * P + cols], m["ident"])
                last.then_inc(turn_ready, 1)

            def values(b):
                r, col = b // ROUND, 32 * (b % ROUND)
                pe.wait_ge(turn_copied, 2 * r + 2)
                pe.wait_ge(vals_loaded[b % 2], 16 * (b // 2 + 1))
                for q in range(4):
                    out = psum[:, 6 + r, (4 * (b % ROUND) + q) * 8:(4 * (b % ROUND) + q) * 8 + 8]
                    for k in range(KT):
                        pe.matmul(out, vals[b % 2][:, k, q * P:(q + 1) * P],
                                  turned[:, k, col + 8 * q:col + 8 * q + 8], start=k == 0, stop=False)
                    last = pe.matmul(out, m["v"][0:NS, TT, q * P:(q + 1) * P],
                                     turned[0:NS, KT, col + 8 * q:col + 8 * q + 8], start=False, stop=True)
                last.then_inc(vals_used, 1)

            pe.wait_ge(new_ready, 9)
            for b in range(SB):
                scores(b)
            for r in range(2):
                turn(r)
                for b in range(ROUND * r, ROUND * r + ROUND):
                    values(b)

        @block.vector
        def _(dve):
            dve.wait_ge(zeroed, 1)
            for h in range(H):
                r = slice(64 * (h % 2), 64 * (h % 2) + 64)
                dve.tensor_copy(q_apart[r, h // 2, :, ST * h:ST * h + ST],
                                feat[r, FQ, h // 2, SEQ:T].rearrange("p (b i) -> p b i", b=SB)).then_inc(new_ready, 1)
            dve.wait_ge(bias_loaded, 16)

            def add_bias(r):
                dve.wait_ge(keys_used, ROUND * r + ROUND)
                scores = psum[:, 2 * r:2 * r + 2, :].rearrange("p a b -> p (a b)")
                dve.tensor_tensor_reduce(probs[:, r, :], scores[:, 0:NCOL], bias[:, r, :], 1.0, LOWEST,
                                         ALU.add, ALU.max, top[:, r, :])
                dve.drain()
                dve.tensor_scalar(neg_top[:, r, :], top[:, r, :], -1.0, None, ALU.mult).then_inc(max_ready, 1)

            def normalize(r):
                dve.wait_ge(exp_ready, r + 1)
                dve.reciprocal(inv[:, r, :], total[:, r, :])
                dve.drain()
                dve.tensor_scalar(probs[:, r, :], probs[:, r, :], inv[:, r, :], None,
                                  ALU.mult).then_inc(probs_ready, 1)

            def write_out(r):
                dve.wait_ge(vals_used, ROUND * r + ROUND)
                for half in range(2):
                    rows = slice(64 * half, 64 * half + 64)
                    new = slice(SEQ + ROUND * ST * r, SEQ + ROUND * ST * (r + 1))
                    dve.tensor_copy(
                        mix[rows, 0:4, new].rearrange("p c (b i) -> p b c i", b=ROUND),
                        psum[rows, 6 + r, 0:P].rearrange("p (b c e) -> p b c e", b=ROUND, c=4)[
                            :, :, :, ST * half:ST * half + ST]).then_inc(out_done, 1)

            add_bias(0)
            normalize(0)
            add_bias(1)
            normalize(1)
            write_out(0)
            write_out(1)
            dve.wait_ge(out_done, 4)

        @block.scalar
        def _(act):
            def exps(r):
                act.wait_ge(max_ready, r + 1)
                act.activation(probs[:, r, :], probs[:, r, :], ACT.Exp, bias=neg_top[:, r, :],
                               accum_out=total[:, r, :]).then_inc(exp_ready, 1)

            def copy_turned(r):
                act.wait_ge(turn_ready, r + 1)
                if r >= 1:
                    act.wait_ge(vals_used, ROUND * r)
                act.copy(turned[:, 0:4, :], psum[:, 4, :].rearrange("p (a b) -> p a b", a=4)).then_inc(turn_copied, 1)
                act.copy(turned[:, 4:KT, :],
                         psum[:, 5, 0:(KT - 4) * P].rearrange("p (a b) -> p a b", a=KT - 4))
                act.copy(turned[0:NS, KT, :], psum[0:NS, 5, (KT - 4) * P:(KT - 3) * P]).then_inc(turn_copied, 1)

            exps(0)
            exps(1)
            copy_turned(0)
            copy_turned(1)



def project_out(nc, x, m):
    psum, at, arena, mix = m["psum"], m["at"], m["arena"], m["mix"]
    x_hi, x_lo = m["x_hi"], m["x_lo"]
    HALVES = 2 * PH
    with ExitStack() as c:
        sem = lambda n: c.enter_context(nc.semaphore(n))
        scores = at(0, 9, HALVES * PK)
        word = DC * T
        w_out = at(word, DC, D); word += DC * D
        x_tile = at(word, 2, D); word += 2 * D
        h_tile = at(word, 2, D); word += 2 * D
        normed = at(word, 2, D); word += 2 * D
        wq = at(word, 2, DC, P); word += 2 * DC * P
        wq_hi = at(word, 2, DC * P // 2).bitcast(F16).rearrange("p s (c n) -> p s c n", c=DC); word += DC * P
        wq_lo = at(word, 2, DC * P // 2).bitcast(F16).rearrange("p s (c n) -> p s c n", c=DC); word += DC * P
        query = at(word, 2, T); word += 2 * T
        word_keys = word
        keys = at(word, HALVES, PK); word += HALVES * PK
        junk = at(word, D); word += D
        norm2 = at(word, D); word += D
        ms = at(word, 9); word += 9
        rstd = at(word, 9); word += 9
        assert word <= XH0 and DC * T + DC * D + 2 * D >= 9 * HALVES * PK
        weights_loaded = sem("out_weights_loaded")
        x_loaded = [sem(f"x_tile_loaded{i}") for i in range(2)]
        wq_loaded = [sem(f"wq_loaded{i}") for i in range(2)]
        mixed = sem("mixed")
        added = sem("added")
        h_stored = [sem(f"h_stored{i}") for i in range(2)]
        rms_ready = sem("rms2_ready")
        normed_ready = sem("normed_ready")
        turn_ready = sem("normed_turned")
        hi_ready = sem("normed_hi_ready")
        lo_ready = sem("normed_lo_ready")
        wq_hi_ready = sem("wq_hi_ready")
        wq_lo_ready = sem("wq_lo_ready")
        query_ready = sem("query_ready")
        query_copied = sem("query_copied")
        scored = sem("scored")
        score_copied = sem("score_copied")
        cleared = sem("scores_cleared")
        stored = sem("scores_stored")
        settled = {e: sem(f"out_settled_{e}") for e in ("pe", "dve", "act")}
        block = c.enter_context(nc.Block())

        @block.sync
        def _(sp):
            sp.dma_start(w_out, x["w_out"]).then_inc(weights_loaded, 16)
            sp.dma_start(norm2, x["norm2"]).then_inc(weights_loaded, 16)
            sp.dma_start(keys, x["sub_keys"]).then_inc(weights_loaded, 16)
            for p in range(2):
                sp.dma_start(wq[:, p], x["wq"][p]).then_inc(wq_loaded[p], 16)

            def load_x(t):
                rows = P if t < TT else NS
                sp.dma_start(x_tile[0:rows, t % 2, :], x["x_tok"][t * P:t * P + rows, :]).then_inc(x_loaded[t % 2], 16)

            load_x(0)
            load_x(1)
            for t in range(9):
                rows = P if t < TT else NS
                sp.wait_ge(added, t + 1)
                sp.dma_start(x["h"][t * P:t * P + rows, :], h_tile[0:rows, t % 2, :]).then_inc(h_stored[t % 2], 16)
                if t + 2 < 9:
                    load_x(t + 2)
            def store_scores(i):
                sp.wait_ge(score_copied, i * 6 + 3 + 6)
                sp.dma_start(x["scores"][:, :, bass.ds(i * 2 * PK, 2 * PK)],
                             arena[:, 0:9 * HALVES * PK].rearrange("p (t n) -> p t n", t=9)[
                                 :, :, bass.ds(i * 2 * PK, 2 * PK)]).then_inc(stored, 16)

            with sp.Fori(1, PH) as i:
                for p in range(2):
                    sp.wait_ge(wq_lo_ready, i * 2 + p - 1)
                    sp.dma_start(wq[:, p], x["wq"][bass.ds(i * 2 + p, 1)].squeeze(0)).then_inc(wq_loaded[p], 16)
                store_scores(i - 1)
            store_scores(PH - 1)
            for p in range(2):
                sp.wait_ge(h_stored[p], 16 * (5 - p))
            sp.wait_ge(stored, 16 * PH)

        @block.gpsimd
        def _(pool):
            pool.wait_ge(added, 9)
            pool.memset(scores[:, TT, :], 0.0).then_inc(cleared, 1)

        @block.tensor
        def _(pe):
            def mix_out(t):
                rows = P if t < TT else NS
                if t >= 2:
                    pe.wait_ge(added, t - 1)
                for s in range(2):
                    for q in range(DC):
                        last = pe.matmul(psum[0:rows, 2 * (t % 2) + s, :], mix[:, q, t * P:t * P + rows],
                                         w_out[:, q, s * 512:(s + 1) * 512], start=q == 0, stop=q == DC - 1)
                last.then_inc(mixed, 1)

            def turn(t):
                rows = P if t < TT else NS
                pe.wait_ge(normed_ready, t + 1)
                if t >= 2:
                    pe.wait_ge(lo_ready, t - 1)
                for q in range(DC):
                    last = pe.transpose(psum[:, 4 + 2 * (t % 2) + q // 4, (q % 4) * P:(q % 4) * P + rows],
                                        normed[0:rows, t % 2, q * P:(q + 1) * P], m["ident"][0:rows, 0:rows])
                last.then_inc(turn_ready, 1)

            pe.wait_ge(weights_loaded, 48)
            for t in range(9):
                mix_out(t)
                if t >= 1:
                    turn(t - 1)
            turn(8)
            pe.wait_ge(lo_ready, 9)
            with pe.Fori(0, PH) as i:
                for p in range(2):
                    pe.wait_ge(wq_lo_ready, i * 2 + p + 1)
                    pe.sem_inc(settled["pe"], 1)
                    pe.wait_ge(query_copied, i * 2 + p + 2)
                    for q in range(DC):
                        for w, xs in ((wq_hi, x_hi), (wq_hi, x_lo), (wq_lo, x_hi)):
                            for s in range(NSL):
                                last = pe.matmul(psum[:, s, 0:SL], w[:, p, q, :], xs[:, q, s * SL:(s + 1) * SL],
                                                 start=q == 0 and w is wq_hi and xs is x_hi,
                                                 stop=q == DC - 1 and w is wq_lo)
                    last.then_inc(query_ready, 1)
                    pe.wait_ge(query_copied, i * 2 + p + 3)
                    pe.sem_inc(settled["pe"], 1)
                    for b in range(3):
                        pe.wait_ge(score_copied, i * 6 + 3 * p + b + 1)
                        pe.sem_inc(settled["pe"], 1)
                        for t in range(4 * b, min(9, 4 * b + 4)):
                            rows = P if t < TT else NS
                            last = pe.matmul(psum[0:rows, 3 + b, (t % 4) * P:(t % 4 + 1) * P],
                                             query[:, p, t * P:t * P + rows],
                                             arena[:, bass.ds(word_keys + i * 2 * PK + p * PK, PK)],
                                             start=True, stop=True)
                        last.then_inc(scored, 1)

        @block.vector
        def _(dve):
            def split_tile(t):
                rows = P if t < TT else NS
                dve.wait_ge(hi_ready, t + 1)
                for b in range(2):
                    last = dve.tensor_tensor(
                        x_lo[:, 4 * b:4 * b + 4, t * P:t * P + rows],
                        psum[:, 4 + 2 * (t % 2) + b, :].rearrange("p (a b) -> p a b", a=4)[:, :, 0:rows],
                        x_hi[:, 4 * b:4 * b + 4, t * P:t * P + rows], ALU.subtract)
                last.then_inc(lo_ready, 1)

            for t in range(9):
                rows = P if t < TT else NS
                dve.wait_ge(mixed, t + 1)
                dve.wait_ge(x_loaded[t % 2], 16 * (t // 2 + 1))
                if t >= 2:
                    dve.wait_ge(h_stored[t % 2], 16 * (t // 2))
                dve.tensor_tensor(h_tile[0:rows, t % 2, :], x_tile[0:rows, t % 2, :],
                                  psum[0:rows, 2 * (t % 2):2 * (t % 2) + 2, :].rearrange("p a b -> p (a b)"),
                                  ALU.add).then_inc(added, 1)
                dve.wait_ge(rms_ready, t + 1)
                dve.reciprocal(rstd[0:rows, t:t + 1], ms[0:rows, t:t + 1])
                dve.drain()
                if t >= 2:
                    dve.wait_ge(turn_ready, t - 1)
                dve.scalar_tensor_tensor(out=normed[0:rows, t % 2, :], in0=h_tile[0:rows, t % 2, :],
                                         scalar=rstd[0:rows, t:t + 1], in1=norm2[0:rows],
                                         op0=ALU.mult, op1=ALU.mult).then_inc(normed_ready, 1)
                if t >= 1:
                    split_tile(t - 1)
            split_tile(8)
            dve.sem_inc(query_copied, 2)
            dve.sem_inc(score_copied, 3)
            dve.wait_ge(cleared, 1)
            with dve.Fori(0, PH) as i:
                for p in range(2):
                    dve.wait_ge(wq_hi_ready, i * 2 + p + 1)
                    dve.scalar_tensor_tensor(out=flat(wq_lo[:, p]), in0=flat(wq[:, p]), scalar=W_SCALE,
                                             in1=flat(wq_hi[:, p]), op0=ALU.mult,
                                             op1=ALU.subtract).then_inc(wq_lo_ready, 1)
                    dve.wait_ge(query_ready, i * 2 + p + 1)
                    dve.sem_inc(settled["dve"], 1)
                    for s in range(NSL):
                        last = dve.tensor_scalar(query[:, p, s * SL:(s + 1) * SL], psum[:, s, 0:SL], 1.0 / W_SCALE,
                                                 None, ALU.mult)
                    last.then_inc(query_copied, 1)
                    for b in range(3):
                        tiles = min(9, 4 * b + 4) - 4 * b
                        rows = P if b < 2 else NS
                        dve.wait_ge(scored, i * 6 + 3 * p + b + 1)
                        dve.tensor_scalar(
                            arena[0:rows, 0:9 * HALVES * PK].rearrange("p (t n) -> p t n", t=9)[
                                :, 4 * b:4 * b + tiles, bass.ds(i * 2 * PK + p * PK, PK)],
                            psum[0:rows, 3 + b, 0:tiles * P].rearrange("p (a b) -> p a b", b=P), 1.0, None,
                            ALU.mult).then_inc(score_copied, 1)

        @block.scalar
        def _(act):
            for t in range(9):
                rows = P if t < TT else NS
                act.wait_ge(added, t + 1)
                act.activation(junk[0:rows], h_tile[0:rows, t % 2, :], ACT.Square, accum_out=ms[0:rows, t:t + 1])
                act.drain()
                act.activation(ms[0:rows, t:t + 1], ms[0:rows, t:t + 1], ACT.Sqrt, bias=m["eps"][0:rows],
                               scale=1.0 / D).then_inc(rms_ready, 1)
                act.wait_ge(turn_ready, t + 1)
                for b in range(2):
                    last = act.copy(x_hi[:, 4 * b:4 * b + 4, t * P:t * P + rows],
                                    psum[:, 4 + 2 * (t % 2) + b, :].rearrange("p (a b) -> p a b", a=4)[:, :, 0:rows])
                last.then_inc(hi_ready, 1)
                act.drain()
            with act.Fori(0, PH) as i:
                for p in range(2):
                    act.wait_ge(wq_loaded[p], i * 16 + 16)
                    act.sem_inc(settled["act"], 1)
                    act.wait_ge(query_copied, i * 2 + p + 1)
                    act.mul(wq_hi[:, p], wq[:, p], W_SCALE).then_inc(wq_hi_ready, 1)


def expert_inputs(nc, x, m, windows_shifted):
    psum, at = m["psum"], m["at"]
    x_hi, x_lo = m["x_hi"], m["x_lo"]
    STEPS = 14
    LAST = PK - STEPS * TT
    GSTEPS = 8
    GROUP = 4
    assert STEPS % 2 == 0 and LAST >= STEPS
    with ExitStack() as c:
        sem = lambda n: c.enter_context(nc.semaphore(n))
        word = 0
        gates = at(word, PK, P); word += PK * P
        top_in = at(word, 2 * PH, PK); word += 2048
        left = at(word, 2 * PH, PK); word += 2048
        sums = at(word, PH, 256); one_hot1 = at(word, P, 16); word += 2048
        inner = at(word, PH, 256); one_hot0 = at(word, P, 16); word += 2048
        val = at(word, 16, 16); word += 256
        idx = at(word, 16, 16).bitcast(U32); word += 256
        idx_f = at(word, 16, 16); word += 256
        best = at(word, PH, 16); word += P
        best_i = at(word, P).bitcast(U32); word += P
        parts_i = at(word, 2, P).bitcast(U32); word += 2 * P
        parts = at(word, 2, P); word += 2 * P
        picks = at(word, 3, P); word += 3 * P
        gate = at(word, PH, 16); word += P
        den = at(word, 2, PH); word += 2 * PH
        turned = at(word, 5, P); word += 5 * P
        gate_hi16 = at(word, P // 2).bitcast(F16); word += P // 2
        iota = at(word, P // 2).bitcast(F16); word += P // 2
        iota_i = at(word, P).bitcast(I32); word += P
        hots = at(word, 2 * 16 * 3 * P // 2).bitcast(F16)\
            .rearrange("p (s t k n) -> p s t k n", s=2, t=16, k=3); word += 2 * 16 * 3 * P // 2
        u = at(word, 2, D); word += 2 * D
        u_hi = at(word, 2 * D // 2).bitcast(F16).rearrange("p (s c n) -> p s c n", s=2, c=DC); word += D
        u_lo = at(word, 2 * D // 2).bitcast(F16).rearrange("p (s c n) -> p s c n", s=2, c=DC); word += D
        acts = at(word, 2, T); word += 2 * T
        assert word <= XH0, word
        iota_ready = sem("iota_ready")
        u_loaded = [sem(f"u_loaded{i}") for i in range(2)]
        hi_ready = sem("u_hi_ready")
        lo_ready = sem("u_lo_ready")
        u_done = sem("u_product_done")
        gelu_done = sem("gelu_done")
        acts_stored = [sem(f"acts_stored{i}") for i in range(2)]
        scores_loaded = sem("scores_loaded")
        scores_read = sem("scores_read")
        gate_ready = sem("gate_ready")
        exp_done = sem("gate_exp_done")
        picks_ready = sem("picks_ready")
        picks_turned = sem("picks_turned")
        picks_copied = sem("picks_copied")
        hots_ready = sem("hots_ready")
        first_hots_ready = sem("first_hots_ready")
        gates_ready = sem("gates_ready")
        gates_copied = sem("gates_copied")
        gates_stored = sem("gates_stored")
        settled = {e: sem(f"u_settled_{e}") for e in ("act", "dve", "pool", "sp")}
        block = c.enter_context(nc.Block())
        GROUPS = P // GROUP
        PER_STEP = GROUPS // GSTEPS
        FIRST_GATES = STEPS - GSTEPS
        STORES = 4

        @block.sync
        def _(sp):
            def load_u(e, p):
                sp.dma_start(u[:, p, :], x["u_feat"][bass.ds(e, 1)].squeeze(0)).then_inc(u_loaded[p], 16)

            def step(t, s):
                n = t * STEPS + s
                whole = t is not TT
                if s == STORES and whole:
                    sp.wait_ge(scores_read, t + 1)
                    sp.dma_start(top_in, x["scores"][:, bass.ds(t + 1, 1)].squeeze(1)).then_inc(scores_loaded, 16)
                if whole or s + 2 < LAST:
                    sp.wait_ge(lo_ready, n + CREDIT + 1)
                    load_u(n + 2, s % 2)
                if STORES <= s < STORES + 8 and whole:
                    name, quarter = ("k", "v")[(s - STORES) // 4], (s - STORES) % 4
                    a, b = quarter * SHIFT, (quarter + 1) * SHIFT
                    sp.dma_start(x[f"{name}_win_sample"][bass.ds(t, 1), a:b, :].squeeze(0),
                                 x[f"cache_{name}"][bass.ds(t, 1), a + ST:b + ST, :].squeeze(0))\
                      .then_inc(windows_shifted, 16)
                sp.wait_ge(gelu_done, n + CREDIT + 1)
                sp.dma_start(x["acts"][bass.ds(n, 1)].squeeze(0), acts[:, s % 2, :])\
                  .then_inc(acts_stored[s % 2], 16)

            load_u(0, 0)
            load_u(1, 1)
            sp.dma_start(top_in, x["scores"][:, 0]).then_inc(scores_loaded, 16)
            for s in range(STORES):
                step(0, s)
            with sp.Fori(0, TT) as t:
                for s in range(STORES, STEPS):
                    step(t, s)
                for s in range(STORES):
                    step(t + 1, s)
                    if s == 0:
                        sp.wait_ge(gates_copied, t * GROUPS + GROUPS + CREDIT)
                    part = slice(s * PK // STORES, (s + 1) * PK // STORES)
                    sp.dma_start(x["gates"][part, :, bass.ds(t * P, P)].rearrange("a p n -> p a n"), gates[:, part, :])\
                      .then_inc(gates_stored, 16)
            for s in range(STORES, LAST):
                step(TT, s)
            sp.wait_ge(gates_copied, TT * GROUPS + NS // GROUP + CREDIT)
            sp.dma_start(x["gates"][:, :, SEQ:T].rearrange("a p n -> p a n"), gates[:, :, 0:NS])\
              .then_inc(gates_stored, 16)
            sp.wait_ge(gates_stored, 16 * (STORES * (TT + 1) + 1))
            for p in range(2):
                sp.wait_ge(acts_stored[p], 16 * (PK // 2 + 1))

        @block.gpsimd
        def _(pool):
            pool.iota(iota_i, pattern=[[1, P]], base=0, channel_multiplier=0).then_inc(iota_ready, 1)
            pool.wait_ge(iota_ready, 1)
            pool.tensor_copy(iota, iota_i).then_inc(iota_ready, 1)
            for n in range(2):
                pool.sem_inc(acts_stored[n], 16)
            pool.sem_inc(gates_stored, 16 * STORES)

            def first_hots(t, s):
                pool.wait_ge(gates_ready, t * GROUPS + PER_STEP * (s + 1))
                pool.sem_inc(settled["pool"], 1)
                pool.wait_ge(picks_copied, t + 1)
                pool.sem_inc(settled["pool"], 1)
                for n in range(16):
                    token = 16 * s + n
                    last = pool.tensor_scalar(hots[:, s % 2, n, 0, :], iota, turned[:, 0, token:token + 1], None,
                                              ALU.is_equal)
                    if n % GROUP == GROUP - 1:
                        last.then_inc(first_hots_ready, 1)

            with pool.Fori(0, TT) as t:
                for s in range(GSTEPS):
                    first_hots(t, s)
            for s in range(NS // 16):
                first_hots(TT, s)

        @block.tensor
        def _(pe):
            def product(n, s, between):
                p = s % 2
                pe.wait_ge(lo_ready, n + CREDIT + 1)
                pe.wait_ge(gelu_done, n + CREDIT - 1)
                for q in range(DC):
                    for w, xs in ((u_hi, x_hi), (u_hi, x_lo), (u_lo, x_hi)):
                        for k in range(NSL):
                            last = pe.matmul(psum[:, 3 * p + k, 0:SL], w[:, p, q, :], xs[:, q, k * SL:(k + 1) * SL],
                                             start=q == 0 and w is u_hi and xs is x_hi,
                                             stop=q == DC - 1 and w is u_lo)
                    if q == DC - 1:
                        last.then_inc(u_done, 1)
                    between(q)

            def turn_picks(t, rows):
                pe.wait_ge(picks_ready, t + 1)
                pe.wait_ge(gates_copied, t * GROUPS + CREDIT)
                for k in range(3):
                    last = pe.transpose(psum[:, 6, k * P:k * P + rows], picks[0:rows, k, :],
                                        m["ident"][0:rows, 0:rows])
                last.then_inc(picks_turned, 1)

            def gate_group(t, s, j):
                g = PER_STEP * s + j
                pe.wait_ge(hots_ready, t * GROUPS + g + 1)
                pe.wait_ge(first_hots_ready, t * GROUPS + g + 1)
                pe.wait_ge(picks_copied, t + 1)
                pe.wait_ge(gates_copied, t * GROUPS + g + CREDIT - 1)
                for i in range(GROUP):
                    row = hots[:, s % 2, GROUP * j + i]
                    for k in range(2):
                        last = pe.matmul(psum[:, 6 + g % 2, i * PK:(i + 1) * PK], row[:, 1 + k, :], row[:, 0, :],
                                         start=k == 0, stop=k == 1)
                last.then_inc(gates_ready, 1)

            pe.sem_inc(u_done, 1)

            def step(t, s, rows):
                def between(q):
                    if s == FIRST_GATES and q == 1:
                        turn_picks(t, rows)
                    if FIRST_GATES <= s < FIRST_GATES + rows // 16 and q >= DC - PER_STEP:
                        gate_group(t, s - FIRST_GATES, q - (DC - PER_STEP))

                product(t * STEPS + s, s, between)

            with pe.Fori(0, TT) as t:
                for s in range(STEPS):
                    step(t, s, P)
            for s in range(LAST):
                step(TT, s, NS)

        @block.vector
        def _(dve):
            def low_part(n, s):
                p = s % 2
                dve.wait_ge(hi_ready, n + CREDIT + 1)
                dve.scalar_tensor_tensor(out=flat(u_lo[:, p]), in0=u[:, p, :], scalar=W_SCALE,
                                         in1=flat(u_hi[:, p]), op0=ALU.mult, op1=ALU.subtract).then_inc(lo_ready, 1)

            def best16(width, values, where, src, tmp, r):
                def greatest(first, of):
                    for i in range(width):
                        dve.max(values[r, i, first:first + 8], of[r, i, :])
                    dve.drain()

                def places(first, of):
                    for i in range(width):
                        dve.max_index(where[r, i, first:first + 8], values[r, i, first:first + 8], of[r, i, :])

                def strike():
                    for i in range(width):
                        dve.match_replace(tmp[r, i, :], values[r, i, 0:8], src[r, i, :], LOWEST)
                    dve.drain()

                return greatest, places, strike

            def pieces(t, rows):
                r = slice(0, rows)
                key_greatest, key_places, key_strike = best16(2 * PH, val, idx, top_in, left, r)
                sum_greatest, sum_places, sum_strike = best16(
                    PH, best, best_i.rearrange("p (h k) -> p h k", h=PH), sums, inner, r)

                def first_eight():
                    dve.wait_ge(scores_loaded, 16 * t + 16)
                    dve.sem_inc(settled["dve"], 1)
                    key_greatest(0, top_in)

                def first_places():
                    key_places(0, top_in)
                    dve.drain()

                def strike_first():
                    key_strike()
                    dve.sem_inc(scores_read, 1)

                def next_places_and_sums():
                    key_places(8, left)
                    both = val[r].rearrange("p (h f) k -> p h f k", f=2)
                    dve.tensor_tensor(sums[r].rearrange("p h (a b) -> p h a b", a=16),
                                      both[:, :, 0, :].unsqueeze(3).broadcast_to([rows, PH, 16, 16]),
                                      both[:, :, 1, :].unsqueeze(2).broadcast_to([rows, PH, 16, 16]), ALU.add)
                    dve.drain()
                    dve.tensor_copy(idx_f[r], idx[r])

                def sums_first():
                    sum_greatest(0, sums)
                    sum_places(0, sums)

                def sums_next():
                    sum_strike()
                    sum_greatest(8, inner)

                def places_to_parts():
                    sum_places(8, inner)
                    dve.tensor_tensor(gate[r], best[r], best[r, :, 0:1].broadcast_to([rows, PH, 16]),
                                      ALU.subtract).then_inc(gate_ready, 1)
                    dve.drain()
                    dve.tensor_scalar(parts_i[r, 0, :], best_i[r], 4, None, ALU.logical_shift_right)
                    dve.tensor_scalar(parts_i[r, 1, :], best_i[r], 15, None, ALU.bitwise_and)
                    dve.drain()
                    dve.tensor_copy(parts[r], parts_i[r])
                    dve.drain()

                def one_hots():
                    for k, hot in enumerate((one_hot0, one_hot1)):
                        dve.tensor_tensor(hot[r], parts[r, k, :].unsqueeze(2).broadcast_to([rows, P, 16]),
                                          m["io16"][r].unsqueeze(1).broadcast_to([rows, P, 16]), ALU.is_equal)
                    dve.drain()

                def select_indices():
                    index = idx_f[r].rearrange("p (h f) k -> p h f k", f=2)
                    for k, hot in enumerate((one_hot0, one_hot1)):
                        o = hot[r].rearrange("p (h k) j -> p h k j", h=PH)
                        dve.tensor_tensor(o, o, index[:, :, k, :].unsqueeze(2).broadcast_to([rows, PH, 16, 16]),
                                          ALU.mult)

                def picks_and_gates():
                    dve.wait_ge(exp_done, t + 1)
                    dve.tensor_reduce(den[r, 0, :], gate[r], AX.X, ALU.add)
                    dve.drain()
                    for k, hot in enumerate((one_hot0, one_hot1)):
                        dve.tensor_reduce(picks[r, k, :], hot[r], AX.X, ALU.add)
                    dve.reciprocal(den[r, 1, :], den[r, 0, :])
                    dve.drain()
                    dve.tensor_tensor(picks[r, 2, :].rearrange("p (h k) -> p h k", h=PH), gate[r],
                                      den[r, 1, :].unsqueeze(2).broadcast_to([rows, PH, 16]), ALU.mult)
                    dve.drain().then_inc(picks_ready, 1)

                return [(first_eight, first_places), (strike_first, lambda: key_greatest(8, left)),
                        (next_places_and_sums, sums_first), (sums_next, places_to_parts),
                        (one_hots, select_indices), (picks_and_gates, None)]

            def copy_picks(t, rows):
                r = slice(0, rows)
                dve.wait_ge(picks_turned, t + 1)
                dve.tensor_copy(turned[:, 0:3, r], psum[:, 6, 0:3 * P].rearrange("p (k t) -> p k t", k=3)[:, :, r])
                dve.drain().then_inc(picks_copied, 1)
                dve.tensor_copy(gate_hi16[:, r], turned[:, 2, r])
                dve.drain()
                dve.tensor_copy(turned[:, 3, r], gate_hi16[:, r])
                dve.drain()
                dve.tensor_tensor(turned[:, 4, r], turned[:, 2, r], turned[:, 3, r], ALU.subtract)
                dve.drain()

            def hot_group(t, s, j):
                if j == 0:
                    dve.wait_ge(gates_ready, t * GROUPS + PER_STEP * (s + 1))
                for i in range(GROUP):
                    n = GROUP * j + i
                    token = 16 * s + n
                    row = hots[:, s % 2, n]
                    for k in range(2):
                        last = dve.tensor_scalar(row[:, 1 + k, :], iota, turned[:, 1, token:token + 1],
                                                 turned[:, 3 + k, token:token + 1], ALU.is_equal, ALU.mult)
                last.then_inc(hots_ready, 1)

            dve.sem_inc(lo_ready, CREDIT)
            dve.sem_inc(gates_ready, 2 * PER_STEP)
            dve.wait_ge(iota_ready, 2)
            low_part(0, 0)

            def step(t, s, rows):
                gating = FIRST_GATES <= s < FIRST_GATES + rows // 16
                if s == FIRST_GATES:
                    copy_picks(t, rows)
                if gating:
                    for j in range(PER_STEP // 2):
                        hot_group(t, s - FIRST_GATES, j)
                if s < FIRST_GATES:
                    before, after = pieces(t, rows)[s]
                    before()
                if t is not TT or s + 1 < LAST:
                    low_part(t * STEPS + s + 1, s + 1)
                if s < FIRST_GATES and after:
                    dve.sem_inc(settled["dve"], 1)
                    after()
                if gating:
                    for j in range(PER_STEP // 2, PER_STEP):
                        hot_group(t, s - FIRST_GATES, j)

            with dve.Fori(0, TT) as t:
                for s in range(STEPS):
                    step(t, s, P)
            for s in range(LAST):
                step(TT, s, NS)

        @block.scalar
        def _(act):
            def copy_gates(t, g):
                act.wait_ge(gates_ready, t * GROUPS + g + 2 * PER_STEP + 1)
                if g == 0:
                    act.wait_ge(gates_stored, 16 * STORES * (t + 1))
                act.copy(gates[:, :, GROUP * g:GROUP * g + GROUP].rearrange("p a t -> p t a"),
                         psum[:, 6 + g % 2, :].rearrange("p (t a) -> p t a", t=GROUP)).then_inc(gates_copied, 1)

            act.sem_inc(hi_ready, CREDIT)
            act.sem_inc(gelu_done, CREDIT)
            act.sem_inc(gates_copied, CREDIT)
            act.wait_ge(u_loaded[0], 16)
            act.mul(flat(u_hi[:, 0]), u[:, 0, :], W_SCALE).then_inc(hi_ready, 1)

            def step(t, s, rows):
                n = t * STEPS + s
                p = (s + 1) % 2
                if t is not TT or s + 1 < LAST:
                    act.wait_ge(u_loaded[p], (t * (STEPS // 2) + (s + 1) // 2) * 16 + 16)
                    act.sem_inc(settled["act"], 1)
                    act.wait_ge(u_done, n + 1)
                    act.mul(flat(u_hi[:, p]), u[:, p, :], W_SCALE).then_inc(hi_ready, 1)
                if FIRST_GATES <= s < FIRST_GATES + rows // 16:
                    for j in range(PER_STEP):
                        copy_gates(t, PER_STEP * (s - FIRST_GATES) + j)
                act.wait_ge(u_done, n + 2)
                act.sem_inc(settled["act"], 1)
                act.wait_ge(acts_stored[s % 2], (t * (STEPS // 2) + s // 2) * 16 + 16)
                act.activation(acts[:, s % 2, :].rearrange("p (k n) -> p k n", k=NSL),
                               psum[:, 3 * (s % 2):3 * (s % 2) + 3, 0:SL], ACT.Gelu,
                               scale=1.0 / W_SCALE).then_inc(gelu_done, 1)
                if s == FIRST_GATES - 2:
                    act.wait_ge(gate_ready, t + 1)
                    act.activation(gate[0:rows], gate[0:rows], ACT.Exp).then_inc(exp_done, 1)

            with act.Fori(0, TT) as t:
                for s in range(STEPS):
                    step(t, s, P)
            for s in range(LAST):
                step(TT, s, NS)


def expert_outputs(nc, x, m, windows_shifted):
    psum, at = m["psum"], m["at"]
    PER = 4
    GROUPS = PK // PER
    with ExitStack() as c:
        sem = lambda n: c.enter_context(nc.semaphore(n))
        word = 0
        y_sum = at(word, DC, T); word += DC * T
        acts = at(word, PER, T); word += PER * T
        gates = at(word, PER, T); word += PER * T
        v = at(word, PER, D); word += PER * D
        prod = at(word, 2, T); word += 2 * T

        def halves(n, width):
            nonlocal word
            view = at(word, n * width // 2).bitcast(F16).rearrange("p (g k n) -> p g k n", g=2, k=PER)
            word += n * width // 2
            return view

        h_hi, h_lo = halves(2 * PER, T), halves(2 * PER, T)
        v_hi, v_lo = halves(2 * PER, D), halves(2 * PER, D)
        norm_f = at(word, D); word += D
        h_tile = at(word, 2, D); word += 2 * D
        y_tile = at(word, 2, D); word += 2 * D
        junk = at(word, D); word += D
        ms = at(word, 9); word += 9
        rstd = at(word, 9); word += 9
        assert word <= WORDS, word
        loaded = [sem(f"expert_loaded{k}") for k in range(PER)]
        inputs_used = sem("inputs_used")
        prod_ready = sem("prod_ready")
        v_hi_ready = sem("v_hi_ready")
        h_hi_ready = sem("h_hi_ready")
        parts_ready = sem("parts_ready")
        chunk_ready = sem("chunk_ready")
        chunk_added = sem("chunk_added")
        h_loaded = [sem(f"h_loaded{i}") for i in range(2)]
        turned = sem("y_turned")
        summed = sem("y_summed")
        rms_ready = sem("rms_f_ready")
        y_ready = sem("y_ready")
        y_stored = [sem(f"y_stored{i}") for i in range(2)]
        settled = {e: sem(f"y_settled_{e}") for e in ("act", "dve")}
        block = c.enter_context(nc.Block())
        CHUNKS0 = 2 * DC

        @block.sync
        def _(sp):
            with sp.Fori(0, GROUPS) as g:
                for k in range(PER):
                    sp.wait_ge(inputs_used, (g * PER + k) * 2 + 2)
                    e = g * PER + k
                    sp.dma_start(v[:, k, :], x["peer_v"][bass.ds(e, 1)].squeeze(0)).then_inc(loaded[k], 16)
                    sp.dma_start(acts[:, k, :], x["acts"][bass.ds(e, 1)].squeeze(0)).then_inc(loaded[k], 16)
                    sp.dma_start(gates[:, k, :], x["gates"][bass.ds(e, 1)].squeeze(0)).then_inc(loaded[k], 16)
            sp.dma_start(norm_f, x["norm_f"]).then_inc(h_loaded[0], 16)
            for t in range(9):
                rows = P if t < TT else NS
                if t >= 2:
                    sp.wait_ge(summed, t - 1)
                sp.dma_start(h_tile[0:rows, t % 2, :], x["h"][t * P:t * P + rows, :]).then_inc(h_loaded[t % 2], 16)
                if t >= 1:
                    sp.wait_ge(y_ready, t)
                    sp.dma_start(x["y"][(t - 1) * P:t * P, :], y_tile[:, (t - 1) % 2, :]).then_inc(y_stored[(t - 1) % 2], 16)
            sp.wait_ge(y_ready, 9)
            sp.dma_start(x["y"][SEQ:T, :], y_tile[0:NS, 0, :]).then_inc(y_stored[0], 16)
            sp.wait_ge(y_stored[0], 16 * 5)
            sp.wait_ge(y_stored[1], 16 * 4)
            sp.wait_ge(windows_shifted, 16 * SHIFTS)

        @block.tensor
        def _(pe):
            pe.sem_inc(chunk_ready, CHUNKS0)
            with pe.Fori(0, GROUPS // 2) as i:
                for s in range(2):
                    pe.wait_ge(parts_ready, (i * 2 + s) * 2 * PER + 2 * PER)
                    for q in range(DC):
                        pe.wait_ge(chunk_added, (i * 2 + s) * DC + q + 1)
                        for k in range(PER):
                            for w, hs in ((v_hi, h_hi), (v_hi, h_lo), (v_lo, h_hi)):
                                for n in range(NSL):
                                    last = pe.matmul(psum[:, 3 * (q % 2) + n, 0:SL], w[:, s, k, q * P:(q + 1) * P],
                                                     hs[:, s, k, n * SL:(n + 1) * SL],
                                                     start=k == 0 and w is v_hi and hs is h_hi,
                                                     stop=k == PER - 1 and w is v_lo)
                        last.then_inc(chunk_ready, 1)
            pe.wait_ge(chunk_added, GROUPS * DC + 2)
            for t in range(9):
                rows = P if t < TT else NS
                if t >= 2:
                    pe.wait_ge(summed, t - 1)
                for q in range(DC):
                    last = pe.transpose(psum[0:rows, 2 * (t % 2) + q // 4, (q % 4) * P:(q % 4 + 1) * P],
                                        y_sum[:, q, t * P:t * P + rows], m["ident"])
                last.then_inc(turned, 1)

        @block.vector
        def _(dve):
            def multiply(g, s, k):
                e = g * PER + k
                dve.wait_ge(loaded[k], g * 48 + 48)
                dve.wait_ge(h_hi_ready, e + 1)
                dve.scalar_tensor_tensor(out=prod[:, k % 2, :], in0=acts[:, k, :], scalar=H_SCALE,
                                         in1=gates[:, k, :], op0=ALU.mult, op1=ALU.mult).then_inc(prod_ready, 1)

            def low_parts(g, s, k):
                e = g * PER + k
                dve.wait_ge(v_hi_ready, e + 1)
                dve.tensor_tensor(v_lo[:, s, k, :], v[:, k, :], v_hi[:, s, k, :], ALU.subtract)\
                   .then_inc(parts_ready, 1)
                dve.wait_ge(parts_ready, e * 2 + 1)
                dve.sem_inc(inputs_used, 2)
                dve.wait_ge(h_hi_ready, e + 3)
                dve.tensor_tensor(h_lo[:, s, k, :], prod[:, k % 2, :], h_hi[:, s, k, :], ALU.subtract)\
                   .then_inc(parts_ready, 1)

            def add_chunk(g, q):
                dve.wait_ge(chunk_ready, g * DC + q + CHUNKS0 + 1)
                y = y_sum[:, q, :].rearrange("p (k n) -> p k n", k=NSL)
                dve.tensor_tensor(y, y, psum[:, 3 * (q % 2):3 * (q % 2) + 3, 0:SL], ALU.add).then_inc(chunk_added, 1)

            def turn(g, s, prepare):
                for k in range(PER):
                    add_chunk(g, 2 * k)
                    if prepare:
                        multiply(g + 1, s, k)
                    add_chunk(g, 2 * k + 1)
                    if prepare:
                        low_parts(g + 1, s, k)

            dve.sem_inc(inputs_used, 2 * PER)
            dve.memset(y_sum, 0.0)
            dve.drain()
            for k in range(PER):
                multiply(0, 0, k)
                low_parts(0, 0, k)
            dve.sem_inc(chunk_added, 2)
            with dve.Fori(0, GROUPS // 2 - 1) as i:
                turn(i * 2, 1, True)
                turn(i * 2 + 1, 0, True)
            turn(GROUPS - 2, 1, True)
            turn(GROUPS - 1, 0, False)

            def finish(t):
                rows = P if t < TT else NS
                dve.wait_ge(rms_ready, t + 1)
                dve.reciprocal(rstd[0:rows, t:t + 1], ms[0:rows, t:t + 1])
                dve.drain()
                dve.scalar_tensor_tensor(out=y_tile[0:rows, t % 2, :], in0=y_tile[0:rows, t % 2, :],
                                         scalar=rstd[0:rows, t:t + 1], in1=norm_f[0:rows],
                                         op0=ALU.mult, op1=ALU.mult).then_inc(y_ready, 1)

            for t in range(9):
                rows = P if t < TT else NS
                dve.wait_ge(turned, t + 1)
                dve.wait_ge(h_loaded[t % 2], 16 * (t // 2 + 1 + (t + 1) % 2))
                if t >= 2:
                    dve.wait_ge(y_stored[t % 2], 16 * (t // 2))
                dve.scalar_tensor_tensor(out=y_tile[0:rows, t % 2, :],
                                         in0=psum[0:rows, 2 * (t % 2):2 * (t % 2) + 2, :].rearrange("p a b -> p (a b)"),
                                         scalar=1.0 / H_SCALE, in1=h_tile[0:rows, t % 2, :],
                                         op0=ALU.mult, op1=ALU.add).then_inc(summed, 1)
                if t >= 1:
                    finish(t - 1)
            finish(8)

        @block.scalar
        def _(act):
            act.sem_inc(h_hi_ready, 2)
            with act.Fori(0, GROUPS // 2) as i:
                for s in range(2):
                    for k in range(PER):
                        g = i * 2 + s
                        e = g * PER + k
                        act.wait_ge(loaded[k], g * 48 + 48)
                        if k == 0:
                            act.sem_inc(settled["act"], 1)
                            act.wait_ge(chunk_ready, g * DC + CHUNKS0 - DC)
                        act.copy(v_hi[:, s, k, :], v[:, k, :]).then_inc(v_hi_ready, 1)
                        act.wait_ge(prod_ready, e + 1)
                        act.copy(h_hi[:, s, k, :], prod[:, k % 2, :]).then_inc(h_hi_ready, 1)
            for t in range(9):
                rows = P if t < TT else NS
                act.wait_ge(summed, t + 1)
                act.activation(junk[0:rows], y_tile[0:rows, t % 2, :], ACT.Square, accum_out=ms[0:rows, t:t + 1])
                act.drain()
                act.activation(ms[0:rows, t:t + 1], ms[0:rows, t:t + 1], ACT.Sqrt, bias=m["eps"][0:rows],
                               scale=1.0 / D).then_inc(rms_ready, 1)


def log_count(distance):
    import numpy as np
    count = sum(((distance >= 0) & (distance <= window) & (distance % dilation == 0)).astype(np.int64)
                for window, dilation in ((128, 1), (512, 4), (2048, 16)))
    return np.where(count > 0, np.log(np.maximum(count, 1)), -1.0e30).astype(np.float32)


def prompt_bias():
    import numpy as np
    return log_count(np.arange(P)[:, None] + (SEQ - P) - np.arange(SEQ)[None, :])


def key_positions():
    import numpy as np
    far = np.arange(0, NB - NRECENT).reshape(-1, 16)[:, :ST].reshape(-1)
    assert len(far) == NSPARSE
    return np.concatenate([far, np.arange(NB - NRECENT, NB)])


def sample_bias():
    import numpy as np
    i = np.arange(ST)
    cached = log_count(NB + i[:, None] - key_positions()[None, :])
    own = np.where(i[:, None] >= i[None, :], log_count(i[:, None] - i[None, :]), np.float32(-1.0e30))
    new = np.full((SB, ST, SB, ST), -1.0e30, np.float32)
    for s in range(SB):
        new[s, :, s, :] = own
    rows = np.concatenate([np.broadcast_to(cached, (SB, ST, NKEY)), new.reshape(SB, ST, NS)], 2)
    rows = np.broadcast_to(rows[:, None], (SB, H, ST, NCOL)).reshape(2, P, NCOL)
    return rows.transpose(1, 0, 2).astype(np.float32)


def hgrn_constants():
    import numpy as np
    t = np.arange(T)
    chunk = np.where(t < SEQ, t // CH, NCH + (t - SEQ) // ST)
    same = lambda a: (chunk[a][:, None] == chunk[a][None, :]) & (t[a][:, None] <= t[a][None, :])
    resets = np.concatenate([[0.0], chunk[1:] == chunk[:-1]])
    return {
        "resets": np.broadcast_to(resets, (P, T)).astype(np.float32),
        "causal": same(slice(0, P)).astype(np.float32),
        "causal_s": same(slice(SEQ, T)).astype(np.float32),
        "only": (np.arange(NS)[:, None] // ST == np.arange(SB)[None, :]).astype(np.float32),
    }


def kernel(**inputs):
    import numpy as np
    import concourse.bacc as bacc
    from concourse.bass_utils import run_bass_kernel_spmd

    a = {k: np.asarray(v) for k, v in inputs.items()}
    x_all = np.concatenate([a["x_prompt"].reshape(SEQ, D), a["x_sample"].reshape(NS, D)], 0)
    w = a["w_in"][0].reshape(D, 7, 512)
    w = np.stack([w[:, i] for i in (0, 1, 3, 4, 6, 2, 5)])
    w = w.reshape(7, DC, P, 2, 256).transpose(0, 3, 2, 1, 4)
    ck = a["cache_k_win"][0].reshape(SB, NB, H * DH)
    cv = a["cache_v_win"][0].reshape(SB, NB, H * DH)
    chunked = lambda t: t.reshape(-1, P).T
    arrays = {
        "x_feat": x_all.T.reshape(DC, P, T).transpose(1, 0, 2),
        "x_tok": x_all,
        "norm1": chunked(a["norm1_w"][0]),
        "w_in": w.reshape(14, P, DC, 256),
        "bias_prompt": prompt_bias(),
        "bias_sample": sample_bias(),
        **hgrn_constants(),
        "keys_feat": ck[:, key_positions()].transpose(0, 2, 1).reshape(SB, 4, P, NKEY).transpose(0, 2, 1, 3),
        "vals_tok": cv[:, key_positions()].reshape(SB, NKEY // P, P, 512).transpose(0, 2, 1, 3),
        "lb_logits": a["hgrn_lb_logits"].reshape(2, G, P).transpose(2, 0, 1),
        "w_out": a["w_out"][0].reshape(DC, P, D).transpose(1, 0, 2),
        "norm2": np.broadcast_to(a["norm2_w"][0], (P, D)),
        "norm_f": np.broadcast_to(a["norm_f_w"], (P, D)),
        "wq": a["peer_wq"][0].reshape(DC, P, 2 * PH, P).transpose(2, 1, 0, 3),
        "sub_keys": a["peer_sub_keys"][0].reshape(2 * PH, PK, P).transpose(2, 0, 1),
        "u_feat": a["peer_u"][0].reshape(PK, PK, DC, P).transpose(0, 3, 2, 1).reshape(PK, P, D),
        "peer_v": a["peer_v"][0].reshape(PK, PK, D),
        "hgrn_norm": a["hgrn_norm_w"][0].reshape(P, 1),
        "state": a["state_hgrn"][0].transpose(2, 1, 0, 3),
        "cache_k": ck,
        "cache_v": cv,
    }
    arrays = {k: np.ascontiguousarray(v) for k, v in arrays.items()}
    outs = {
        "y": (T, D), "k_feat_out": (P, 4, T), "v_out": (P, TT, 512), "v_out_s": (NS, 512),
        "k_win_sample": (SB, NB, 512), "v_win_sample": (SB, NB, 512),
        "hgrn_p": (P, G, P), "hgrn_s": (P, G, SB, P),
    }
    nc = bacc.Bacc("TRN2", target_bir_lowering=False, num_devices=1)
    x = {k: nc.dram_tensor(f"in_{k}", v.shape, mybir.dt.from_np(v.dtype), kind="ExternalInput").ap()
         for k, v in arrays.items()}
    x.update({k: nc.dram_tensor(f"out_{k}", s, F32, kind="ExternalOutput").ap() for k, s in outs.items()})
    scratch = {"h": (T, D), "scores": (P, 9, 2 * PH * PK), "acts": (PK, P, T), "gates": (PK, P, T)}
    x.update({k: nc.dram_tensor(f"scratch_{k}", s, F32, kind="Internal").ap() for k, s in scratch.items()})
    build(nc, x)
    r = run_bass_kernel_spmd(nc, [{f"in_{k}": v for k, v in arrays.items()}], core_ids=[0]).results[0]
    got = {k: np.asarray(r[f"out_{k}"]) for k in outs}
    k_all = got["k_feat_out"].transpose(2, 1, 0).reshape(T, 512)
    v_all = got["v_out"].transpose(1, 0, 2).reshape(SEQ, 512)
    kw, vw = got["k_win_sample"], got["v_win_sample"]
    kw = np.concatenate([kw[:, :NB - ST], k_all[SEQ:].reshape(SB, ST, 512)], 1)
    vw = np.concatenate([vw[:, :NB - ST], got["v_out_s"].reshape(SB, ST, 512)], 1)
    win = (1, SB, NB, H, DH)
    return (
        got["y"][:SEQ].reshape(1, SEQ, D),
        got["y"][SEQ:].reshape(SB, ST, D),
        np.ascontiguousarray(k_all[:SEQ]).reshape(1, 1, SEQ, H, DH),
        np.ascontiguousarray(v_all).reshape(1, 1, SEQ, H, DH),
        np.ascontiguousarray(got["hgrn_p"].transpose(1, 0, 2)).reshape(1, 1, G, DK, DK),
        kw.reshape(win), vw.reshape(win),
        np.ascontiguousarray(got["hgrn_s"].transpose(2, 1, 0, 3)).reshape(1, SB, G, DK, DK),
    )
```

```python
from contextlib import ExitStack

import concourse.bass as bass
from concourse import mybir

F32 = mybir.dt.float32
F16 = mybir.dt.float16
I32 = mybir.dt.int32
U32 = mybir.dt.uint32
ALU = mybir.AluOpType
ACT = mybir.ActivationFunctionType
AX = mybir.AxisListType

P = 128
D = 1024
DC = D // P
SEQ = 1024
SB, ST = 8, 4
NS = SB * ST
T = SEQ + NS
TT = SEQ // P
SL = 352
NSL = T // SL
H, DH = 8, 64
G, DK = 4, 128
NB = 2048
EPS = 1e-6
EXPERTS = 16384
PH, PK, TOPK = 8, 128, 16
LOWEST = -3.0e38
NSPARSE = 384
NRECENT = 512
NKEY = NSPARSE + NRECENT
NCOL = NKEY + NS
CH = 32
NCH = SEQ // CH

FQ, FK, FHQ, FHF, FHG = range(5)

XT0 = 0
F0 = XT0 + DC * T
V0 = F0 + 5 * 4 * T
HI0 = V0 + 9 * 512
W0 = HI0 + 9 * 512
WORDS = 52880
XH0 = WORDS - DC * T

PRODUCTS = ((0, 0), (0, 1), (1, 0))
W_SCALE = 16.0
H_SCALE = 16.0
CREDIT = 2
SHIFT = (NB - ST) // 4
SHIFTS = 2 * SB * 4
PER = 4
INPUTS0 = PK * P


def expert_slots(at):
    return (at(INPUTS0, PER, D), at(INPUTS0 + PER * D, PER, T), at(INPUTS0 + PER * (D + T), PER, T))


def load_expert(sp, x, slots, e, k, loaded):
    for slot, name in zip(slots, ("peer_v", "acts", "gates")):
        sp.dma_start(slot[:, k, :], x[name][bass.ds(e, 1)].squeeze(0)).then_inc(loaded[k], 16)


def flat(ap):
    return ap.rearrange("p a b -> p (a b)")


def build(nc, x):
    with ExitStack() as whole:
        arena = whole.enter_context(nc.sbuf_tensor("arena", [P, WORDS], F32))
        psum = whole.enter_context(nc.psum_tensor("psum", [P, 8, 512], F32))
        consts = whole.enter_context(nc.sbuf_tensor("consts", [P, 288], F32))

        def at(word, *shape):
            n = 1
            for s in shape:
                n *= s
            v = arena[:, word:word + n]
            if len(shape) == 2:
                v = v.rearrange("p (a b) -> p a b", a=shape[0])
            if len(shape) == 3:
                v = v.rearrange("p (a b c) -> p a b c", a=shape[0], b=shape[1])
            return v

        m = {
            "arena": arena, "psum": psum, "at": at,
            "xn": at(XT0, DC, T), "mix": at(XT0, DC, T),
            "feat": at(F0, 5, 4, T), "v": at(V0, 9, 512), "hi": at(HI0, 9, 512),
            "ident": consts[:, 0:128], "ones": consts[:, 128:256], "io16": consts[:, 256:272],
            "eps": consts[:, 272:273],
            "x_hi": at(XH0, DC * T // 2).bitcast(F16).rearrange("p (c t) -> p c t", c=DC),
            "x_lo": at(XH0 + DC * T // 2, DC * T // 2).bitcast(F16).rearrange("p (c t) -> p c t", c=DC),
        }
        kv_out = whole.enter_context(nc.semaphore("kv_out"))
        done = whole.enter_context(nc.semaphore("windows_shifted"))
        loaded = [whole.enter_context(nc.semaphore(f"expert_loaded{k}")) for k in range(PER)]
        project_in(nc, x, m, kv_out)
        attend_prompt(nc, x, m, kv_out)
        attend_sample(nc, x, m)
        hgrn(nc, x, m)
        project_out(nc, x, m)
        expert_inputs(nc, x, m, done, loaded)
        expert_outputs(nc, x, m, done, loaded)


def project_in(nc, x, m, kv_out):
    psum, xn, feat, at = m["psum"], m["xn"], m["feat"], m["at"]
    parts = xn.bitcast(F16).rearrange("p c (k t) -> p c k t", k=2)
    with ExitStack() as c:
        sem = lambda n: c.enter_context(nc.semaphore(n))
        word = W0
        w = at(word, 2, DC, 256); word += 2 * DC * 256
        w_parts = at(word, 2 * DC * 256).bitcast(F16)\
            .rearrange("p (s k c n) -> p s k c n", s=2, k=2, c=DC); word += 2 * DC * 256
        sq = at(word, 2, T); word += 2 * T
        rstd = at(word, T); word += T
        nw = at(word, DC); word += DC
        kscale = at(word, 5); word += 5
        assert word <= WORDS
        chunk_loaded = [sem(f"chunk{q}_loaded") for q in range(DC)]
        norm_loaded = sem("norm_loaded")
        w_hi_ready = sem("w_hi_ready")
        w_lo_ready = sem("w_lo_ready")
        x_scaled = sem("x_scaled")
        x_hi_ready = sem("x_hi_ready")
        w_loaded = [sem(f"w_loaded{i}") for i in range(2)]
        consts_ready = sem("consts_ready")
        squared = sem("squared")
        square_used = sem("square_used")
        sums_ready = sem("sums_ready")
        rms_ready = sem("rms_ready")
        x_normed = sem("x_normed")
        piece_done = sem("piece_done")
        group_ready = sem("group_ready")
        bank_free = sem("bank_free")
        tile_ready = sem("tile_ready")
        tile_free = sem("tile_free")
        settled = {e: sem(f"in_settled_{e}") for e in ("act", "dve")}
        block = c.enter_context(nc.Block())

        @block.sync
        def _(sp):
            for q in range(DC):
                sp.dma_start(xn[:, q, :], x["x_feat"][:, q, :]).then_inc(chunk_loaded[q], 16)
            sp.dma_start(nw, x["norm1"]).then_inc(norm_loaded, 16)
            for p in range(2):
                sp.dma_start(w[:, p, :, :], x["w_in"][p]).then_inc(w_loaded[p], 16)
            with sp.Fori(1, 7) as i:
                for p in range(2):
                    sp.wait_ge(w_lo_ready, i * 2 + p - 1)
                    sp.dma_start(w[:, p, :, :], x["w_in"][bass.ds(i * 2 + p, 1)].squeeze(0)).then_inc(w_loaded[p], 16)
            sp.wait_ge(x_normed, DC + 6)
            sp.wait_ge(tile_free, 2 + 4 * 9)
            sp.dma_start(x["k_feat_out"], feat[:, FK, :, :]).then_inc(kv_out, 16)
            sp.dma_start(x["v_out"], m["v"][:, 0:TT, :]).then_inc(kv_out, 16)
            sp.dma_start(x["v_out_s"], m["v"][0:NS, TT, :]).then_inc(kv_out, 16)

        @block.gpsimd
        def _(pool):
            pool.memset(m["ones"], 1.0).then_inc(consts_ready, 1)
            pool.memset(m["ident"], 0.0).then_inc(consts_ready, 1)
            pool.wait_ge(consts_ready, 2)
            pool.affine_select(out=m["ident"], in_=m["ident"], compare_op=ALU.not_equal, fill=1.0,
                               base=0, pattern=[[-1, P]], channel_multiplier=1).then_inc(consts_ready, 1)
            pool.iota(m["io16"].bitcast(I32), pattern=[[1, 16]], base=0, channel_multiplier=0).then_inc(consts_ready, 1)
            pool.memset(m["eps"], EPS).then_inc(consts_ready, 1)
            pool.wait_ge(consts_ready, 5)
            pool.tensor_copy(m["io16"], m["io16"].bitcast(I32)).then_inc(consts_ready, 1)
            pool.wait_ge(consts_ready, 6)

        @block.scalar
        def _(act):
            for q in range(DC):
                act.wait_ge(chunk_loaded[q], 16)
                if q >= 2:
                    act.wait_ge(square_used, q - 1)
                act.activation(sq[:, q % 2, :], xn[:, q, :], ACT.Square).then_inc(squared, 1)
            for p in range(2):
                act.wait_ge(w_loaded[p], 16)
                act.mul(w_parts[:, p, 0], w[:, p], W_SCALE).then_inc(w_hi_ready, 1)
            act.wait_ge(consts_ready, 6)
            act.wait_ge(square_used, DC)
            for s in range(NSL):
                last = act.activation(rstd[:, s * SL:(s + 1) * SL], psum[:, s, 0:SL], ACT.Sqrt,
                                      bias=m["eps"], scale=1.0 / D)
            last.then_inc(rms_ready, 1)
            for q in range(DC):
                act.wait_ge(x_scaled, q + 1)
                act.copy(parts[:, q, 0, :], sq[:, q % 2, :]).then_inc(x_hi_ready, 1)
            with act.Fori(1, 7) as i:
                for p in range(2):
                    act.wait_ge(w_loaded[p], i * 16 + 16)
                    act.sem_inc(settled["act"], 1)
                    act.wait_ge(piece_done, i * 2 + p - 1)
                    act.sem_inc(settled["act"], 1)
                    act.mul(w_parts[:, p, 0], w[:, p], W_SCALE).then_inc(w_hi_ready, 1)

        @block.tensor
        def _(pe):
            pe.wait_ge(consts_ready, 6)
            for q in range(DC):
                pe.wait_ge(squared, q + 1)
                for s in range(NSL):
                    last = pe.matmul(psum[:, s, 0:SL], m["ones"], sq[:, q % 2, s * SL:(s + 1) * SL],
                                     start=q == 0, stop=q == DC - 1)
                last.then_inc(square_used, 1)
            with pe.Fori(0, 5) as i:
                for p in range(2):
                    pe.wait_ge(w_lo_ready, i * 2 + p + 1)
                    for j in range(2):
                        pe.wait_ge(bank_free, i * 4 + 2 * p + j + 1)
                        for q in range(DC):
                            if p == 0 and j == 0:
                                pe.wait_ge(x_normed, q + 1)
                            for w_part, x_part in PRODUCTS:
                                for s in range(NSL):
                                    last = pe.matmul(psum[:, 3 * j + s, 0:SL],
                                                     w_parts[:, p, w_part, q, j * P:(j + 1) * P],
                                                     parts[:, q, x_part, s * SL:(s + 1) * SL],
                                                     start=q == 0 and w_part == x_part,
                                                     stop=q == DC - 1 and w_part == 1)
                        last.then_inc(group_ready, 1)
                    pe.wait_ge(group_ready, i * 4 + 2 * p + 2)
                    pe.sem_inc(piece_done, 1)
            for i in range(2):
                for p in range(2):
                    pe.wait_ge(w_lo_ready, (5 + i) * 2 + p + 1)
                    n0 = (2 * i + p) * 9
                    for t in range(9):
                        rows = P if t < TT else NS
                        pe.wait_ge(tile_free, n0 + t + 1)
                        for q in range(DC):
                            for w_part, x_part in PRODUCTS:
                                last = pe.matmul(psum[0:rows, 6 + (n0 + t) % 2, 0:256],
                                                 parts[:, q, x_part, t * P:t * P + rows], w_parts[:, p, w_part, q, :],
                                                 start=q == 0 and w_part == x_part,
                                                 stop=q == DC - 1 and w_part == 1)
                        last.then_inc(tile_ready, 1)
                    pe.wait_ge(tile_ready, n0 + 9)
                    pe.sem_inc(piece_done, 1)

        @block.vector
        def _(dve):
            for i in range(5):
                dve.memset(kscale[:, i:i + 1], (DH ** -0.5 if i == FQ else 1.0) / W_SCALE)
            dve.drain()
            dve.sem_inc(bank_free, 2)
            dve.sem_inc(tile_free, 2)
            def w_low_part(p, n):
                dve.wait_ge(w_hi_ready, n)
                dve.scalar_tensor_tensor(out=w_parts[:, p, 1].rearrange("p c n -> p (c n)"), in0=flat(w[:, p]),
                                         scalar=W_SCALE, in1=w_parts[:, p, 0].rearrange("p c n -> p (c n)"),
                                         op0=ALU.mult, op1=ALU.subtract).then_inc(w_lo_ready, 1)

            def x_low_part(q):
                dve.wait_ge(x_hi_ready, q + 1)
                dve.tensor_tensor(parts[:, q, 1, :], sq[:, q % 2, :], parts[:, q, 0, :],
                                  ALU.subtract).then_inc(x_normed, 1)

            w_low_part(0, 1)
            w_low_part(1, 2)
            dve.wait_ge(rms_ready, 1)
            dve.reciprocal(rstd, rstd)
            dve.drain()
            dve.wait_ge(norm_loaded, 16)
            for q in range(DC):
                if q >= 2:
                    dve.wait_ge(x_normed, q - 1)
                dve.scalar_tensor_tensor(out=sq[:, q % 2, :], in0=xn[:, q, :], scalar=nw[:, q:q + 1], in1=rstd,
                                         op0=ALU.mult, op1=ALU.mult).then_inc(x_scaled, 1)
                if q >= 1:
                    x_low_part(q - 1)
            x_low_part(DC - 1)
            with dve.Fori(0, 5) as i:
                for p in range(2):
                    for j in range(2):
                        dve.wait_ge(group_ready, i * 4 + 2 * p + j + 1)
                        dve.sem_inc(settled["dve"], 1)
                        for s in range(NSL):
                            last = dve.tensor_scalar(
                                m["arena"][:, bass.ds(F0 + i * (4 * T) + (2 * p + j) * T + s * SL, SL)],
                                psum[:, 3 * j + s, 0:SL], kscale[:, bass.ds(i, 1)], None, ALU.mult)
                        last.then_inc(bank_free, 1)
                    w_low_part(p, i * 2 + p + 3)
            dve.drain().then_inc(x_normed, 6)
            for i in range(2):
                for p in range(2):
                    for t in range(9):
                        n = (2 * i + p) * 9 + t
                        rows = P if t < TT else NS
                        dve.wait_ge(tile_ready, n + 1)
                        dst = (m["v"], m["hi"])[i]
                        dve.tensor_scalar(dst[0:rows, t, p * 256:(p + 1) * 256], psum[0:rows, 6 + n % 2, 0:256],
                                          1.0 / W_SCALE, None, ALU.mult).then_inc(tile_free, 1)
                    if i == 0:
                        w_low_part(p, 13 + p)


def attend_prompt(nc, x, m, kv_out):
    psum, at, arena = m["psum"], m["at"], m["arena"]
    with ExitStack() as c:
        sem = lambda n: c.enter_context(nc.semaphore(n))
        word = W0
        bias = at(word, SEQ); word += SEQ
        probs = at(word, 2, SEQ); word += 2 * SEQ
        turned = at(word, 2, SEQ); word += 2 * SEQ
        pair_q = at(word, 2, SEQ); word += 2 * SEQ
        pair_k = at(word, 2, SEQ); word += 2 * SEQ
        out_tok = at(word, 2, P); word += 2 * P
        top = at(word, 2, 1); word += 2
        neg_top = at(word, 2, 1); word += 2
        total = at(word, 2, 2); word += 4
        inv = at(word, 2, 2); word += 4
        assert word <= WORDS
        bias_loaded = sem("bias_loaded")
        pair_staged = sem("pair_staged")
        scores_ready = sem("scores_ready")
        scores_read = sem("scores_read")
        max_ready = sem("max_ready")
        exp_ready = sem("exp_ready")
        piece_ready = sem("piece_ready")
        piece_copied = sem("piece_copied")
        values_ready = sem("values_ready")
        out_scaled = sem("out_scaled")
        out_turned = sem("out_turned")
        out_copied = sem("out_copied")
        settled = {e: sem(f"settled_{e}") for e in ("pe", "act", "dve")}
        block = c.enter_context(nc.Block())

        PAIRS = 2
        BLOCKS = PAIRS * 2 * TT
        TILES = PAIRS * TT
        tile = [n // 2 % TT for n in range(BLOCKS)]
        pieces = [1 if i < 4 else 2 for i in tile]
        before = [sum(pieces[:n]) for n in range(BLOCKS + 1)]
        PIECES = before[-1]
        SPARE = 4

        @block.sync
        def _(sp):
            sp.dma_start(bias, x["bias_prompt"]).then_inc(bias_loaded, 16)
            sp.wait_ge(kv_out, 48)

        @block.gpsimd
        def _(pool):
            for j in range(H // 2):
                if j >= PAIRS:
                    pool.wait_ge(scores_ready, (j - PAIRS + 1) * 2 * TT)
                pool.tensor_copy(pair_q[:, j % PAIRS, :], m["feat"][:, FQ, j, 0:SEQ]).then_inc(pair_staged, 1)
                pool.tensor_copy(pair_k[:, j % PAIRS, :], m["feat"][:, FK, j, 0:SEQ]).then_inc(pair_staged, 1)

        @block.tensor
        def _(pe):
            with pe.Fori(0, H // 2 // PAIRS) as turns:
                def scores(n):
                    pair, half, i = n // (2 * TT), n % 2, tile[n]
                    r = slice(64 * half, 64 * half + 64)
                    if n % (2 * TT) == 0:
                        pe.wait_ge(pair_staged, turns * (2 * PAIRS) + 2 * pair + 2)
                        pe.sem_inc(settled["pe"], 1)
                    pe.wait_ge(scores_read, turns * BLOCKS + n + 1)
                    pe.sem_inc(settled["pe"], 1)
                    width = (i + 1) * P
                    for s in range(0, width, 512):
                        e = min(width, s + 512)
                        last = pe.matmul(psum[:, 2 * (n % 2) + s // 512, 0:e - s],
                                         pair_q[r, pair, i * P:(i + 1) * P], pair_k[r, pair, s:e],
                                         start=True, stop=True)
                    last.then_inc(scores_ready, 1)

                def turn(n):
                    i = tile[n]
                    pe.wait_ge(exp_ready, turns * BLOCKS + n + 1)
                    for b in range(pieces[n]):
                        pe.wait_ge(piece_copied, turns * PIECES + before[n] + b + SPARE - 1)
                        for k in range(4 * b, min(i + 1, 4 * b + 4)):
                            last = pe.transpose(psum[:, 4 + (before[n] + b) % 2, (k % 4) * P:(k % 4 + 1) * P],
                                                probs[:, n % 2, k * P:(k + 1) * P], m["ident"])
                        last.then_inc(piece_ready, 1)

                def values(n):
                    pair, half, i = n // (2 * TT), n % 2, tile[n]
                    pe.wait_ge(piece_copied, turns * PIECES + before[n + 1] + SPARE)
                    pe.sem_inc(settled["pe"], 1)
                    pe.wait_ge(out_copied, turns * TILES + n // 2 + 1)
                    pe.sem_inc(settled["pe"], 1)
                    for k in range(i + 1):
                        last = pe.matmul(psum[:, 6 + n // 2 % 2, 64 * half:64 * half + 64],
                                         turned[:, n % 2, k * P:(k + 1) * P],
                                         arena[:, bass.ds(V0 + k * 512 + turns * (PAIRS * P) + pair * P + 64 * half, 64)],
                                         start=k == 0, stop=k == i)
                    last.then_inc(values_ready, 1)

                def turn_out(t):
                    pe.wait_ge(out_scaled, turns * TILES + t + 1)
                    pe.transpose(psum[:, 6 + t % 2, P:2 * P], out_tok[:, t % 2, :], m["ident"]).then_inc(out_turned, 1)

                scores(0)
                for n in range(BLOCKS):
                    if n + 1 < BLOCKS:
                        scores(n + 1)
                    turn(n)
                    if n >= 1:
                        values(n - 1)
                    if n >= 3 and n % 2 == 1:
                        turn_out(n // 2 - 1)
                values(BLOCKS - 1)
                turn_out(TILES - 1)

        @block.vector
        def _(dve):
            dve.sem_inc(scores_read, 2)
            dve.wait_ge(bias_loaded, 16)
            with dve.Fori(0, H // 2 // PAIRS) as turns:
                def add_bias(n):
                    width = (tile[n] + 1) * P
                    dve.wait_ge(scores_ready, turns * BLOCKS + n + 1)
                    dve.sem_inc(settled["dve"], 1)
                    dve.wait_ge(piece_copied, turns * PIECES + SPARE + (before[n - 1] if n else -pieces[-1]))
                    dve.sem_inc(settled["dve"], 1)
                    scores = psum[:, 2 * (n % 2):2 * (n % 2) + 2, :].rearrange("p a b -> p (a b)")
                    dve.tensor_tensor_reduce(probs[:, n % 2, 0:width], scores[:, 0:width],
                                             bias[:, SEQ - width:SEQ], 1.0, LOWEST, ALU.add, ALU.max,
                                             top[:, n % 2, :]).then_inc(scores_read, 1)
                    dve.drain()
                    dve.tensor_scalar(neg_top[:, n % 2, :], top[:, n % 2, :], -1.0, None,
                                      ALU.mult).then_inc(max_ready, 1)

                def scale_out(t):
                    dve.wait_ge(values_ready, turns * BLOCKS + 2 * t + 4)
                    dve.sem_inc(settled["dve"], 1)
                    dve.reciprocal(inv[:, t % 2, :], total[:, t % 2, :])
                    dve.drain()
                    dve.tensor_tensor(out_tok[:, t % 2, :].rearrange("p (h d) -> p h d", h=2),
                                      psum[:, 6 + t % 2, 0:P].rearrange("p (h d) -> p h d", h=2),
                                      inv[:, t % 2, :].unsqueeze(2).broadcast_to([P, 2, 64]),
                                      ALU.mult).then_inc(out_scaled, 1)

                for n in range(BLOCKS):
                    add_bias(n)
                    if n >= 3 and n % 2 == 1:
                        scale_out(n // 2 - 1)
                scale_out(TILES - 1)

        @block.scalar
        def _(act):
            act.sem_inc(piece_copied, SPARE)
            act.sem_inc(out_copied, 2)
            act.sem_inc(values_ready, 2)
            with act.Fori(0, H // 2 // PAIRS) as turns:
                def exps(n):
                    width = (tile[n] + 1) * P
                    act.wait_ge(max_ready, turns * BLOCKS + n + 1)
                    act.activation(probs[:, n % 2, 0:width], probs[:, n % 2, 0:width], ACT.Exp,
                                   bias=neg_top[:, n % 2, :],
                                   accum_out=total[:, n // 2 % 2, n % 2:n % 2 + 1]).then_inc(exp_ready, 1)

                def copy_pieces(n):
                    width = (tile[n] + 1) * P
                    act.wait_ge(values_ready, turns * BLOCKS + n + 1)
                    act.sem_inc(settled["act"], 1)
                    for b in range(pieces[n]):
                        s, e = 512 * b, min(width, 512 * b + 512)
                        act.wait_ge(piece_ready, turns * PIECES + before[n] + b + 1)
                        act.copy(turned[:, n % 2, s:e],
                                 psum[:, 4 + (before[n] + b) % 2, 0:e - s]).then_inc(piece_copied, 1)

                def copy_out(t):
                    pair, i = divmod(t, TT)
                    act.wait_ge(out_turned, turns * TILES + t + 1)
                    act.sem_inc(settled["act"], 1)
                    act.copy(arena[:, bass.ds(XT0 + i * P + pair * T + turns * (PAIRS * T), P)],
                             psum[:, 6 + t % 2, P:2 * P]).then_inc(out_copied, 1)

                for n in range(BLOCKS):
                    exps(n)
                    if n >= 1:
                        copy_pieces(n - 1)
                    if n >= 4 and n % 2 == 0:
                        copy_out(n // 2 - 2)
                copy_pieces(BLOCKS - 1)
                copy_out(TILES - 2)
                copy_out(TILES - 1)


def hgrn(nc, x, m):
    psum, at, feat, mix, hi = m["psum"], m["at"], m["feat"], m["mix"], m["hi"]
    GT = 4 * T
    with ExitStack() as c:
        sem = lambda n: c.enter_context(nc.semaphore(n))
        q, b, gate = feat[:, FHQ, :, :], feat[:, FHF, :, :], feat[:, FHG, :, :]
        word = W0
        k = mix[:, 4:8, :]
        ek = at(word, G, T); word += GT
        causal = at(word, P); word += P
        causal_s = at(word, NS); word += NS
        only = at(word, SB); word += SB
        hnorm = at(word, 1); word += 1
        carry = at(word, G, NCH + 1); word += G * (NCH + 1)
        carry_s = at(word, 2, G * SB).rearrange("p a (g b) -> p a g b", g=G); word += 2 * G * SB
        state = at(word, 4, G, P); word += 4 * G * P
        sum_state = at(word, 2, G, P); word += 2 * G * P
        masked = at(word, G, P); word += G * P
        assert word <= WORDS, word
        mean = ek[:, 0, :]
        eq = at(F0, G, T)
        state_s = at(F0 + GT, G, SB * P).rearrange("p g (b v) -> p g b v", b=SB)
        k_tok = at(V0, 9, 512)
        hi_only = m["arena"][0:NS, W0:W0 + SB * 512].rearrange("p (b n) -> p b n", b=SB)
        loaded = sem("hgrn_loaded")
        step_act = sem("hgrn_act")
        step_dve = sem("hgrn_dve")
        keys_scaled = sem("hgrn_keys_scaled")
        turn_ready = sem("hgrn_turn_ready")
        turn_copied = sem("hgrn_turn_copied")
        pair_ready = sem("hgrn_pair_ready")
        masked_ready = sem("hgrn_masked_ready")
        masked_used = sem("hgrn_masked_used")
        update_ready = sem("hgrn_update_ready")
        update_read = sem("hgrn_update_read")
        state_ready = sem("hgrn_state_ready")
        out_ready = sem("hgrn_out_ready")
        out_copied = sem("hgrn_out_copied")
        squared = sem("hgrn_squared")
        scaled = sem("hgrn_scaled")
        stored = sem("hgrn_stored")
        block = c.enter_context(nc.Block())

        @block.sync
        def _(sp):
            for dst, name in ((causal, "causal"), (causal_s[0:NS], "causal_s"), (only[0:NS], "only"),
                              (hnorm, "hgrn_norm"), (state_s, "state")):
                sp.dma_start(dst, x[name]).then_inc(loaded, 16)
            sp.wait_ge(step_dve, 4)
            sp.dma_start(x["hgrn_p"], sum_state[:, NCH % 2]).then_inc(stored, 16)
            sp.dma_start(x["hgrn_s"], state_s).then_inc(stored, 16)
            sp.wait_ge(stored, 32)

        @block.scalar
        def _(act):
            act.wait_ge(step_dve, 1)
            act.activation(ek, eq, ACT.Exp, scale=-1.0).then_inc(step_act, 1)
            act.drain()
            act.activation(eq, eq, ACT.Exp)
            act.activation(carry[:, :, 1:], carry[:, :, 1:], ACT.Exp)
            act.activation(carry_s, carry_s, ACT.Exp).then_inc(step_act, 1)
            for t in range(9):
                rows = P if t < TT else NS
                act.wait_ge(turn_ready, t + 1)
                act.copy(k_tok[0:rows, t, :], psum[0:rows, t % 2, :]).then_inc(turn_copied, 1)
            for n in range(NCH):
                if n >= 1:
                    act.wait_ge(update_read, G * n)
                if n >= 4:
                    act.wait_ge(out_ready, n - 3)
                for g in range(G):
                    last = act.activation(state[:, n % 4, g, :], sum_state[:, n % 2, g, :], ACT.Copy,
                                          scale=carry[:, g, n:n + 1])
                last.then_inc(state_ready, 1)
            act.wait_ge(step_dve, 5)
            act.activation(mean, mean, ACT.Sqrt).then_inc(step_act, 1)

        @block.tensor
        def _(pe):
            pe.wait_ge(keys_scaled, 1)
            for t in range(9):
                rows = P if t < TT else NS
                if t >= 2:
                    pe.wait_ge(turn_copied, t - 1)
                for g in range(G):
                    last = pe.transpose(psum[0:rows, t % 2, g * P:(g + 1) * P], k[:, g, t * P:t * P + rows],
                                        m["ident"])
                last.then_inc(turn_ready, 1)
            pe.wait_ge(turn_copied, 9)
            pe.wait_ge(step_dve, 2)

            def pairs_and_updates(t):
                tok = slice(t * P, (t + 1) * P)
                if t >= 1:
                    pe.wait_ge(masked_ready, t)
                for g in range(G):
                    last = pe.matmul(psum[:, 2, g * P:(g + 1) * P], k[:, g, tok], q[:, g, tok],
                                     start=True, stop=True)
                last.then_inc(pair_ready, 1)
                for j in range(4):
                    if t >= 1:
                        pe.wait_ge(update_read, G * (4 * t + j - 3))
                    rows = slice(CH * j, CH * j + CH)
                    for g in range(G):
                        last = pe.matmul(psum[:, 4 + j, g * P:(g + 1) * P], k_tok[rows, t, g * P:(g + 1) * P],
                                         hi[rows, t, g * P:(g + 1) * P], start=True, stop=True)
                    last.then_inc(update_ready, 1)

            pairs_and_updates(0)
            for t in range(TT):
                if t + 1 < TT:
                    pairs_and_updates(t + 1)
                pe.wait_ge(masked_ready, t + 1)
                if t >= 1:
                    pe.wait_ge(out_copied, t)
                for g in range(G):
                    last = pe.matmul(psum[:, 3, g * P:(g + 1) * P], hi[:, t, g * P:(g + 1) * P], masked[:, g, :],
                                     start=g == 0, stop=False, skip_group_check=True)
                last.then_inc(masked_used, 1)
                for j in range(4):
                    n = 4 * t + j
                    pe.wait_ge(state_ready, n + 1)
                    for g in range(G):
                        last = pe.matmul(psum[:, 3, g * P + CH * j:g * P + CH * j + CH], state[:, n % 4, g, :],
                                         q[:, g, n * CH:n * CH + CH], start=False, stop=j == 3,
                                         skip_group_check=True)
                    last.then_inc(out_ready, 1)
            tok = slice(SEQ, T)
            pe.wait_ge(masked_ready, TT)
            for g in range(G):
                last = pe.matmul(psum[0:NS, 2, g * NS:(g + 1) * NS], k[:, g, tok], q[:, g, tok],
                                 start=True, stop=True)
            last.then_inc(pair_ready, 1)
            pe.wait_ge(masked_ready, TT + 1)
            pe.wait_ge(out_copied, TT)
            for g in range(G):
                pe.matmul(psum[:, 3, g * NS:(g + 1) * NS], hi[0:NS, TT, g * P:(g + 1) * P],
                          masked[0:NS, g, 0:NS], start=g == 0, stop=False, skip_group_check=True)
            pe.wait_ge(step_dve, 3)
            for g in range(G):
                for s in range(SB):
                    last = pe.matmul(psum[:, 3, g * NS + ST * s:g * NS + ST * s + ST], state_s[:, g, s, :],
                                     q[:, g, SEQ + ST * s:SEQ + ST * s + ST], start=False, stop=s == SB - 1,
                                     skip_group_check=True)
            last.then_inc(out_ready, 1)
            for n in range(2 * G):
                g, half = divmod(n, 2)
                if n < 4:
                    pe.wait_ge(update_read, 4 * NCH)
                else:
                    pe.wait_ge(update_read, 4 * NCH + n - 3)
                last = pe.matmul(psum[:, 4 + n % 4, :].rearrange("p (b v) -> p b v", b=4),
                                 k_tok[0:NS, TT, g * P:(g + 1) * P],
                                 hi_only[:, 4 * half:4 * half + 4, g * P:(g + 1) * P], start=True, stop=True)
                last.then_inc(update_ready, 1)
            pe.wait_ge(squared, 1)
            pe.wait_ge(update_read, G * NCH + 2 * G)
            for s in range(NSL):
                for g in range(G):
                    last = pe.matmul(psum[32 * g:32 * g + 32, 4 + s, 0:SL], m["ones"][:, 0:32],
                                     eq[:, g, s * SL:(s + 1) * SL], start=True, stop=True)
            last.then_inc(turn_ready, 1)
            pe.wait_ge(step_dve, 6)
            for g in range(G):
                if g >= 2:
                    pe.wait_ge(scaled, g - 1)
                for s in range(NSL):
                    last = pe.matmul(psum[:, 4 * (g % 2) + s, 0:SL], masked[:, g, :],
                                     mean[:, s * SL:(s + 1) * SL], start=True, stop=True)
                last.then_inc(turn_ready, 1)

        @block.vector
        def _(dve):
            dve.wait_ge(loaded, 16 * 5)
            mid, mid_s = CH // 2 - 1, ST // 2 - 1
            chunks = b[:, :, 0:SEQ].rearrange("p g (n c) -> p g n c", c=CH)
            chunks_s = b[:, :, SEQ:T].rearrange("p g (n c) -> p g n c", c=ST)
            for g in range(G):
                dve.tensor_tensor(eq[:, g, 0:SEQ].rearrange("p (n c) -> p n c", c=CH), chunks[:, g],
                                  chunks[:, g, :, mid:mid + 1].broadcast_to([P, NCH, CH]), ALU.subtract)
                dve.tensor_tensor(eq[:, g, SEQ:T].rearrange("p (n c) -> p n c", c=ST), chunks_s[:, g],
                                  chunks_s[:, g, :, mid_s:mid_s + 1].broadcast_to([P, SB, ST]), ALU.subtract)
            dve.drain()
            ends = eq[:, :, 0:SEQ].rearrange("p g (n c) -> p g n c", c=CH)[:, :, :, CH - 1]
            ends_s = eq[:, :, SEQ:T].rearrange("p g (n c) -> p g n c", c=ST)[:, :, :, ST - 1]
            dve.tensor_copy(carry[:, :, NCH], ends[:, :, NCH - 1])
            dve.memset(carry[:, :, 0], 1.0)
            dve.tensor_tensor(carry[:, :, 1:NCH], ends[:, :, 0:NCH - 1], chunks[:, :, 1:NCH, mid], ALU.add)
            dve.tensor_copy(carry_s[:, 0], chunks_s[:, :, :, mid_s])
            dve.tensor_copy(carry_s[:, 1], ends_s)
            dve.drain()
            dve.tensor_scalar(eq, eq, 40.0, -40.0, ALU.min, ALU.max)
            dve.drain().then_inc(step_dve, 1)
            dve.wait_ge(step_act, 1)
            dve.memset(sum_state[:, 0], 0.0)
            dve.tensor_tensor(k, k, ek, ALU.mult)
            dve.drain().then_inc(keys_scaled, 1)
            dve.wait_ge(step_act, 2)
            dve.tensor_tensor(q, q, eq, ALU.mult)
            dve.drain().then_inc(step_dve, 1)

            def copy_out(t):
                dve.wait_ge(out_ready, 4 * t + 4)
                dve.tensor_copy(mix[:, 4:8, t * P:(t + 1) * P],
                                psum[:, 3, :].rearrange("p (g t) -> p g t", g=G)).then_inc(out_copied, 1)

            for t in range(TT):
                dve.wait_ge(pair_ready, t + 1)
                if t >= 1:
                    dve.wait_ge(masked_used, t)
                dve.tensor_tensor(masked, psum[:, 2, :].rearrange("p (g t) -> p g t", g=G),
                                  causal.unsqueeze(1).broadcast_to([P, G, P]), ALU.mult).then_inc(masked_ready, 1)
                for j in range(4):
                    n = 4 * t + j
                    dve.wait_ge(update_ready, n + 1)
                    if n >= 1:
                        dve.wait_ge(update_read, G * n)
                        dve.wait_ge(state_ready, n)
                    for g in range(G):
                        dve.scalar_tensor_tensor(out=sum_state[:, (n + 1) % 2, g, :], in0=sum_state[:, n % 2, g, :],
                                                 scalar=carry[:, g, n:n + 1], in1=psum[:, 4 + j, g * P:(g + 1) * P],
                                                 op0=ALU.mult, op1=ALU.add).then_inc(update_read, 1)
                if t >= 1:
                    copy_out(t - 1)
            copy_out(TT - 1)
            dve.wait_ge(update_read, G * NCH)
            for g in range(G):
                final = sum_state[:, NCH % 2, g, :]
                dve.tensor_scalar(final, final, carry[:, g, NCH:NCH + 1], None, ALU.mult)
            dve.wait_ge(masked_used, TT)
            dve.wait_ge(pair_ready, TT + 1)
            dve.tensor_tensor(masked[0:NS, :, 0:NS], psum[0:NS, 2, 0:P].rearrange("p (g t) -> p g t", g=G),
                              causal_s[0:NS].unsqueeze(1).broadcast_to([NS, G, NS]), ALU.mult).then_inc(masked_ready, 1)
            dve.tensor_tensor(state_s, state_s, carry_s[:, 0].unsqueeze(3).broadcast_to([P, G, SB, P]), ALU.mult)
            for s in range(SB):
                dve.tensor_scalar(hi_only[:, s, :], hi[0:NS, TT, :], only[0:NS, s:s + 1], None, ALU.mult)
            dve.drain().then_inc(step_dve, 1)
            dve.wait_ge(out_ready, 4 * TT + 1)
            dve.tensor_copy(mix[:, 4:8, SEQ:T],
                            psum[:, 3, 0:P].rearrange("p (g t) -> p g t", g=G)).then_inc(out_copied, 1)
            for n in range(2 * G):
                g, half = divmod(n, 2)
                dve.wait_ge(update_ready, NCH + n + 1)
                dve.tensor_tensor(state_s[:, g, 4 * half:4 * half + 4, :], state_s[:, g, 4 * half:4 * half + 4, :],
                                  psum[:, 4 + n % 4, :].rearrange("p (b v) -> p b v", b=4),
                                  ALU.add).then_inc(update_read, 1)
            dve.drain()
            dve.tensor_tensor(state_s, state_s, carry_s[:, 1].unsqueeze(3).broadcast_to([P, G, SB, P]), ALU.mult)
            dve.drain().then_inc(step_dve, 1)
            dve.tensor_tensor(eq, mix[:, 4:8, :], mix[:, 4:8, :], ALU.mult)
            for g in range(G):
                dve.tensor_copy(masked[:, g, :], m["ident"][:, 32 * g:32 * g + 1].broadcast_to([P, P]))
            dve.drain().then_inc(squared, 1)
            dve.scalar_tensor_tensor(out=mix[:, 4:8, :], in0=mix[:, 4:8, :], scalar=hnorm, in1=gate,
                                     op0=ALU.mult, op1=ALU.mult)
            dve.wait_ge(turn_ready, 10)
            dve.tensor_scalar(mean.rearrange("p (k n) -> p k n", k=NSL), psum[:, 4:4 + NSL, 0:SL], 1.0 / DK, EPS,
                              ALU.mult, ALU.add)
            dve.drain().then_inc(step_dve, 1)
            dve.wait_ge(step_act, 3)
            dve.reciprocal(mean, mean)
            dve.drain().then_inc(step_dve, 1)
            for g in range(G):
                dve.wait_ge(turn_ready, 10 + g + 1)
                o = mix[:, 4 + g, :].rearrange("p (k n) -> p k n", k=NSL)
                dve.tensor_tensor(o, o, psum[:, 4 * (g % 2):4 * (g % 2) + NSL, 0:SL], ALU.mult).then_inc(scaled, 1)
            dve.wait_ge(scaled, G)


def attend_sample(nc, x, m):
    psum, at, feat, mix = m["psum"], m["at"], m["feat"], m["mix"]
    KT = NKEY // P
    ROUND = 4
    with ExitStack() as c:
        sem = lambda n: c.enter_context(nc.semaphore(n))
        word = W0
        q_apart = at(word, 4 * SB, NS).rearrange("p (c b) r -> p c b r", c=4); word += 4 * SB * NS
        k_new = at(word, 4, NS); word += 4 * NS
        bias = at(word, 2, NCOL); word += 2 * NCOL
        probs = at(word, 2, NCOL); word += 2 * NCOL
        turned = at(word, KT + 1, P); word += (KT + 1) * P
        out_tok = at(word, 512); word += 512
        top = at(word, 2, 1); neg_top = at(word + 2, 2, 1); total = at(word + 4, 2, 1); inv = at(word + 6, 2, 1)
        word += 8
        keys = [at(word, 4, NKEY), at(F0, 4, NKEY)]
        vals = [at(word + 4 * NKEY, KT, 512), at(F0 + 4 * NKEY, KT, 512)]
        assert word + 4 * NKEY + KT * 512 <= WORDS
        f, k, silus = feat[:, FHF, :, :], mix[:, 4:8, :], (feat[:, FHQ, :, :], feat[:, FHG, :, :])
        word = F0 + 4 * NKEY + KT * 512
        resets = at(word, T); word += T
        logits = at(word, 2, G); word += 2 * G
        lbt = at(word, 8, G); word += 8 * G
        assert word <= F0 + 8 * T
        decay_act = sem("decay_act")
        decay_dve = sem("decay_dve")
        constants_loaded = sem("sample_constants_loaded")
        keys_loaded = [sem(f"keys_loaded{i}") for i in range(2)]
        vals_loaded = [sem(f"vals_loaded{i}") for i in range(2)]
        zeroed = sem("q_zeroed")
        new_ready = sem("new_ready")
        keys_used = sem("keys_used")
        vals_used = sem("vals_used")
        max_ready = sem("sample_max_ready")
        exp_ready = sem("sample_exp_ready")
        probs_ready = sem("sample_probs_ready")
        turn_ready = sem("sample_turn_ready")
        turn_copied = sem("sample_turn_copied")
        out_read = sem("sample_out_read")
        out_turned = sem("sample_out_turned")
        out_done = sem("sample_out_done")
        block = c.enter_context(nc.Block())

        @block.sync
        def _(sp):
            sp.dma_start(bias, x["bias_sample"]).then_inc(constants_loaded, 16)

            def load_keys(b):
                if b >= 2:
                    sp.wait_ge(keys_used, b - 1)
                sp.dma_start(keys[b % 2], x["keys_feat"][b]).then_inc(keys_loaded[b % 2], 16)

            def load_vals(b):
                if b >= 2:
                    sp.wait_ge(vals_used, b - 1)
                sp.dma_start(vals[b % 2], x["vals_tok"][b]).then_inc(vals_loaded[b % 2], 16)

            load_keys(0)
            sp.wait_ge(new_ready, 9)
            sp.dma_start(logits, x["lb_logits"]).then_inc(constants_loaded, 16)
            sp.dma_start(resets, x["resets"]).then_inc(constants_loaded, 16)
            load_keys(1)
            load_keys(2)
            load_keys(3)
            load_vals(0)
            load_vals(1)
            for b in range(ROUND, SB):
                load_keys(b)
            for b in range(2, SB):
                load_vals(b)

        @block.gpsimd
        def _(pool):
            pool.memset(q_apart, 0.0).then_inc(zeroed, 1)
            pool.tensor_copy(k_new, feat[:, FK, :, SEQ:T]).then_inc(new_ready, 1)

        @block.tensor
        def _(pe):
            def scores(b):
                rows = slice(32 * (b % ROUND), 32 * (b % ROUND) + 32)
                bank = 2 * (b // ROUND)
                pe.wait_ge(keys_loaded[b % 2], 16 * (b // 2 + 1))
                for (k0, k1, where) in ((0, 512, bank), (512, NKEY, bank + 1)):
                    for q in range(4):
                        pe.matmul(psum[rows, where, 0:k1 - k0], q_apart[:, q, b, :], keys[b % 2][:, q, k0:k1],
                                  start=q == 0, stop=q == 3)
                for q in range(4):
                    last = pe.matmul(psum[rows, bank + 1, NKEY - 512:NCOL - 512], q_apart[:, q, b, :], k_new[:, q, :],
                                     start=q == 0, stop=q == 3)
                last.then_inc(keys_used, 1)

            def turn(r):
                pe.wait_ge(probs_ready, r + 1)
                if r >= 1:
                    pe.wait_ge(turn_copied, 2 * r)
                for k in range(KT + 1):
                    cols = P if k < KT else NS
                    last = pe.transpose(psum[0:cols, 4 + k // 4, (k % 4) * P:(k % 4 + 1) * P],
                                        probs[:, r, k * P:k * P + cols], m["ident"])
                last.then_inc(turn_ready, 1)

            def values(b):
                r, col = b // ROUND, 32 * (b % ROUND)
                pe.wait_ge(turn_copied, 2 * r + 2)
                pe.wait_ge(vals_loaded[b % 2], 16 * (b // 2 + 1))
                out = psum[col:col + 32, 6 + r, :]
                for k in range(KT):
                    pe.matmul(out, turned[:, k, col:col + 32], vals[b % 2][:, k, :], start=k == 0, stop=False)
                last = pe.matmul(out, turned[0:NS, KT, col:col + 32], m["v"][0:NS, TT, :], start=False, stop=True)
                last.then_inc(vals_used, 1)

            def turn_out(r):
                pe.wait_ge(out_read, r + 1)
                for q in range(4):
                    last = pe.transpose(psum[:, 2 * r, q * P:(q + 1) * P], out_tok[:, q * P:(q + 1) * P], m["ident"])
                last.then_inc(out_turned, 1)

            pe.wait_ge(new_ready, 9)
            for b in range(SB):
                scores(b)
            for r in range(2):
                turn(r)
                for b in range(ROUND * r, ROUND * r + ROUND):
                    values(b)
                turn_out(r)

        @block.vector
        def _(dve):
            dve.wait_ge(zeroed, 1)
            for h in range(H):
                r = slice(64 * (h % 2), 64 * (h % 2) + 64)
                dve.tensor_copy(q_apart[r, h // 2, :, ST * h:ST * h + ST],
                                feat[r, FQ, h // 2, SEQ:T].rearrange("p (b i) -> p b i", b=SB)).then_inc(new_ready, 1)
            dve.wait_ge(constants_loaded, 48)
            dve.tensor_tensor(lbt[:, 0, :], logits[:, 0, :], logits[:, 1, :], ALU.max)
            dve.drain()
            for i in range(2):
                last = dve.tensor_tensor(lbt[:, 1 + i, :], logits[:, i, :], lbt[:, 0, :], ALU.subtract)
            last.then_inc(decay_dve, 1)
            dve.wait_ge(decay_act, 1)
            dve.tensor_tensor(lbt[:, 3, :], lbt[:, 1, :], lbt[:, 2, :], ALU.add)
            dve.drain()
            dve.reciprocal(lbt[:, 4, :], lbt[:, 3, :])
            dve.drain()
            dve.tensor_tensor(lbt[:, 5, :], lbt[:, 1, :], lbt[:, 4, :], ALU.mult)
            dve.drain()
            dve.tensor_scalar(lbt[:, 6, :], lbt[:, 5, :], -1.0, 1.0, ALU.mult, ALU.add)
            dve.drain()
            dve.wait_ge(decay_act, 2)
            for g in range(G):
                dve.tensor_scalar(f[:, g, :], f[:, g, :], lbt[:, 6, g:g + 1], lbt[:, 5, g:g + 1], ALU.mult, ALU.add)
            dve.drain()
            dve.tensor_scalar(k, f, -1.0, 1.0, ALU.mult, ALU.add)
            dve.drain().then_inc(decay_dve, 1)

            def sum_decays():
                dve.wait_ge(decay_act, 3)
                for g in range(G):
                    dve.tensor_tensor_scan(f[:, g, :], resets, f[:, g, :], 0.0, ALU.mult, ALU.add)
                dve.drain()

            def add_bias(r):
                dve.wait_ge(keys_used, ROUND * r + ROUND)
                scores = psum[:, 2 * r:2 * r + 2, :].rearrange("p a b -> p (a b)")
                dve.tensor_tensor_reduce(probs[:, r, :], scores[:, 0:NCOL], bias[:, r, :], 1.0, LOWEST,
                                         ALU.add, ALU.max, top[:, r, :])
                dve.drain()
                dve.tensor_scalar(neg_top[:, r, :], top[:, r, :], -1.0, None, ALU.mult).then_inc(max_ready, 1)

            def normalize(r):
                dve.wait_ge(exp_ready, r + 1)
                dve.reciprocal(inv[:, r, :], total[:, r, :])
                dve.drain()
                dve.tensor_scalar(probs[:, r, :], probs[:, r, :], inv[:, r, :], None,
                                  ALU.mult).then_inc(probs_ready, 1)

            def write_out(r):
                dve.wait_ge(vals_used, ROUND * r + ROUND)
                if r >= 1:
                    dve.wait_ge(out_turned, r)
                dve.tensor_copy(out_tok, psum[:, 6 + r, :]).then_inc(out_read, 1)
                dve.wait_ge(out_turned, r + 1)
                new = slice(SEQ + ROUND * ST * r, SEQ + ROUND * ST * (r + 1))
                for h in range(H):
                    rows, q = slice(64 * (h % 2), 64 * (h % 2) + 64), h // 2
                    own = psum[rows, 2 * r, q * P:(q + 1) * P].rearrange("p (b h i) -> p b h i", b=ROUND, h=H)
                    dve.tensor_copy(mix[rows, q, new].rearrange("p (b i) -> p b i", b=ROUND),
                                    own[:, :, h, :]).then_inc(out_done, 1)

            add_bias(0)
            normalize(0)
            sum_decays()
            add_bias(1)
            normalize(1)
            write_out(0)
            write_out(1)
            dve.wait_ge(out_done, 2 * H)

        @block.scalar
        def _(act):
            def exps(r):
                act.wait_ge(max_ready, r + 1)
                act.activation(probs[:, r, :], probs[:, r, :], ACT.Exp, bias=neg_top[:, r, :],
                               accum_out=total[:, r, :]).then_inc(exp_ready, 1)

            def copy_turned(r):
                act.wait_ge(turn_ready, r + 1)
                if r >= 1:
                    act.wait_ge(vals_used, ROUND * r)
                act.copy(turned[:, 0:4, :], psum[:, 4, :].rearrange("p (a b) -> p a b", a=4)).then_inc(turn_copied, 1)
                act.copy(turned[:, 4:KT, :],
                         psum[:, 5, 0:(KT - 4) * P].rearrange("p (a b) -> p a b", a=KT - 4))
                act.copy(turned[0:NS, KT, :], psum[0:NS, 5, (KT - 4) * P:(KT - 3) * P]).then_inc(turn_copied, 1)

            act.wait_ge(decay_dve, 1)
            act.activation(lbt[:, 1:3, :], lbt[:, 1:3, :], ACT.Exp).then_inc(decay_act, 1)
            act.activation(f, f, ACT.Sigmoid).then_inc(decay_act, 1)
            act.wait_ge(decay_dve, 2)
            act.activation(f, f, ACT.Ln).then_inc(decay_act, 1)
            exps(0)
            copy_turned(0)
            exps(1)
            for silu in silus:
                act.activation(silu, silu, ACT.Silu)
            copy_turned(1)
            act.drain()


def project_out(nc, x, m):
    psum, at, arena, mix = m["psum"], m["at"], m["arena"], m["mix"]
    x_hi, x_lo = m["x_hi"], m["x_lo"]
    HALVES = 2 * PH
    with ExitStack() as c:
        sem = lambda n: c.enter_context(nc.semaphore(n))
        scores = at(0, 9, HALVES * PK)
        word = DC * T
        w_out = at(word, DC, D); word += DC * D
        x_tile = at(word, 2, D); word += 2 * D
        h_tile = at(word, 2, D); word += 2 * D
        normed = at(word, 2, D); word += 2 * D
        wq = at(word, 2, DC, P); word += 2 * DC * P
        wq_hi = at(word, 2, DC * P // 2).bitcast(F16).rearrange("p s (c n) -> p s c n", c=DC); word += DC * P
        wq_lo = at(word, 2, DC * P // 2).bitcast(F16).rearrange("p s (c n) -> p s c n", c=DC); word += DC * P
        query = at(word, 2, T); word += 2 * T
        word_keys = word
        keys = at(word, HALVES, PK); word += HALVES * PK
        junk = at(word, D); word += D
        norm2 = at(word, D); word += D
        ms = at(word, 9); word += 9
        rstd = at(word, 9); word += 9
        assert word <= XH0 and DC * T + DC * D + 2 * D >= 9 * HALVES * PK
        w_out_loaded = [sem(f"w_out{q}_loaded") for q in range(4)]
        weights_loaded = sem("out_weights_loaded")
        x_loaded = [sem(f"x_tile_loaded{i}") for i in range(2)]
        wq_loaded = [sem(f"wq_loaded{i}") for i in range(2)]
        mixed = sem("mixed")
        added = sem("added")
        h_stored = [sem(f"h_stored{i}") for i in range(2)]
        rms_ready = sem("rms2_ready")
        normed_ready = sem("normed_ready")
        turn_ready = sem("normed_turned")
        hi_ready = sem("normed_hi_ready")
        lo_ready = sem("normed_lo_ready")
        wq_hi_ready = sem("wq_hi_ready")
        wq_lo_ready = sem("wq_lo_ready")
        query_ready = sem("query_ready")
        query_copied = sem("query_copied")
        scored = sem("scored")
        score_copied = sem("score_copied")
        cleared = sem("scores_cleared")
        stored = sem("scores_stored")
        settled = {e: sem(f"out_settled_{e}") for e in ("pe", "dve", "act")}
        block = c.enter_context(nc.Block())

        @block.sync
        def _(sp):
            for q in range(4):
                sp.dma_start(w_out[:, 2 * q:2 * q + 2, :], x["w_out"][:, 2 * q:2 * q + 2, :])\
                  .then_inc(w_out_loaded[q], 16)

            def load_x(t):
                rows = P if t < TT else NS
                sp.dma_start(x_tile[0:rows, t % 2, :], x["x_tok"][t * P:t * P + rows, :]).then_inc(x_loaded[t % 2], 16)

            load_x(0)
            sp.dma_start(norm2, x["norm2"]).then_inc(weights_loaded, 16)
            load_x(1)
            sp.dma_start(keys, x["sub_keys"]).then_inc(weights_loaded, 16)
            for p in range(2):
                sp.dma_start(wq[:, p], x["wq"][p]).then_inc(wq_loaded[p], 16)
            for t in range(9):
                rows = P if t < TT else NS
                sp.wait_ge(added, t + 1)
                sp.dma_start(x["h"][t * P:t * P + rows, :], h_tile[0:rows, t % 2, :]).then_inc(h_stored[t % 2], 16)
                if t + 2 < 9:
                    load_x(t + 2)
            def store_scores(i):
                sp.wait_ge(score_copied, i * 6 + 3 + 6)
                sp.dma_start(x["scores"][:, :, bass.ds(i * 2 * PK, 2 * PK)],
                             arena[:, 0:9 * HALVES * PK].rearrange("p (t n) -> p t n", t=9)[
                                 :, :, bass.ds(i * 2 * PK, 2 * PK)]).then_inc(stored, 16)

            with sp.Fori(1, PH) as i:
                for p in range(2):
                    sp.wait_ge(wq_lo_ready, i * 2 + p - 1)
                    sp.dma_start(wq[:, p], x["wq"][bass.ds(i * 2 + p, 1)].squeeze(0)).then_inc(wq_loaded[p], 16)
                store_scores(i - 1)
            store_scores(PH - 1)
            for p in range(2):
                sp.wait_ge(h_stored[p], 16 * (5 - p))
            sp.wait_ge(stored, 16 * PH)

        @block.gpsimd
        def _(pool):
            pool.wait_ge(added, 9)
            pool.memset(scores[:, TT, :], 0.0).then_inc(cleared, 1)

        @block.tensor
        def _(pe):
            def mix_out(t):
                rows = P if t < TT else NS
                if t >= 2:
                    pe.wait_ge(added, t - 1)
                for q in range(DC):
                    if t == 0 and q % 2 == 0:
                        pe.wait_ge(w_out_loaded[q // 2], 16)
                    for s in range(2):
                        last = pe.matmul(psum[0:rows, 2 * (t % 2) + s, :], mix[:, q, t * P:t * P + rows],
                                         w_out[:, q, s * 512:(s + 1) * 512], start=q == 0, stop=q == DC - 1)
                last.then_inc(mixed, 1)

            def turn(t):
                rows = P if t < TT else NS
                pe.wait_ge(normed_ready, t + 1)
                if t >= 2:
                    pe.wait_ge(lo_ready, t - 1)
                for q in range(DC):
                    last = pe.transpose(psum[:, 4 + 2 * (t % 2) + q // 4, (q % 4) * P:(q % 4) * P + rows],
                                        normed[0:rows, t % 2, q * P:(q + 1) * P], m["ident"][0:rows, 0:rows])
                last.then_inc(turn_ready, 1)

            for t in range(9):
                mix_out(t)
                if t >= 1:
                    turn(t - 1)
            turn(8)
            pe.wait_ge(lo_ready, 9)

            def product(i, p):
                pe.wait_ge(wq_lo_ready, i * 2 + p + 1)
                pe.wait_ge(query_copied, i * 2 + p + 1)
                for q in range(DC):
                    for w, xs in ((wq_hi, x_hi), (wq_hi, x_lo), (wq_lo, x_hi)):
                        for s in range(NSL):
                            last = pe.matmul(psum[:, 3 * (p % 2) + s, 0:SL], w[:, p % 2, q, :],
                                             xs[:, q, s * SL:(s + 1) * SL],
                                             start=q == 0 and w is wq_hi and xs is x_hi,
                                             stop=q == DC - 1 and w is wq_lo)
                last.then_inc(query_ready, 1)

            def score(i, p):
                pe.wait_ge(query_copied, i * 2 + p + 3)
                pe.sem_inc(settled["pe"], 1)
                for b in range(3):
                    pe.wait_ge(score_copied, i * 6 + 3 * p + b + 2)
                    pe.sem_inc(settled["pe"], 1)
                    for t in range(4 * b, min(9, 4 * b + 4)):
                        rows = P if t < TT else NS
                        last = pe.matmul(psum[0:rows, 6 + (p + b) % 2, (t % 4) * P:(t % 4 + 1) * P],
                                         query[:, p, t * P:t * P + rows],
                                         arena[:, bass.ds(word_keys + i * 2 * PK + p * PK, PK)],
                                         start=True, stop=True)
                    last.then_inc(scored, 1)

            pe.wait_ge(weights_loaded, 32)
            product(0, 0)
            with pe.Fori(0, PH - 1) as i:
                for p in range(2):
                    product(i, p + 1)
                    score(i, p)
            product(PH - 1, 1)
            score(PH - 1, 0)
            score(PH - 1, 1)

        @block.vector
        def _(dve):
            def split_tile(t):
                rows = P if t < TT else NS
                dve.wait_ge(hi_ready, t + 1)
                for b in range(2):
                    last = dve.tensor_tensor(
                        x_lo[:, 4 * b:4 * b + 4, t * P:t * P + rows],
                        psum[:, 4 + 2 * (t % 2) + b, :].rearrange("p (a b) -> p a b", a=4)[:, :, 0:rows],
                        x_hi[:, 4 * b:4 * b + 4, t * P:t * P + rows], ALU.subtract)
                last.then_inc(lo_ready, 1)

            dve.wait_ge(weights_loaded, 32)
            for t in range(9):
                rows = P if t < TT else NS
                dve.wait_ge(mixed, t + 1)
                dve.wait_ge(x_loaded[t % 2], 16 * (t // 2 + 1))
                if t >= 2:
                    dve.wait_ge(h_stored[t % 2], 16 * (t // 2))
                dve.tensor_tensor(h_tile[0:rows, t % 2, :], x_tile[0:rows, t % 2, :],
                                  psum[0:rows, 2 * (t % 2):2 * (t % 2) + 2, :].rearrange("p a b -> p (a b)"),
                                  ALU.add).then_inc(added, 1)
                dve.wait_ge(rms_ready, t + 1)
                dve.reciprocal(rstd[0:rows, t:t + 1], ms[0:rows, t:t + 1])
                dve.drain()
                if t >= 2:
                    dve.wait_ge(turn_ready, t - 1)
                dve.scalar_tensor_tensor(out=normed[0:rows, t % 2, :], in0=h_tile[0:rows, t % 2, :],
                                         scalar=rstd[0:rows, t:t + 1], in1=norm2[0:rows],
                                         op0=ALU.mult, op1=ALU.mult).then_inc(normed_ready, 1)
                if t >= 1:
                    split_tile(t - 1)
            split_tile(8)
            dve.sem_inc(query_copied, 2)
            dve.sem_inc(score_copied, 3)
            dve.wait_ge(cleared, 1)

            def low_part(i, p):
                dve.wait_ge(wq_hi_ready, i * 2 + p + 1)
                dve.scalar_tensor_tensor(out=flat(wq_lo[:, p % 2]), in0=flat(wq[:, p % 2]), scalar=W_SCALE,
                                         in1=flat(wq_hi[:, p % 2]), op0=ALU.mult,
                                         op1=ALU.subtract).then_inc(wq_lo_ready, 1)

            def copies(i, p, more):
                dve.wait_ge(query_ready, i * 2 + p + 1)
                dve.sem_inc(settled["dve"], 1)
                dve.tensor_scalar(query[:, p, :].rearrange("p (k n) -> p k n", k=NSL),
                                  psum[:, 3 * p:3 * p + NSL, 0:SL], 1.0 / W_SCALE,
                                  None, ALU.mult).then_inc(query_copied, 1)
                if more:
                    low_part(i, p + 2)
                for b in range(3):
                    tiles = min(9, 4 * b + 4) - 4 * b
                    rows = P if b < 2 else NS
                    dve.wait_ge(scored, i * 6 + 3 * p + b + 1)
                    dve.tensor_scalar(
                        arena[0:rows, 0:9 * HALVES * PK].rearrange("p (t n) -> p t n", t=9)[
                            :, 4 * b:4 * b + tiles, bass.ds(i * 2 * PK + p * PK, PK)],
                        psum[0:rows, 6 + (p + b) % 2, 0:tiles * P].rearrange("p (a b) -> p a b", b=P), 1.0, None,
                        ALU.mult).then_inc(score_copied, 1)

            low_part(0, 0)
            low_part(0, 1)
            with dve.Fori(0, PH - 1) as i:
                for p in range(2):
                    copies(i, p, True)
            for p in range(2):
                copies(PH - 1, p, False)

        @block.scalar
        def _(act):
            for t in range(9):
                rows = P if t < TT else NS
                act.wait_ge(added, t + 1)
                act.activation(junk[0:rows], h_tile[0:rows, t % 2, :], ACT.Square, accum_out=ms[0:rows, t:t + 1])
                act.drain()
                act.activation(ms[0:rows, t:t + 1], ms[0:rows, t:t + 1], ACT.Sqrt, bias=m["eps"][0:rows],
                               scale=1.0 / D).then_inc(rms_ready, 1)
                act.wait_ge(turn_ready, t + 1)
                for b in range(2):
                    last = act.copy(x_hi[:, 4 * b:4 * b + 4, t * P:t * P + rows],
                                    psum[:, 4 + 2 * (t % 2) + b, :].rearrange("p (a b) -> p a b", a=4)[:, :, 0:rows])
                last.then_inc(hi_ready, 1)
                act.drain()
            with act.Fori(0, PH) as i:
                for p in range(2):
                    act.wait_ge(wq_loaded[p], i * 16 + 16)
                    act.sem_inc(settled["act"], 1)
                    act.wait_ge(query_copied, i * 2 + p + 1)
                    act.mul(wq_hi[:, p], wq[:, p], W_SCALE).then_inc(wq_hi_ready, 1)


def expert_inputs(nc, x, m, windows_shifted, expert_loaded):
    psum, at = m["psum"], m["at"]
    x_hi, x_lo = m["x_hi"], m["x_lo"]
    STEPS = 14
    LAST = PK - STEPS * TT
    GSTEPS = 8
    GROUP = 4
    assert STEPS % 2 == 0 and LAST >= STEPS
    with ExitStack() as c:
        sem = lambda n: c.enter_context(nc.semaphore(n))
        word = 0
        gates = at(word, PK, P); word += PK * P
        top_in = at(word, 2 * PH, PK); word += 2048
        left = at(word, 2 * PH, PK); word += 2048
        sums = at(word, PH, 256); one_hot1 = at(word, P, 16); word += 2048
        inner = at(word, PH, 256); one_hot0 = at(word, P, 16); word += 2048
        val = at(word, 16, 16); word += 256
        idx = at(word, 16, 16).bitcast(U32); word += 256
        idx_f = at(word, 16, 16); word += 256
        best = at(word, PH, 16); word += P
        best_i = at(word, P).bitcast(U32); word += P
        parts_i = at(word, 2, P).bitcast(U32); word += 2 * P
        parts = at(word, 2, P); word += 2 * P
        picks = at(word, 3, P); word += 3 * P
        gate = at(word, PH, 16); word += P
        den = at(word, 2, PH); word += 2 * PH
        turned = at(word, 5, P); word += 5 * P
        gate_hi16 = at(word, P // 2).bitcast(F16); word += P // 2
        iota = at(word, P // 2).bitcast(F16); word += P // 2
        iota_i = at(word, P).bitcast(I32); word += P
        hots = at(word, 2 * 16 * 3 * P // 2).bitcast(F16)\
            .rearrange("p (s t k n) -> p s t k n", s=2, t=16, k=3); word += 2 * 16 * 3 * P // 2
        u = at(word, 2, D); word += 2 * D
        u_hi = at(word, 2 * D // 2).bitcast(F16).rearrange("p (s c n) -> p s c n", s=2, c=DC); word += D
        u_lo = at(word, 2 * D // 2).bitcast(F16).rearrange("p (s c n) -> p s c n", s=2, c=DC); word += D
        acts = at(word, 2, T); word += 2 * T
        assert word <= XH0, word
        slots = expert_slots(at)
        iota_ready = sem("iota_ready")
        u_loaded = [sem(f"u_loaded{i}") for i in range(2)]
        hi_ready = sem("u_hi_ready")
        lo_ready = sem("u_lo_ready")
        u_done = sem("u_product_done")
        gelu_done = sem("gelu_done")
        acts_stored = [sem(f"acts_stored{i}") for i in range(2)]
        scores_loaded = sem("scores_loaded")
        scores_read = sem("scores_read")
        gate_ready = sem("gate_ready")
        exp_done = sem("gate_exp_done")
        picks_ready = sem("picks_ready")
        picks_turned = sem("picks_turned")
        picks_copied = sem("picks_copied")
        hots_ready = sem("hots_ready")
        first_hots_ready = sem("first_hots_ready")
        gates_ready = sem("gates_ready")
        gates_copied = sem("gates_copied")
        gates_stored = sem("gates_stored")
        settled = {e: sem(f"u_settled_{e}") for e in ("act", "dve", "pool")}
        block = c.enter_context(nc.Block())
        GROUPS = P // GROUP
        PER_STEP = GROUPS // GSTEPS
        FIRST_GATES = STEPS - GSTEPS
        STORES = 4

        @block.sync
        def _(sp):
            def load_u(e, p):
                sp.dma_start(u[:, p, :], x["u_feat"][bass.ds(e, 1)].squeeze(0)).then_inc(u_loaded[p], 16)

            def step(t, s):
                n = t * STEPS + s
                whole = t is not TT
                if s == STORES and whole:
                    sp.wait_ge(scores_read, t + 1)
                    sp.dma_start(top_in, x["scores"][:, bass.ds(t + 1, 1)].squeeze(1)).then_inc(scores_loaded, 16)
                if whole or s + 2 < LAST:
                    sp.wait_ge(lo_ready, n + CREDIT + 1)
                    load_u(n + 2, s % 2)
                if STORES <= s < STORES + 8 and whole:
                    name, quarter = ("k", "v")[(s - STORES) // 4], (s - STORES) % 4
                    a, b = quarter * SHIFT, (quarter + 1) * SHIFT
                    sp.dma_start(x[f"{name}_win_sample"][bass.ds(t, 1), a:b, :].squeeze(0),
                                 x[f"cache_{name}"][bass.ds(t, 1), a + ST:b + ST, :].squeeze(0))\
                      .then_inc(windows_shifted, 16)
                sp.wait_ge(gelu_done, n + CREDIT + 1)
                sp.dma_start(x["acts"][bass.ds(n, 1)].squeeze(0), acts[:, s % 2, :])\
                  .then_inc(acts_stored[s % 2], 16)

            load_u(0, 0)
            load_u(1, 1)
            sp.dma_start(top_in, x["scores"][:, 0]).then_inc(scores_loaded, 16)
            for s in range(STORES):
                step(0, s)
            with sp.Fori(0, TT) as t:
                for s in range(STORES, STEPS):
                    step(t, s)
                for s in range(STORES):
                    step(t + 1, s)
                    if s == 0:
                        sp.wait_ge(gates_copied, t * GROUPS + GROUPS + CREDIT)
                    part = slice(s * PK // STORES, (s + 1) * PK // STORES)
                    sp.dma_start(x["gates"][part, :, bass.ds(t * P, P)].rearrange("a p n -> p a n"), gates[:, part, :])\
                      .then_inc(gates_stored, 16)
            for s in range(STORES, LAST):
                step(TT, s)
                if s == FIRST_GATES + NS // 16 + 1:
                    sp.wait_ge(gates_copied, TT * GROUPS + NS // GROUP + CREDIT)
                    sp.dma_start(x["gates"][:, :, SEQ:T].rearrange("a p n -> p a n"), gates[:, :, 0:NS])\
                      .then_inc(gates_stored, 16)
                if s == LAST - 3:
                    sp.wait_ge(gates_stored, 16 * (STORES * (TT + 1) + 1))
                    for p in range(2):
                        sp.wait_ge(acts_stored[p], 16 * ((PK - 2) // 2 + 1))
                    for k in range(2):
                        load_expert(sp, x, slots, k, k, expert_loaded)
                if s > LAST - 3:
                    k = s - (LAST - 2) + 2
                    load_expert(sp, x, slots, k, k, expert_loaded)
            for p in range(2):
                sp.wait_ge(acts_stored[p], 16 * (PK // 2 + 1))

        @block.gpsimd
        def _(pool):
            pool.iota(iota_i, pattern=[[1, P]], base=0, channel_multiplier=0).then_inc(iota_ready, 1)
            pool.wait_ge(iota_ready, 1)
            pool.tensor_copy(iota, iota_i).then_inc(iota_ready, 1)
            for n in range(2):
                pool.sem_inc(acts_stored[n], 16)
            pool.sem_inc(gates_stored, 16 * STORES)

            def first_hots(t, s):
                pool.wait_ge(gates_ready, t * GROUPS + PER_STEP * (s + 1))
                pool.sem_inc(settled["pool"], 1)
                pool.wait_ge(picks_copied, t + 1)
                pool.sem_inc(settled["pool"], 1)
                for n in range(16):
                    token = 16 * s + n
                    last = pool.tensor_scalar(hots[:, s % 2, n, 0, :], iota, turned[:, 0, token:token + 1], None,
                                              ALU.is_equal)
                    if n % GROUP == GROUP - 1:
                        last.then_inc(first_hots_ready, 1)

            with pool.Fori(0, TT) as t:
                for s in range(GSTEPS):
                    first_hots(t, s)
            for s in range(NS // 16):
                first_hots(TT, s)

        @block.tensor
        def _(pe):
            def product(n, s, between):
                p = s % 2
                pe.wait_ge(lo_ready, n + CREDIT + 1)
                pe.wait_ge(gelu_done, n + CREDIT - 1)
                for q in range(DC):
                    for w, xs in ((u_hi, x_hi), (u_hi, x_lo), (u_lo, x_hi)):
                        for k in range(NSL):
                            last = pe.matmul(psum[:, 3 * p + k, 0:SL], w[:, p, q, :], xs[:, q, k * SL:(k + 1) * SL],
                                             start=q == 0 and w is u_hi and xs is x_hi,
                                             stop=q == DC - 1 and w is u_lo)
                    if q == DC - 1:
                        last.then_inc(u_done, 1)
                    between(q)

            def turn_picks(t, rows):
                pe.wait_ge(picks_ready, t + 1)
                pe.wait_ge(gates_copied, t * GROUPS + CREDIT)
                for k in range(3):
                    last = pe.transpose(psum[:, 6, k * P:k * P + rows], picks[0:rows, k, :],
                                        m["ident"][0:rows, 0:rows])
                last.then_inc(picks_turned, 1)

            def gate_group(t, s, j):
                g = PER_STEP * s + j
                pe.wait_ge(hots_ready, t * GROUPS + g + 1)
                pe.wait_ge(first_hots_ready, t * GROUPS + g + 1)
                pe.wait_ge(picks_copied, t + 1)
                pe.wait_ge(gates_copied, t * GROUPS + g + CREDIT - 1)
                for i in range(GROUP):
                    row = hots[:, s % 2, GROUP * j + i]
                    for k in range(2):
                        last = pe.matmul(psum[:, 6 + g % 2, i * PK:(i + 1) * PK], row[:, 1 + k, :], row[:, 0, :],
                                         start=k == 0, stop=k == 1)
                last.then_inc(gates_ready, 1)

            pe.sem_inc(u_done, 1)

            def step(t, s, rows):
                def between(q):
                    if s == FIRST_GATES and q == 1:
                        turn_picks(t, rows)
                    if FIRST_GATES <= s < FIRST_GATES + rows // 16 and q >= DC - PER_STEP:
                        gate_group(t, s - FIRST_GATES, q - (DC - PER_STEP))

                product(t * STEPS + s, s, between)

            with pe.Fori(0, TT) as t:
                for s in range(STEPS):
                    step(t, s, P)
            for s in range(LAST):
                step(TT, s, NS)

        @block.vector
        def _(dve):
            def low_part(n, s):
                p = s % 2
                dve.wait_ge(hi_ready, n + CREDIT + 1)
                dve.scalar_tensor_tensor(out=flat(u_lo[:, p]), in0=u[:, p, :], scalar=W_SCALE,
                                         in1=flat(u_hi[:, p]), op0=ALU.mult, op1=ALU.subtract).then_inc(lo_ready, 1)

            def best16(width, values, where, src, tmp, r):
                def greatest(first, of):
                    for i in range(width):
                        dve.max(values[r, i, first:first + 8], of[r, i, :])
                    dve.drain()

                def places(first, of):
                    for i in range(width):
                        dve.max_index(where[r, i, first:first + 8], values[r, i, first:first + 8], of[r, i, :])

                def strike():
                    for i in range(width):
                        dve.match_replace(tmp[r, i, :], values[r, i, 0:8], src[r, i, :], LOWEST)
                    dve.drain()

                return greatest, places, strike

            def pieces(t, rows):
                r = slice(0, rows)
                key_greatest, key_places, key_strike = best16(2 * PH, val, idx, top_in, left, r)
                sum_greatest, sum_places, sum_strike = best16(
                    PH, best, best_i.rearrange("p (h k) -> p h k", h=PH), sums, inner, r)

                def first_eight():
                    dve.wait_ge(scores_loaded, 16 * t + 16)
                    dve.sem_inc(settled["dve"], 1)
                    key_greatest(0, top_in)

                def first_places():
                    key_places(0, top_in)
                    dve.drain()

                def strike_first():
                    key_strike()
                    dve.sem_inc(scores_read, 1)

                def next_places_and_sums():
                    key_places(8, left)
                    both = val[r].rearrange("p (h f) k -> p h f k", f=2)
                    dve.tensor_tensor(sums[r].rearrange("p h (a b) -> p h a b", a=16),
                                      both[:, :, 0, :].unsqueeze(3).broadcast_to([rows, PH, 16, 16]),
                                      both[:, :, 1, :].unsqueeze(2).broadcast_to([rows, PH, 16, 16]), ALU.add)
                    dve.drain()
                    dve.tensor_copy(idx_f[r], idx[r])

                def sums_first():
                    sum_greatest(0, sums)
                    sum_places(0, sums)

                def sums_next():
                    sum_strike()
                    sum_greatest(8, inner)

                def places_to_parts():
                    sum_places(8, inner)
                    dve.tensor_tensor(gate[r], best[r], best[r, :, 0:1].broadcast_to([rows, PH, 16]),
                                      ALU.subtract).then_inc(gate_ready, 1)
                    dve.drain()
                    dve.tensor_scalar(parts_i[r, 0, :], best_i[r], 4, None, ALU.logical_shift_right)
                    dve.tensor_scalar(parts_i[r, 1, :], best_i[r], 15, None, ALU.bitwise_and)
                    dve.drain()
                    dve.tensor_copy(parts[r], parts_i[r])
                    dve.drain()

                def one_hots():
                    for k, hot in enumerate((one_hot0, one_hot1)):
                        dve.tensor_tensor(hot[r], parts[r, k, :].unsqueeze(2).broadcast_to([rows, P, 16]),
                                          m["io16"][r].unsqueeze(1).broadcast_to([rows, P, 16]), ALU.is_equal)
                    dve.drain()

                def select_indices():
                    index = idx_f[r].rearrange("p (h f) k -> p h f k", f=2)
                    for k, hot in enumerate((one_hot0, one_hot1)):
                        o = hot[r].rearrange("p (h k) j -> p h k j", h=PH)
                        dve.tensor_tensor(o, o, index[:, :, k, :].unsqueeze(2).broadcast_to([rows, PH, 16, 16]),
                                          ALU.mult)

                def picks_and_gates():
                    dve.wait_ge(exp_done, t + 1)
                    dve.tensor_reduce(den[r, 0, :], gate[r], AX.X, ALU.add)
                    dve.drain()
                    for k, hot in enumerate((one_hot0, one_hot1)):
                        dve.tensor_reduce(picks[r, k, :], hot[r], AX.X, ALU.add)
                    dve.reciprocal(den[r, 1, :], den[r, 0, :])
                    dve.drain()
                    dve.tensor_tensor(picks[r, 2, :].rearrange("p (h k) -> p h k", h=PH), gate[r],
                                      den[r, 1, :].unsqueeze(2).broadcast_to([rows, PH, 16]), ALU.mult)
                    dve.drain().then_inc(picks_ready, 1)

                return [(first_eight, first_places), (strike_first, lambda: key_greatest(8, left)),
                        (next_places_and_sums, sums_first), (sums_next, places_to_parts),
                        (one_hots, select_indices), (picks_and_gates, None)]

            def copy_picks(t, rows):
                r = slice(0, rows)
                dve.wait_ge(picks_turned, t + 1)
                dve.tensor_copy(turned[:, 0:3, r], psum[:, 6, 0:3 * P].rearrange("p (k t) -> p k t", k=3)[:, :, r])
                dve.drain().then_inc(picks_copied, 1)
                dve.tensor_copy(gate_hi16[:, r], turned[:, 2, r])
                dve.drain()
                dve.tensor_copy(turned[:, 3, r], gate_hi16[:, r])
                dve.drain()
                dve.tensor_tensor(turned[:, 4, r], turned[:, 2, r], turned[:, 3, r], ALU.subtract)
                dve.drain()

            def hot_group(t, s, j):
                if j == 0:
                    dve.wait_ge(gates_ready, t * GROUPS + PER_STEP * (s + 1))
                for i in range(GROUP):
                    n = GROUP * j + i
                    token = 16 * s + n
                    row = hots[:, s % 2, n]
                    for k in range(2):
                        last = dve.tensor_scalar(row[:, 1 + k, :], iota, turned[:, 1, token:token + 1],
                                                 turned[:, 3 + k, token:token + 1], ALU.is_equal, ALU.mult)
                last.then_inc(hots_ready, 1)

            dve.sem_inc(lo_ready, CREDIT)
            dve.sem_inc(gates_ready, 2 * PER_STEP)
            dve.wait_ge(iota_ready, 2)
            low_part(0, 0)

            def step(t, s, rows):
                gating = FIRST_GATES <= s < FIRST_GATES + rows // 16
                if s == FIRST_GATES:
                    copy_picks(t, rows)
                if gating:
                    for j in range(PER_STEP // 2):
                        hot_group(t, s - FIRST_GATES, j)
                if s < FIRST_GATES:
                    before, after = pieces(t, rows)[s]
                    before()
                if t is not TT or s + 1 < LAST:
                    low_part(t * STEPS + s + 1, s + 1)
                if s < FIRST_GATES and after:
                    dve.sem_inc(settled["dve"], 1)
                    after()
                if gating:
                    for j in range(PER_STEP // 2, PER_STEP):
                        hot_group(t, s - FIRST_GATES, j)

            with dve.Fori(0, TT) as t:
                for s in range(STEPS):
                    step(t, s, P)
            for s in range(LAST):
                step(TT, s, NS)

        @block.scalar
        def _(act):
            def copy_gates(t, g):
                act.wait_ge(gates_ready, t * GROUPS + g + 2 * PER_STEP + 1)
                if g == 0:
                    act.wait_ge(gates_stored, 16 * STORES * (t + 1))
                act.copy(gates[:, :, GROUP * g:GROUP * g + GROUP].rearrange("p a t -> p t a"),
                         psum[:, 6 + g % 2, :].rearrange("p (t a) -> p t a", t=GROUP)).then_inc(gates_copied, 1)

            act.sem_inc(hi_ready, CREDIT)
            act.sem_inc(gelu_done, CREDIT)
            act.sem_inc(gates_copied, CREDIT)
            act.wait_ge(u_loaded[0], 16)
            act.mul(flat(u_hi[:, 0]), u[:, 0, :], W_SCALE).then_inc(hi_ready, 1)

            def step(t, s, rows):
                n = t * STEPS + s
                p = (s + 1) % 2
                if t is not TT or s + 1 < LAST:
                    act.wait_ge(u_loaded[p], (t * (STEPS // 2) + (s + 1) // 2) * 16 + 16)
                    act.sem_inc(settled["act"], 1)
                    act.wait_ge(u_done, n + 1)
                    act.mul(flat(u_hi[:, p]), u[:, p, :], W_SCALE).then_inc(hi_ready, 1)
                if FIRST_GATES <= s < FIRST_GATES + rows // 16:
                    for j in range(PER_STEP):
                        copy_gates(t, PER_STEP * (s - FIRST_GATES) + j)
                act.wait_ge(u_done, n + 2)
                act.sem_inc(settled["act"], 1)
                act.wait_ge(acts_stored[s % 2], (t * (STEPS // 2) + s // 2) * 16 + 16)
                act.activation(acts[:, s % 2, :].rearrange("p (k n) -> p k n", k=NSL),
                               psum[:, 3 * (s % 2):3 * (s % 2) + 3, 0:SL], ACT.Gelu,
                               scale=1.0 / W_SCALE).then_inc(gelu_done, 1)
                if s == FIRST_GATES - 2:
                    act.wait_ge(gate_ready, t + 1)
                    act.activation(gate[0:rows], gate[0:rows], ACT.Exp).then_inc(exp_done, 1)

            with act.Fori(0, TT) as t:
                for s in range(STEPS):
                    step(t, s, P)
            for s in range(LAST):
                step(TT, s, NS)


def expert_outputs(nc, x, m, windows_shifted, loaded):
    psum, at = m["psum"], m["at"]
    GROUPS = PK // PER
    with ExitStack() as c:
        sem = lambda n: c.enter_context(nc.semaphore(n))
        word = 0
        y_sum = at(word, DC, T); word += DC * T
        prod = at(word, 2, T); word += 2 * T
        norm_f = at(word, D); word += D
        y_tile = at(word, 4, D); word += 4 * D
        ms = at(word, 9); word += 9
        rstd = at(word, 9); word += 9
        assert word <= INPUTS0
        h_tile = at(INPUTS0, 9, D)
        assert 9 * D <= PER * (D + 2 * T)
        v, acts, gates = slots = expert_slots(at)
        word = INPUTS0 + PER * (D + 2 * T)

        def halves(n, width):
            nonlocal word
            view = at(word, n * width // 2).bitcast(F16).rearrange("p (g k n) -> p g k n", g=2, k=PER)
            word += n * width // 2
            return view

        h_hi, h_lo = halves(2 * PER, T), halves(2 * PER, T)
        v_hi, v_lo = halves(2 * PER, D), halves(2 * PER, D)
        junk = at(word, D); word += D
        assert word <= WORDS, word
        inputs_used = sem("inputs_used")
        prod_ready = sem("prod_ready")
        v_hi_ready = sem("v_hi_ready")
        h_hi_ready = sem("h_hi_ready")
        parts_ready = sem("parts_ready")
        chunk_ready = sem("chunk_ready")
        chunk_added = sem("chunk_added")
        h_loaded = sem("h_loaded")
        cleared = sem("y_cleared")
        turned = sem("y_turned")
        summed = sem("y_summed")
        rms_ready = sem("rms_f_ready")
        y_ready = sem("y_ready")
        y_stored = [sem(f"y_stored{i}") for i in range(4)]
        settled = {e: sem(f"y_settled_{e}") for e in ("act", "dve")}
        block = c.enter_context(nc.Block())
        CHUNKS0 = 2 * DC

        @block.sync
        def _(sp):
            with sp.Fori(1, GROUPS) as g:
                for k in range(PER):
                    sp.wait_ge(inputs_used, (g * PER + k) * 2 + 2)
                    load_expert(sp, x, slots, g * PER + k, k, loaded)
            sp.dma_start(norm_f, x["norm_f"]).then_inc(h_loaded, 16)
            sp.wait_ge(inputs_used, 2 * PER + 2 * PK)
            sp.dma_start(h_tile[:, 0:TT, :], x["h"][0:SEQ, :].rearrange("(t p) d -> p t d", p=P)).then_inc(h_loaded, 16)
            sp.dma_start(h_tile[0:NS, TT, :], x["h"][SEQ:T, :]).then_inc(h_loaded, 16)
            for t in range(9):
                rows = P if t < TT else NS
                sp.wait_ge(y_ready, t + 1)
                sp.dma_start(x["y"][t * P:t * P + rows, :], y_tile[0:rows, t % 4, :]).then_inc(y_stored[t % 4], 16)
            for i in range(4):
                sp.wait_ge(y_stored[i], 16 * len(range(i, 9, 4)))
            sp.wait_ge(windows_shifted, 16 * SHIFTS)

        @block.gpsimd
        def _(pool):
            pool.memset(y_sum, 0.0).then_inc(cleared, 1)

        @block.tensor
        def _(pe):
            pe.sem_inc(chunk_ready, CHUNKS0)
            with pe.Fori(0, GROUPS // 2) as i:
                for s in range(2):
                    pe.wait_ge(parts_ready, (i * 2 + s) * 2 * PER + 2 * PER)
                    for q in range(DC):
                        pe.wait_ge(chunk_added, (i * 2 + s) * DC + q + 1)
                        for k in range(PER):
                            for w, hs in ((v_hi, h_hi), (v_hi, h_lo), (v_lo, h_hi)):
                                for n in range(NSL):
                                    last = pe.matmul(psum[:, 3 * (q % 2) + n, 0:SL], w[:, s, k, q * P:(q + 1) * P],
                                                     hs[:, s, k, n * SL:(n + 1) * SL],
                                                     start=k == 0 and w is v_hi and hs is h_hi,
                                                     stop=k == PER - 1 and w is v_lo)
                        last.then_inc(chunk_ready, 1)
            pe.wait_ge(chunk_added, GROUPS * DC + 2)
            for t in range(9):
                rows = P if t < TT else NS
                if t >= 2:
                    pe.wait_ge(summed, t - 1)
                for q in range(DC):
                    last = pe.transpose(psum[0:rows, 2 * (t % 2) + q // 4, (q % 4) * P:(q % 4 + 1) * P],
                                        y_sum[:, q, t * P:t * P + rows], m["ident"])
                last.then_inc(turned, 1)

        @block.vector
        def _(dve):
            def multiply(g, s, k):
                e = g * PER + k
                dve.wait_ge(loaded[k], g * 48 + 48)
                dve.wait_ge(h_hi_ready, e + 1)
                dve.scalar_tensor_tensor(out=prod[:, k % 2, :], in0=acts[:, k, :], scalar=H_SCALE,
                                         in1=gates[:, k, :], op0=ALU.mult, op1=ALU.mult).then_inc(prod_ready, 1)

            def low_parts(g, s, k):
                e = g * PER + k
                dve.wait_ge(v_hi_ready, e + 1)
                dve.tensor_tensor(v_lo[:, s, k, :], v[:, k, :], v_hi[:, s, k, :], ALU.subtract)\
                   .then_inc(parts_ready, 1)
                dve.wait_ge(parts_ready, e * 2 + 1)
                dve.sem_inc(inputs_used, 2)
                dve.wait_ge(h_hi_ready, e + 3)
                dve.tensor_tensor(h_lo[:, s, k, :], prod[:, k % 2, :], h_hi[:, s, k, :], ALU.subtract)\
                   .then_inc(parts_ready, 1)

            def add_chunk(g, q):
                dve.wait_ge(chunk_ready, g * DC + q + CHUNKS0 + 1)
                y = y_sum[:, q, :].rearrange("p (k n) -> p k n", k=NSL)
                dve.tensor_tensor(y, y, psum[:, 3 * (q % 2):3 * (q % 2) + 3, 0:SL], ALU.add).then_inc(chunk_added, 1)

            def turn(g, s, prepare):
                for k in range(PER):
                    if prepare:
                        multiply(g + 1, s, k)
                    add_chunk(g, 2 * k)
                    if prepare:
                        low_parts(g + 1, s, k)
                    add_chunk(g, 2 * k + 1)

            dve.sem_inc(inputs_used, 2 * PER)
            for k in range(PER):
                multiply(0, 0, k)
                low_parts(0, 0, k)
            dve.wait_ge(cleared, 1)
            dve.sem_inc(chunk_added, 2)
            with dve.Fori(0, GROUPS // 2 - 1) as i:
                turn(i * 2, 1, True)
                turn(i * 2 + 1, 0, True)
            turn(GROUPS - 2, 1, True)
            turn(GROUPS - 1, 0, False)

            def finish(t):
                rows = P if t < TT else NS
                dve.wait_ge(rms_ready, t + 1)
                dve.reciprocal(rstd[0:rows, t:t + 1], ms[0:rows, t:t + 1])
                dve.drain()
                dve.scalar_tensor_tensor(out=y_tile[0:rows, t % 4, :], in0=y_tile[0:rows, t % 4, :],
                                         scalar=rstd[0:rows, t:t + 1], in1=norm_f[0:rows],
                                         op0=ALU.mult, op1=ALU.mult).then_inc(y_ready, 1)

            for t in range(9):
                rows = P if t < TT else NS
                dve.wait_ge(turned, t + 1)
                dve.wait_ge(h_loaded, 48)
                if t >= 4:
                    dve.wait_ge(y_stored[t % 4], 16 * (t // 4))
                dve.scalar_tensor_tensor(out=y_tile[0:rows, t % 4, :],
                                         in0=psum[0:rows, 2 * (t % 2):2 * (t % 2) + 2, :].rearrange("p a b -> p (a b)"),
                                         scalar=1.0 / H_SCALE, in1=h_tile[0:rows, t, :],
                                         op0=ALU.mult, op1=ALU.add).then_inc(summed, 1)
                if t >= 1:
                    finish(t - 1)
            finish(8)

        @block.scalar
        def _(act):
            act.sem_inc(h_hi_ready, 2)
            with act.Fori(0, GROUPS // 2) as i:
                for s in range(2):
                    for k in range(PER):
                        g = i * 2 + s
                        e = g * PER + k
                        act.wait_ge(loaded[k], g * 48 + 48)
                        if k == 0:
                            act.sem_inc(settled["act"], 1)
                            act.wait_ge(chunk_ready, g * DC + CHUNKS0 - DC)
                        act.copy(v_hi[:, s, k, :], v[:, k, :]).then_inc(v_hi_ready, 1)
                        act.wait_ge(prod_ready, e + 1)
                        act.copy(h_hi[:, s, k, :], prod[:, k % 2, :]).then_inc(h_hi_ready, 1)
            for t in range(9):
                rows = P if t < TT else NS
                act.wait_ge(summed, t + 1)
                act.activation(junk[0:rows], y_tile[0:rows, t % 4, :], ACT.Square, accum_out=ms[0:rows, t:t + 1])
                act.drain()
                act.activation(ms[0:rows, t:t + 1], ms[0:rows, t:t + 1], ACT.Sqrt, bias=m["eps"][0:rows],
                               scale=1.0 / D).then_inc(rms_ready, 1)


def log_count(distance):
    import numpy as np
    count = sum(((distance >= 0) & (distance <= window) & (distance % dilation == 0)).astype(np.int64)
                for window, dilation in ((128, 1), (512, 4), (2048, 16)))
    return np.where(count > 0, np.log(np.maximum(count, 1)), -1.0e30).astype(np.float32)


def prompt_bias():
    import numpy as np
    return log_count(np.arange(P)[:, None] + (SEQ - P) - np.arange(SEQ)[None, :])


def key_positions():
    import numpy as np
    far = np.arange(0, NB - NRECENT).reshape(-1, 16)[:, :ST].reshape(-1)
    assert len(far) == NSPARSE
    return np.concatenate([far, np.arange(NB - NRECENT, NB)])


def sample_bias():
    import numpy as np
    i = np.arange(ST)
    cached = log_count(NB + i[:, None] - key_positions()[None, :])
    own = np.where(i[:, None] >= i[None, :], log_count(i[:, None] - i[None, :]), np.float32(-1.0e30))
    new = np.full((SB, ST, SB, ST), -1.0e30, np.float32)
    for s in range(SB):
        new[s, :, s, :] = own
    rows = np.concatenate([np.broadcast_to(cached, (SB, ST, NKEY)), new.reshape(SB, ST, NS)], 2)
    rows = np.broadcast_to(rows[:, None], (SB, H, ST, NCOL)).reshape(2, P, NCOL)
    return rows.transpose(1, 0, 2).astype(np.float32)


def hgrn_constants():
    import numpy as np
    t = np.arange(T)
    chunk = np.where(t < SEQ, t // CH, NCH + (t - SEQ) // ST)
    same = lambda a: (chunk[a][:, None] == chunk[a][None, :]) & (t[a][:, None] <= t[a][None, :])
    resets = np.concatenate([[0.0], chunk[1:] == chunk[:-1]])
    return {
        "resets": np.broadcast_to(resets, (P, T)).astype(np.float32),
        "causal": same(slice(0, P)).astype(np.float32),
        "causal_s": same(slice(SEQ, T)).astype(np.float32),
        "only": (np.arange(NS)[:, None] // ST == np.arange(SB)[None, :]).astype(np.float32),
    }


def kernel(**inputs):
    import numpy as np
    import concourse.bacc as bacc
    from concourse.bass_utils import run_bass_kernel_spmd

    a = {k: np.asarray(v) for k, v in inputs.items()}
    x_all = np.concatenate([a["x_prompt"].reshape(SEQ, D), a["x_sample"].reshape(NS, D)], 0)
    w = a["w_in"][0].reshape(D, 7, 512)
    w = np.stack([w[:, i] for i in (0, 1, 3, 4, 6, 2, 5)])
    w = w.reshape(7, DC, P, 2, 256).transpose(0, 3, 2, 1, 4)
    ck = a["cache_k_win"][0].reshape(SB, NB, H * DH)
    cv = a["cache_v_win"][0].reshape(SB, NB, H * DH)
    chunked = lambda t: t.reshape(-1, P).T
    arrays = {
        "x_feat": x_all.T.reshape(DC, P, T).transpose(1, 0, 2),
        "x_tok": x_all,
        "norm1": chunked(a["norm1_w"][0]),
        "w_in": w.reshape(14, P, DC, 256),
        "bias_prompt": prompt_bias(),
        "bias_sample": sample_bias(),
        **hgrn_constants(),
        "keys_feat": ck[:, key_positions()].transpose(0, 2, 1).reshape(SB, 4, P, NKEY).transpose(0, 2, 1, 3),
        "vals_tok": cv[:, key_positions()].reshape(SB, NKEY // P, P, 512).transpose(0, 2, 1, 3),
        "lb_logits": a["hgrn_lb_logits"].reshape(2, G, P).transpose(2, 0, 1),
        "w_out": a["w_out"][0].reshape(DC, P, D).transpose(1, 0, 2),
        "norm2": np.broadcast_to(a["norm2_w"][0], (P, D)),
        "norm_f": np.broadcast_to(a["norm_f_w"], (P, D)),
        "wq": a["peer_wq"][0].reshape(DC, P, 2 * PH, P).transpose(2, 1, 0, 3),
        "sub_keys": a["peer_sub_keys"][0].reshape(2 * PH, PK, P).transpose(2, 0, 1),
        "u_feat": a["peer_u"][0].reshape(PK, PK, DC, P).transpose(0, 3, 2, 1).reshape(PK, P, D),
        "peer_v": a["peer_v"][0].reshape(PK, PK, D),
        "hgrn_norm": a["hgrn_norm_w"][0].reshape(P, 1),
        "state": a["state_hgrn"][0].transpose(2, 1, 0, 3),
        "cache_k": ck,
        "cache_v": cv,
    }
    arrays = {k: np.ascontiguousarray(v) for k, v in arrays.items()}
    outs = {
        "y": (T, D), "k_feat_out": (P, 4, T), "v_out": (P, TT, 512), "v_out_s": (NS, 512),
        "k_win_sample": (SB, NB, 512), "v_win_sample": (SB, NB, 512),
        "hgrn_p": (P, G, P), "hgrn_s": (P, G, SB, P),
    }
    nc = bacc.Bacc("TRN2", target_bir_lowering=False, num_devices=1)
    x = {k: nc.dram_tensor(f"in_{k}", v.shape, mybir.dt.from_np(v.dtype), kind="ExternalInput").ap()
         for k, v in arrays.items()}
    x.update({k: nc.dram_tensor(f"out_{k}", s, F32, kind="ExternalOutput").ap() for k, s in outs.items()})
    scratch = {"h": (T, D), "scores": (P, 9, 2 * PH * PK), "acts": (PK, P, T), "gates": (PK, P, T)}
    x.update({k: nc.dram_tensor(f"scratch_{k}", s, F32, kind="Internal").ap() for k, s in scratch.items()})
    build(nc, x)
    r = run_bass_kernel_spmd(nc, [{f"in_{k}": v for k, v in arrays.items()}], core_ids=[0]).results[0]
    got = {k: np.asarray(r[f"out_{k}"]) for k in outs}
    k_all = got["k_feat_out"].transpose(2, 1, 0).reshape(T, 512)
    v_all = got["v_out"].transpose(1, 0, 2).reshape(SEQ, 512)
    kw, vw = got["k_win_sample"], got["v_win_sample"]
    kw = np.concatenate([kw[:, :NB - ST], k_all[SEQ:].reshape(SB, ST, 512)], 1)
    vw = np.concatenate([vw[:, :NB - ST], got["v_out_s"].reshape(SB, ST, 512)], 1)
    win = (1, SB, NB, H, DH)
    return (
        got["y"][:SEQ].reshape(1, SEQ, D),
        got["y"][SEQ:].reshape(SB, ST, D),
        np.ascontiguousarray(k_all[:SEQ]).reshape(1, 1, SEQ, H, DH),
        np.ascontiguousarray(v_all).reshape(1, 1, SEQ, H, DH),
        np.ascontiguousarray(got["hgrn_p"].transpose(1, 0, 2)).reshape(1, 1, G, DK, DK),
        kw.reshape(win), vw.reshape(win),
        np.ascontiguousarray(got["hgrn_s"].transpose(2, 1, 0, 3)).reshape(1, SB, G, DK, DK),
    )
```
